# Optimizing a Trainium2 kernel written in Bass

```python
import jax, jax.numpy as jnp
from jax import lax
import numpy as np

D_MODEL = 1024
BATCH = 1
SEQ = 128
DEPTH = 2
DEC_BATCH = 1
DEC_SEQ = 512
PAST_LEN = 128

GRID_W = 64
N_HEADS = 16
N_KV_HEADS = 4
HEAD_DIM = 64
GROUP = N_HEADS // N_KV_HEADS
Q_W = N_HEADS * HEAD_DIM
KV_W = N_KV_HEADS * HEAD_DIM
CONV_W = D_MODEL // 2
CONV_K = 3
IN_W = Q_W + 2 * KV_W + 3 * CONV_W + 2 * D_MODEL
N_EXPERTS = 16
EC_FACTOR = 2
D_EXPERT = 1024
Q_BLOCK = 128
AXIS_DIM = HEAD_DIM // 2
ROPE_THETA = 10000.0
EPS = 1e-6

kernel_name = "hybrid_conv_gqa_ec_diffusion_step"

def rmsnorm(x, g):
    x32 = x.astype(jnp.float32)
    y = x32 * lax.rsqrt(jnp.mean(x32 * x32, axis=-1, keepdims=True) + EPS)
    return y.astype(x.dtype) * g

def axial_rope(x, row, col):
    half = AXIS_DIM // 2
    inv_freq = ROPE_THETA ** (-jnp.arange(half, dtype=jnp.float32) / half)

    def rot(xa, pos):
        ang = pos.astype(jnp.float32)[:, None] * inv_freq[None, :]
        cos = jnp.cos(ang)[None, :, None, :].astype(x.dtype)
        sin = jnp.sin(ang)[None, :, None, :].astype(x.dtype)
        x1, x2 = xa[..., :half], xa[..., half:]
        return jnp.concatenate([x1 * cos - x2 * sin, x1 * sin + x2 * cos], axis=-1)

    return jnp.concatenate([rot(x[..., :AXIS_DIM], row), rot(x[..., AXIS_DIM:], col)], axis=-1)

def block_attention(q, k, v):
    b, n, _, hd = q.shape
    nblk = n // Q_BLOCK
    qb = q.reshape(b, nblk, Q_BLOCK, N_KV_HEADS, GROUP, hd).transpose(1, 0, 2, 3, 4, 5)
    scale = HEAD_DIM ** -0.5

    def one(qblk):
        s = jnp.einsum('bqkgd,bmkd->bkgqm', qblk, k).astype(jnp.float32) * scale
        p = jax.nn.softmax(s, axis=-1).astype(v.dtype)
        return jnp.einsum('bkgqm,bmkd->bqkgd', p, v)

    o = lax.map(one, qb)
    return o.transpose(1, 0, 2, 3, 4, 5).reshape(b, n, Q_W)

def dwconv3(u, w):
    up = jnp.pad(u, ((0, 0), (1, 1), (0, 0)))
    return w[0] * up[:, :-2] + w[1] * up[:, 1:-1] + w[2] * up[:, 2:]

def token_mixer(h, lp, grid_pos, ctx_k, ctx_v):
    b, n, _ = h.shape
    proj = h @ lp['w_in']
    offs = np.cumsum([Q_W, KV_W, KV_W, CONV_W, CONV_W, CONV_W, D_MODEL]).tolist()
    q, k, v, gb, gc, xin, ga_lin, gat_lin = jnp.split(proj, offs, axis=-1)
    q = rmsnorm(q.reshape(b, n, N_HEADS, HEAD_DIM), lp['q_norm'])
    k = rmsnorm(k.reshape(b, n, N_KV_HEADS, HEAD_DIM), lp['k_norm'])
    v = v.reshape(b, n, N_KV_HEADS, HEAD_DIM)
    if grid_pos is None:
        q_r, k_all, v_all = q, k, v
    else:
        row, col = grid_pos
        q_r = axial_rope(q, row, col)
        k_r = axial_rope(k, row, col)
        k_all = jnp.concatenate([ctx_k, k_r], axis=1)
        v_all = jnp.concatenate([ctx_v, v], axis=1)
    attn = block_attention(q_r, k_all, v_all) @ lp['w_attn_out']
    conv = (gb * dwconv3(gc * xin, lp['conv_w'])) @ lp['w_conv_out']
    merged = jax.nn.sigmoid(ga_lin) * conv + jax.nn.sigmoid(gat_lin) * attn
    return merged @ lp['w_o'], k, v

def expert_choice_ffn(h, lp):
    b, n, d = h.shape
    cap = max(1, EC_FACTOR * n // N_EXPERTS)
    logits = jnp.einsum('bnd,de->bne', h, lp['w_router']).astype(jnp.float32)
    aff = jax.nn.softmax(logits, axis=-1)
    vals, idx = lax.top_k(jnp.swapaxes(aff, 1, 2), cap)
    x_sel = jax.vmap(lambda hb, ib: hb[ib])(h, idx)
    gate = jnp.einsum('becd,edf->becf', x_sel, lp['w_gate'])
    up = jnp.einsum('becd,edf->becf', x_sel, lp['w_up'])
    y = jnp.einsum('becf,efd->becd', jax.nn.silu(gate) * up, lp['w_down'])
    y = y * vals[..., None].astype(h.dtype)
    return jax.vmap(lambda yb, ib: jnp.zeros((n, d), h.dtype).at[ib.reshape(-1)].add(yb.reshape(-1, d)))(y, idx)

def layer(x, mod, lp, grid_pos, ctx_k, ctx_v):
    sh1, sc1, g1, sh2, sc2, g2 = jnp.split(mod, 6, axis=-1)
    h = rmsnorm(x, lp['norm1']) * (1 + sc1) + sh1
    mix, k, v = token_mixer(h, lp, grid_pos, ctx_k, ctx_v)
    x = x + g1 * mix
    h2 = rmsnorm(x, lp['norm2']) * (1 + sc2) + sh2
    x = x + g2 * expert_choice_ffn(h2, lp)
    return x, k, v

def setup_inputs(seed: int = 0) -> dict:
    key = jax.random.key(seed)
    ks = jax.random.split(key, 24)
    f32 = jnp.float32
    nrm = lambda k, s, sc: (jax.random.normal(k, s, f32) * sc)
    return {
        'x_prompt': nrm(ks[0], (BATCH, SEQ, D_MODEL), 1.0),
        'x_sample': nrm(ks[1], (DEC_BATCH, DEC_SEQ, D_MODEL), 1.0),
        'cache_k': nrm(ks[2], (DEC_BATCH, DEPTH, PAST_LEN, N_KV_HEADS, HEAD_DIM), 1.0),
        'cache_v': nrm(ks[3], (DEC_BATCH, DEPTH, PAST_LEN, N_KV_HEADS, HEAD_DIM), 1.0),
        'c': nrm(ks[4], (DEC_BATCH, D_MODEL), 1.0),
        'c_ctx': nrm(ks[5], (D_MODEL,), 1.0),
        'w_mod': nrm(ks[6], (DEPTH, D_MODEL, 6 * D_MODEL), 0.5 * D_MODEL ** -0.5),
        'b_mod': nrm(ks[7], (DEPTH, 6 * D_MODEL), 0.02),
        'norm1': 1.0 + nrm(ks[8], (DEPTH, D_MODEL), 0.02),
        'norm2': 1.0 + nrm(ks[9], (DEPTH, D_MODEL), 0.02),
        'w_in': nrm(ks[10], (DEPTH, D_MODEL, IN_W), D_MODEL ** -0.5),
        'q_norm': 1.0 + nrm(ks[11], (DEPTH, HEAD_DIM), 0.02),
        'k_norm': 1.0 + nrm(ks[12], (DEPTH, HEAD_DIM), 0.02),
        'conv_w': nrm(ks[13], (DEPTH, CONV_K, CONV_W), CONV_K ** -0.5),
        'w_conv_out': nrm(ks[14], (DEPTH, CONV_W, D_MODEL), CONV_W ** -0.5),
        'w_attn_out': nrm(ks[15], (DEPTH, Q_W, D_MODEL), Q_W ** -0.5),
        'w_o': nrm(ks[16], (DEPTH, D_MODEL, D_MODEL), D_MODEL ** -0.5),
        'w_router': nrm(ks[17], (DEPTH, D_MODEL, N_EXPERTS), D_MODEL ** -0.5),
        'w_gate': nrm(ks[18], (DEPTH, N_EXPERTS, D_MODEL, D_EXPERT), D_MODEL ** -0.5),
        'w_up': nrm(ks[19], (DEPTH, N_EXPERTS, D_MODEL, D_EXPERT), D_MODEL ** -0.5),
        'w_down': nrm(ks[20], (DEPTH, N_EXPERTS, D_EXPERT, D_MODEL), D_EXPERT ** -0.5),
        'final_norm': 1.0 + nrm(ks[21], (D_MODEL,), 0.02),
    }

def reference(x_prompt, x_sample, cache_k, cache_v, c, c_ctx, w_mod, b_mod, norm1, norm2, w_in, q_norm, k_norm,
              conv_w, w_conv_out, w_attn_out, w_o, w_router, w_gate, w_up, w_down, final_norm):
    n_lat = x_sample.shape[1]
    rows = n_lat // GRID_W
    row = jnp.repeat(jnp.arange(rows, dtype=jnp.int32), GRID_W)
    col = jnp.tile(jnp.arange(GRID_W, dtype=jnp.int32), rows)

    xp = x_prompt
    xs = x_sample
    new_k, new_v = [], []
    for l in range(DEPTH):
        lp = {'norm1': norm1[l], 'norm2': norm2[l], 'w_in': w_in[l], 'q_norm': q_norm[l], 'k_norm': k_norm[l],
              'conv_w': conv_w[l], 'w_conv_out': w_conv_out[l], 'w_attn_out': w_attn_out[l], 'w_o': w_o[l],
              'w_router': w_router[l], 'w_gate': w_gate[l], 'w_up': w_up[l], 'w_down': w_down[l]}
        mod_ctx = (jax.nn.silu(c_ctx) @ w_mod[l] + b_mod[l])[None, None, :]
        xp, k_ctx, v_ctx = layer(xp, mod_ctx, lp, None, None, None)
        new_k.append(k_ctx)
        new_v.append(v_ctx)
        mod_lat = (jax.nn.silu(c) @ w_mod[l] + b_mod[l])[:, None, :]
        xs, _, _ = layer(xs, mod_lat, lp, (row, col), cache_k[:, l], cache_v[:, l])

    y_prompt = rmsnorm(xp, final_norm)
    y_sample = rmsnorm(xs, final_norm)
    new_cache_k = jnp.stack(new_k, axis=1)
    new_cache_v = jnp.stack(new_v, axis=1)
    return (y_prompt, y_sample, new_cache_k, new_cache_v)


_drawn_inputs = setup_inputs


def setup_inputs(seed=0):
    import zlib

    import numpy as np

    out = dict(_drawn_inputs(seed))
    spreads = {}
    factors = {'cache_k': 8.0,
     'cache_v': 7.39,
     'norm1': 2.803,
     'norm2': 6.439,
     'q_norm': 8.0,
     'k_norm': 3.068,
     'final_norm': 2.751}
    for name, (base, spread) in spreads.items():
        noise = np.random.default_rng([zlib.crc32(name.encode()), seed]).standard_normal(out[name].shape)
        drawn = base * np.exp(spread * noise) if base else spread * noise
        out[name] = __import__('jax').numpy.asarray(drawn.astype(out[name].dtype))
    for name, factor in factors.items():
        out[name] = (out[name] * factor).astype(out[name].dtype)
    return out
```

```python
from contextlib import ExitStack, contextmanager

import numpy as np
import concourse.bass as bass
from concourse import mybir

F32 = mybir.dt.float32
F32R = mybir.dt.float32r
ALU = mybir.AluOpType
ACT = mybir.ActivationFunctionType
AX = mybir.AxisListType
ds = bass.ds

P = 128
D = 1024
KT = D // P
DEPTH = 2
LAT, CTX = 512, 128
T = LAT + CTX
NT = T // P
LT = LAT // P
H, KV, HD = 16, 4, 64
GRID_W = 64
QW, KVW, CW = H * HD, KV * HD, D // 2
E = 16
DE = 1024
CAP_L = 2 * LAT // E
CAP_C = 2 * CTX // E
SL = CAP_L + CAP_C
PAST = 128
EPS = 1e-6
KEYS = PAST + LAT + CTX
AXD = HD // 2
HALF = AXD // 2

UW = 256
U5 = NT * UW
OQ, OK_, OV = 0, QW, QW + KVW
OGB = QW + 2 * KVW
OGC, OXI = OGB + CW, OGB + 2 * CW
OGA = OGB + 3 * CW
OGT = OGA + D
U_Q, U_K, U_V, U_CONV, U_GATE, U_GT, U_AO, U_WO = 0, 4, 5, 6, 12, 20, 24, 28
UNITS = 32
RING = 6
MOD_UNITS = DEPTH * 12
EU = 6 * E
ITEMS = NT * H


class Signal:

    def __init__(self, sem, per_layer, before=0):
        self.sem, self.per_layer, self.before = sem, per_layer, before

    def at(self, layer, n):
        return layer * self.per_layer + (self.before + n)


class Chain:

    def __init__(self, eng, per_layer):
        self.eng, self.per_layer, self.n, self.base = eng, per_layer, 0, 0

    def next(self):
        self.n += 1
        return self.base + self.n

    @contextmanager
    def loop(self, count, body):
        first, base = self.n, self.base
        with self.eng.Fori(0, count) as i:
            self.base = base + i * body
            yield i
        assert self.n - first == body, f"loop body: {self.n - first} steps"
        self.n, self.base = first + count * body, base

    @contextmanager
    def layers(self):
        first = self.n
        with self.eng.Fori(0, DEPTH) as layer:
            self.base = layer * self.per_layer
            yield layer
        assert self.n - first == self.per_layer, f"layer: {self.n - first} steps"
        self.n, self.base = first + DEPTH * self.per_layer, 0


def build(nc, x_prompt, x_sample, cache_k, cache_v, c, c_ctx, w_mod, b_mod, norm1, norm2, w_in, q_norm,
          k_norm, conv_w, w_conv_out, w_attn_out, w_o, w_router, w_gate, w_up, w_down, final_norm,
          ident_c, slots_c, cos_c, sin_c, y_prompt, y_sample, new_k, new_v):
    ctx = ExitStack()
    with ctx:
        KB = 1024
        B0 = 16640

        def at(name, shape, dt, off):
            return nc.alloc_sbuf_tensor_at(name, shape, dt, offset=B0 + off)

        x = at("x", [P, NT, D], F32, 0)
        gbc = at("gate1_rows", [P, 2, D], F32, 20 * KB)
        g2mix = at("gate2_rows", [P, D], F32, 28 * KB)
        bump = [32 * KB]

        def small(name, shape, dt=F32):
            t = at(name, shape, dt, bump[0])
            n = 4
            for s in shape[1:]:
                n *= s
            bump[0] += (n + 31) // 32 * 32
            assert bump[0] <= 44 * KB, bump
            return t

        ident = small("ident", [P, P])
        slot_ids = small("slot_ids", [P, SL])
        cosT = small("cosT", [P, LT, HD])
        sinT = small("sinT", [P, LT, HD])
        qC = small("qC", [P, LT, HD])
        qS = small("qS", [P, LT, HD])
        kC = small("kC", [P, LT, HD])
        kS = small("kS", [P, LT, HD])
        gq = small("gq", [P, HD])
        gk = small("gk", [P, HD])
        wr = small("wr", [P, KT, E])
        mod = small("mod", [P, DEPTH * 48, 2])
        modl = small("modl", [P, 48, 2])
        A1 = small("A1", [P, KT, 2])
        A2 = small("A2", [P, KT, 2])
        colsA = small("colsA", [P, P])
        colsB = small("colsB", [P, 40])
        sc = small("silu_c", [P, KT, 2])
        ss = small("ss", [P, 2, 8])
        rq = small("rq", [P, NT, H])
        rk = small("rk", [P, NT, KV])
        nmax = small("nmax", [P, 2])
        rsum = small("rsum", [P, H])
        rinv = small("rinv", [P, H])
        lgm = small("lgm", [P, NT])
        lg = small("lg", [P, NT, E])
        aff = small("aff", [P, NT, E])
        lsum = small("lsum", [P, NT])
        slotT = small("slotT", [P, NT, E])
        top8 = small("top8", [E, 8])
        vals = small("vals", [SL, 2])
        minus_half = small("minus_half", [P, 1])

        ring = [at(f"ring{s}", [P, KT, 512], F32, (44 + 16 * s) * KB) for s in range(RING)]
        raw = [at(f"raw{s}", [P, KT, UW], F32, (44 + 8 * s) * KB) for s in range(2)]
        whi = [at(f"whi{s}", [P, KT, UW], F32R, (60 + 8 * s) * KB) for s in range(2)]
        wlo = [at(f"wlo{s}", [P, KT, UW], F32R, (76 + 8 * s) * KB) for s in range(2)]
        hThi = at("hThi", [P, KT, T], F32R, 167 * KB)
        hTlo = at("hTlo", [P, KT, T], F32R, 187 * KB)
        oThi = at("oThi", [P, KT, T], F32R, 167 * KB)
        oTlo = at("oTlo", [P, KT, T], F32R, 187 * KB)
        xnhi = at("xnhi", [P, NT, D], F32R, 167 * KB)
        xnlo = at("xnlo", [P, NT, D], F32R, 187 * KB)
        m = at("m", [P, KT, T], F32, 92 * KB)
        gcs = at("gcs", [P, 2, T], F32, 92 * KB)
        ub = at("ub", [P, 2, T + 3], F32, 97 * KB)
        cb = at("cb", [P, 2, T + 3], F32, 97 * KB + 5152)
        t1 = at("t1", [P, D], F32, 97 * KB + 2 * 5152)
        rowsA = at("rowsA", [P, P], F32, 150 * KB)
        rowsB = at("rowsB", [40, P], F32, 151 * KB)
        xnb1 = [at(f"xnb1_{s}", [P, D], F32, (92 + 4 * s) * KB) for s in range(2)]
        hb1 = [at(f"hb1_{s}", [P, KT, P], F32, (100 + 4 * s) * KB) for s in range(2)]
        xnb2 = [at(f"xnb2_{s}", [P, D], F32, (140 + 4 * s) * KB) for s in range(2)]
        hb2 = [at(f"hb2_{s}", [P, KT, P], F32, (148 + 4 * s) * KB) for s in range(2)]
        zhi = at("zhi", [P, KT // 2, T], F32R, 112 * KB)
        zlo = at("zlo", [P, KT // 2, T], F32R, 122 * KB)
        G = at("G", [P, KT, T], F32, 112 * KB)
        mlo = at("mlo", [P, KT, T], F32R, 112 * KB)
        q = at("q", [P, NT, D], F32, 132 * KB)
        mhi = at("mhi", [P, KT, T], F32R, 132 * KB)
        k = at("k", [P, NT, KVW], F32, 152 * KB)
        v = at("v", [P, NT, KVW], F32, 157 * KB)
        t2 = at("t2", [P, D], F32, 162 * KB)
        tw = at("tw", [P, U5], F32, 162 * KB)
        prob = [at(f"prob{s}", [P, 5 * P], F32, 44 * KB + 2560 * s) for s in range(2)]
        probT = [at(f"probT{s}", [P, 5, P], F32, 49 * KB + 2560 * s) for s in range(2)]
        ot = at("ot", [P, D], F32, 54 * KB)
        qs = [at(f"qs{s}", [P, 4, P], F32R, (163 + 2 * s) * KB) for s in range(2)]
        ck = at("ck", [P, KVW], F32, 59 * KB)
        kst = at("kst", [P, 2, KV, KEYS], F32R, 60 * KB)
        qsp = at("qsp", [P, H, 2, HD], F32, 84 * KB)
        ksp = at("ksp", [P, 2, KV, 2, HD], F32, 49 * KB)
        cv = at("cv", [P, KVW], F32, 162 * KB)
        xsel = at("xsel", [P, KT, 2, SL], F32, 20 * KB)
        hid = at("hid", [P, KT, SL], F32, 25 * KB)
        yhi = at("yhi", [SL, 2, D], F32R, 140 * KB)
        ylo = at("ylo", [SL, 2, D], F32R, 148 * KB)
        ym = at("ym", [SL, 512], F32, 156 * KB)
        S = at("S", [P, NT, 2, SL], F32R, 158 * KB)
        ST = at("ST", [SL, 2, T], F32R, 162 * KB)
        affT = at("affT", [E, T], F32, 156 * KB)
        work = at("work", [E, T], F32, 159 * KB)
        cum = at("cum", [E, T], F32, 162 * KB)

        ps = nc.alloc_psum_tensor("ps", [P, 8 * 512], F32)

        def bank(b, n=1):
            return ps[:, 512 * b:512 * (b + n)]

        acc = [ps[:, 0:U5], ps[:, 1536:1536 + U5]]
        tp = [bank(0, 2), bank(2, 2)]
        scores = [bank(0, 2), bank(2, 2)]
        ptp = ps[:, 2048:2048 + 5 * P]
        pso = bank(6)
        qtp = bank(7)
        gate_ps = [bank(0)[:, 0:4 * SL], bank(1)[:, 0:4 * SL]]
        up_ps = [bank(2)[:, 0:4 * SL], bank(3)[:, 0:4 * SL]]
        down_ps = [ps[0:SL, 2048:2560], ps[0:SL, 2560:3072]]
        side = [bank(6), bank(7)]

        def sem(name):
            return ctx.enter_context(nc.semaphore(name))

        waits_passed = sem("waits_passed")
        params_loaded = sem("params_loaded")
        x_loaded = sem("x_loaded")
        setup_tp = sem("setup_tp")
        cols_ready = sem("cols_ready")
        silu_c_ready = sem("silu_c_ready")
        mod_taken = sem("mod_taken")
        out_stored = sem("out_stored")
        fn_loaded = sem("fn_loaded")
        dve_chain = sem("dve_chain")
        pool_chain = sem("pool_chain")
        act_chain = sem("act_chain")

        def sig(name, per_layer, before=0):
            return Signal(sem(name), per_layer, before)

        lp_loaded = sig("lp_loaded", 16 * 3)
        cache_loaded = sig("cache_loaded", 16 * 2)
        kv_stored = sig("kv_stored", 16 * 2)
        raw_loaded = [sig(f"raw_loaded{s}", 16 * UNITS // 2) for s in range(2)]
        ring_loaded = [sig(f"ring_loaded{s}", 16 * E, 16 * 4) for s in range(RING)]
        ring_done = sig("ring_done", EU, MOD_UNITS)
        x_ready = sig("x_ready", 2, 1)
        modl_ready = sig("modl_ready", 1)
        rows_ready = sig("rows_ready", 2)
        rows_taken = sig("rows_taken", 2)
        sq_ready = sig("sq_ready", 10)
        rstd_ready = sig("rstd_ready", 2)
        xn_ready = sig("xn_ready", 10)
        tp_ready = sig("tp_ready", 10)
        h32_ready = sig("h32_ready", 10)
        hi_ready = sig("hi_ready", 10)
        lo_ready = sig("lo_ready", 10)
        logits_done = sig("logits_done", NT)
        whi_ready = sig("whi_ready", UNITS)
        wlo_ready = sig("wlo_ready", UNITS, 2)
        unit_done = sig("unit_done", UNITS, 2)
        acc_taken = [sig(f"acc_taken{s}", UNITS // 2, 1) for s in range(2)]
        ssq_ready = sig("ssq_ready", 1)
        rqk_ready = sig("rqk_ready", 1)
        qk_ready = sig("qk_ready", 1)
        zhi_ready = sig("zhi_ready", 2)
        z_ready = sig("z_ready", 2)
        khi_ready = sig("khi_ready", 6)
        ksplit = sig("ksplit", 6)
        ktp_ready = sig("ktp_ready", 6, 1)
        kst_ready = sig("kst_ready", 6)
        qhi_ready = sig("qhi_ready", NT)
        qsplit = sig("qsplit", NT)
        qt_ready = sig("qt_ready", ITEMS // 4, 1)
        qs_ready = sig("qs_ready", ITEMS // 4, 1)
        s_ready = sig("s_ready", ITEMS, 4)
        nmax_ready = sig("nmax_ready", ITEMS)
        p_ready = sig("p_ready", ITEMS, 2)
        pt_ready = sig("pt_ready", ITEMS, 2)
        pts_ready = sig("pts_ready", ITEMS, 1)
        pv_done = sig("pv_done", ITEMS, 2)
        o_ready = sig("o_ready", 2 * NT, 1)
        otp_ready = sig("otp_ready", NT, 1)
        ohi_ready = sig("ohi_ready", NT)
        oT_ready = sig("oT_ready", NT, 1)
        mrg_ready = sig("mrg_ready", 4)
        mhi_ready = sig("mhi_ready", 4)
        m_ready = sig("m_ready", 4)
        aff_ready = sig("aff_ready", 1)
        lgsub_ready = sig("lgsub_ready", 1)
        lgexp_ready = sig("lgexp_ready", 1)
        affT_ready = sig("affT_ready", 1)
        slots_ready = sig("slots_ready", 1)
        slotsT_ready = sig("slotsT_ready", 1)
        S_ready = sig("S_ready", E // 2)
        side_ready = sig("side_ready", 18 * E // 2)
        side_taken = [sig(f"side_taken{s}", 9 * E // 2, 1) for s in range(2)]
        silu_ready = sig("silu_ready", 2 * E, 2)
        hid_ready = sig("hid_ready", 2 * E, 2)
        ym_ready = sig("ym_ready", 2 * E, 2)
        yhi_ready = sig("yhi_ready", 2 * E)
        ylo_ready = sig("ylo_ready", 2 * E)

        def f32(ap):
            return ap.bitcast(F32)

        block = ctx.enter_context(nc.Block())

        @block.sync
        def _(sp):
            b_mod_rows = b_mod.rearrange("l (j p) -> (l j) p", p=P)
            for dst, src in ((rowsA[0:96, :], b_mod_rows),
                             (rowsA[96:112, :], norm1.rearrange("l (j p) -> (l j) p", p=P)),
                             (rowsA[112:128, :], norm2.rearrange("l (j p) -> (l j) p", p=P)),
                             (rowsB[0:8, :], c.rearrange("b (j p) -> (b j) p", p=P)),
                             (rowsB[8:16, :], c_ctx.rearrange("(j p) -> j p", p=P)),
                             (rowsB[16:40, :], conv_w.rearrange("l j (f p) -> (l j f) p", p=P)),
                             (ident[:, :], ident_c), (slot_ids[:, :], slots_c),
                             (cosT[:, :, :], cos_c.rearrange("(t p) d -> p t d", p=P)),
                             (sinT[:, :, :], sin_c.rearrange("(t p) d -> p t d", p=P))):
                sp.dma_start(dst, src).then_inc(params_loaded, 16)

            def mod_piece(i, s):
                src = w_mod[i // 2].rearrange("(k p) n -> p k n", p=P)
                col = (i % 2 * RING + s) * 512
                sp.dma_start(ring[s][:, :, :], src[:, :, col:col + 512]).then_inc(ring_loaded[s].sem, 16)

            for s in range(RING):
                mod_piece(0, s)
            sp.dma_start(x[:, 0:LT, :], x_sample[0].rearrange("(t p) d -> p t d", p=P)).then_inc(x_loaded, 16)
            sp.dma_start(x[:, LT, :], x_prompt[0]).then_inc(x_loaded, 16)
            for i in range(1, MOD_UNITS // RING):
                for s in range(RING):
                    sp.wait_ge(ring_done.sem, i * RING + (s + 1 - RING))
                    mod_piece(i, s)

            with sp.Fori(0, DEPTH) as layer:
                one = ds(layer, 1)
                sp.wait_ge(x_ready.sem, x_ready.at(layer, 0))
                sp.dma_start(wr[:, :, :], w_router[one].rearrange("o (k p) e -> p (o k) e", p=P)).then_inc(lp_loaded.sem, 16)
                sp.dma_start(gq[:, :], q_norm[one, :].broadcast_to([P, HD])).then_inc(lp_loaded.sem, 16)
                sp.dma_start(gk[:, :], k_norm[one, :].broadcast_to([P, HD])).then_inc(lp_loaded.sem, 16)
                sp.wait_ge(ring_done.sem, ring_done.at(layer, 0))
                sp.sem_inc(waits_passed, 1)

                def unit(u, b, src):
                    sp.wait_ge(wlo_ready.sem, wlo_ready.at(layer, u - 1))
                    nk = src.shape[1]
                    sp.dma_start(raw[b][:, 0:nk, :], src).then_inc(raw_loaded[b].sem, 16)

                win = w_in[one].rearrange("o (k p) n -> p (o k) n", p=P)
                wco = w_conv_out[one].rearrange("o (k p) n -> p (o k) n", p=P)
                wao = w_attn_out[one].rearrange("o (k p) n -> p (o k) n", p=P)
                woo = w_o[one].rearrange("o (k p) n -> p (o k) n", p=P)
                with sp.Fori(0, 2) as i:
                    for b in range(2):
                        unit(U_Q + 2 * i + b, b, win[:, :, ds(OQ + (2 * i + b) * UW, UW)])
                unit(U_K, 0, win[:, :, OK_:OK_ + UW])
                unit(U_V, 1, win[:, :, OV:OV + UW])
                for hf in range(2):
                    for j, o in enumerate((OGC, OXI, OGB)):
                        u = U_CONV + 3 * hf + j
                        unit(u, u % 2, win[:, :, o + hf * UW:o + (hf + 1) * UW])
                with sp.Fori(0, 4) as i:
                    unit(U_GATE + 2 * i, 0, win[:, :, ds(OGA + i * UW, UW)])
                    unit(U_GATE + 2 * i + 1, 1, wco[:, :, ds(i * UW, UW)])
                sp.wait_ge(qk_ready.sem, qk_ready.at(layer, 1))
                nk_dst = new_k[0][one].rearrange("l s h d -> (l s) (h d)")
                nv_dst = new_v[0][one].rearrange("l s h d -> (l s) (h d)")
                sp.dma_start(nk_dst, k[:, LT, :]).then_inc(kv_stored.sem, 16)
                sp.dma_start(nv_dst, v[:, LT, :]).then_inc(kv_stored.sem, 16)
                with sp.Fori(0, 2) as i:
                    for b in range(2):
                        unit(U_GT + 2 * i + b, b, win[:, :, ds(OGT + (2 * i + b) * UW, UW)])
                sp.wait_ge(wlo_ready.sem, wlo_ready.at(layer, U_AO))
                for b in range(2):
                    sp.wait_ge(acc_taken[b].sem, acc_taken[b].at(layer, U_AO // 2))
                sp.dma_start(ck[:, :], cache_k[0][one].rearrange("l s h d -> (l s) (h d)")).then_inc(cache_loaded.sem, 16)
                sp.dma_start(cv[:, :], cache_v[0][one].rearrange("l s h d -> (l s) (h d)")).then_inc(cache_loaded.sem, 16)
                sp.wait_ge(oT_ready.sem, oT_ready.at(layer, NT))
                sp.sem_inc(waits_passed, 1)
                with sp.Fori(0, 2) as i:
                    for b in range(2):
                        unit(U_AO + 2 * i + b, b, wao[:, :, ds((2 * i + b) * UW, UW)])
                with sp.Fori(0, 2) as i:
                    for b in range(2):
                        unit(U_WO + 2 * i + b, b, woo[:, :, ds((2 * i + b) * UW, UW)])
                sp.wait_ge(kv_stored.sem, kv_stored.at(layer, 32))
                sp.sem_inc(waits_passed, 1)
                sp.wait_ge(x_ready.sem, x_ready.at(layer, 1))
                sp.sem_inc(waits_passed, 1)
                with sp.Fori(0, E) as e:
                    pieces = [(w, hf) for hf in range(2) for w in (w_gate, w_up)] + [(w_down, 0), (w_down, 1)]
                    for s, (w, hf) in enumerate(pieces):
                        sp.wait_ge(ring_done.sem, ring_done.at(layer, 6 * e + (s + 1 - RING)))
                        src = w[one][:, ds(e, 1)].rearrange("l e (k p) n -> p (l e k) n", p=P)
                        sp.dma_start(ring[s][:, :, :], src[:, :, hf * 512:(hf + 1) * 512]).then_inc(ring_loaded[s].sem, 16)

            sp.wait_ge(x_ready.sem, x_ready.at(DEPTH, 0))
            sp.dma_start(gbc[:, 0, :], final_norm.rearrange("(o d) -> o d", o=1).broadcast_to([P, D])).then_inc(fn_loaded, 16)
            ys = y_sample[0].rearrange("(t p) d -> p t d", p=P)
            for t in range(NT):
                sp.wait_ge(xn_ready.sem, xn_ready.at(DEPTH, t + 1))
                sp.dma_start(ys[:, t, :] if t < LT else y_prompt[0], x[:, t, :]).then_inc(out_stored, 16)
            sp.wait_ge(out_stored, 16 * NT)

        @block.gpsimd
        def _(pool):
            ch = Chain(pool, 5)

            def rsqrt(ap, n, done):
                pool.tensor_scalar(ap, ap, 1.0 / n, EPS, ALU.mult, ALU.add).then_inc(pool_chain, 1)
                pool.wait_ge(pool_chain, ch.next())
                pool.tensor_tensor(ap, ap, minus_half[:, 0:1].broadcast_to(list(ap.shape)), ALU.pow).then_inc(done, 1)

            pool.memset(minus_half[:, :], -0.5).then_inc(pool_chain, 1)
            ch.n = 1
            pool.wait_ge(pool_chain, 1)
            with ch.layers() as layer:
                pool.wait_ge(sq_ready.sem, sq_ready.at(layer, NT))
                pool.sem_inc(waits_passed, 1)
                rsqrt(ss[:, 0, 0:NT], D, rstd_ready.sem)
                pool.wait_ge(ssq_ready.sem, ssq_ready.at(layer, 1))
                pool.sem_inc(waits_passed, 1)
                pool.tensor_scalar(rq[:, :, :], rq[:, :, :], 1.0 / HD, EPS, ALU.mult, ALU.add).then_inc(pool_chain, 1)
                pool.wait_ge(pool_chain, ch.next())
                pool.tensor_tensor(rq[:, :, :].rearrange("p t h -> p (t h)"), rq[:, :, :].rearrange("p t h -> p (t h)"),
                                                 minus_half[:, 0:1].broadcast_to([P, NT * H]), ALU.pow).then_inc(pool_chain, 1)
                pool.wait_ge(pool_chain, ch.next())
                pool.sem_inc(waits_passed, 1)
                rsqrt(rk[:, :, :].rearrange("p t h -> p (t h)"), HD, rqk_ready.sem)
                pool.wait_ge(sq_ready.sem, sq_ready.at(layer, 2 * NT))
                pool.sem_inc(waits_passed, 1)
                rsqrt(ss[:, 1, 0:NT], D, rstd_ready.sem)
            pool.wait_ge(sq_ready.sem, sq_ready.at(DEPTH, NT))
            rsqrt(ss[:, 0, 0:NT], D, rstd_ready.sem)

        @block.scalar
        def _(act):
            act.sem_inc(qs_ready.sem, 1)
            act.sem_inc(p_ready.sem, 2)
            act.sem_inc(silu_ready.sem, 2)
            act.wait_ge(cols_ready, 1)
            for s in range(2):
                ins = act.activation(sc[:, :, s], colsB[:, 8 * s:8 * s + 8], ACT.Silu)
            ins.then_inc(silu_c_ready, 1)

            def squares(layer, t, row):
                if t >= 2:
                    act.wait_ge(sq_ready.sem, sq_ready.at(layer, NT * row + t - 1))
                act.activation(tp[t % 2], x[:, t, :], ACT.Square, accum_out=ss[:, row, t:t + 1]).then_inc(sq_ready.sem, 1)

            with act.Fori(0, DEPTH) as layer:
                def split(h, b, nk=KT):
                    act.wait_ge(raw_loaded[b].sem, raw_loaded[b].at(layer, (h + 1) * 16))
                    act.wait_ge(unit_done.sem, unit_done.at(layer, 2 * h + (b - 1)))
                    act.activation(whi[b][:, 0:nk, :], raw[b][:, 0:nk, :], ACT.Copy).then_inc(whi_ready.sem, 1)

                def take(h, b, out, func=ACT.Copy):
                    act.wait_ge(unit_done.sem, unit_done.at(layer, 2 * h + (b + 1)))
                    act.activation(out, acc[b], func).then_inc(acc_taken[b].sem, 1)

                act.wait_ge(x_ready.sem, x_ready.at(layer, 0))
                for t in range(NT):
                    squares(layer, t, 0)
                act.wait_ge(rows_ready.sem, rows_ready.at(layer, 1))
                act.activation(gbc[:, :, :].rearrange("p s d -> p (s d)"), bank(4, 4), ACT.Copy).then_inc(rows_taken.sem, 1)
                act.wait_ge(rows_ready.sem, rows_ready.at(layer, 2))
                act.activation(g2mix[0:64, :], ps[0:64, 2048:3072], ACT.Copy)
                act.activation(g2mix[64:SL, :], ps[64:SL, 3072:4096], ACT.Copy).then_inc(rows_taken.sem, 1)
                for t in range(NT):
                    act.wait_ge(h32_ready.sem, h32_ready.at(layer, t + 1))
                    act.activation(hThi[:, :, t * P:(t + 1) * P], hb1[t % 2][:, :, :], ACT.Copy).then_inc(hi_ready.sem, 1)
                split(0, 0)
                with act.Fori(0, 2) as i:
                    split(i, 1)
                    take(i, 0, q[:, :, ds(i * (2 * UW), UW)])
                    split(i + 1, 0)
                    take(i, 1, q[:, :, ds(i * (2 * UW) + UW, UW)])
                split(2, 1)
                take(2, 0, k[:, :, :].rearrange("p t n -> p (t n)"))
                split(3, 0)
                take(2, 1, v[:, :, :].rearrange("p t n -> p (t n)"))
                for hf in range(2):
                    u = U_CONV + 3 * hf
                    split((u + 1) // 2, (u + 1) % 2)
                    if hf:
                        act.wait_ge(z_ready.sem, z_ready.at(layer, 1))
                    take(u // 2, u % 2, gcs[:, :, :].rearrange("p a n -> p (a n)"))
                    split((u + 2) // 2, (u + 2) % 2)
                    split((u + 3) // 2, (u + 3) % 2)
                    act.wait_ge(acc_taken[u % 2].sem, acc_taken[u % 2].at(layer, (u + 2) // 2 + 1))
                    act.activation(zhi[:, 2 * hf:2 * hf + 2, :], gcs[:, :, :], ACT.Copy).then_inc(zhi_ready.sem, 1)
                act.wait_ge(qk_ready.sem, qk_ready.at(layer, 1))
                act.sem_inc(waits_passed, 1)
                with act.Fori(0, 4) as i:
                    split(U_GATE // 2 + i, 1, KT // 2)
                    act.wait_ge(acc_taken[1].sem, acc_taken[1].at(layer, U_GATE // 2 + i))
                    take(U_GATE // 2 + i, 0, tw[:, :], ACT.Sigmoid)
                    split(U_GATE // 2 + 1 + i, 0)
                for j in range(4):
                    if j < 3:
                        if j:
                            split((U_GT + j + 1) // 2, (j + 1) % 2)
                        else:
                            split(U_GT // 2, 1)
                    take((U_GT + j) // 2, j % 2, G[:, 2 * j:2 * j + 2, :].rearrange("p a n -> p (a n)"), ACT.Sigmoid)
                act.wait_ge(unit_done.sem, unit_done.at(layer, U_AO))
                act.wait_ge(wlo_ready.sem, wlo_ready.at(layer, U_AO))
                act.wait_ge(cache_loaded.sem, cache_loaded.at(layer, 32))
                for kt in range(6):
                    src = ck[:, :] if kt == 0 else k[:, kt - 1, :]
                    act.wait_ge(ktp_ready.sem, ktp_ready.at(layer, kt))
                    act.activation(ksp[:, 0].bitcast(F32R), src.rearrange("p (v d) -> p v d", v=KV).unsqueeze(2).to_broadcast(
                        [P, KV, 2, HD]), ACT.Copy).then_inc(khi_ready.sem, 1)
                    act.wait_ge(ktp_ready.sem, ktp_ready.at(layer, kt + 1))
                    act.activation(kst[:, :, :, kt * P:(kt + 1) * P], tp[kt % 2].rearrange("p (s v n) -> p s v n", s=2, v=KV), ACT.Copy).then_inc(kst_ready.sem, 1)

                def attend(t, nk):
                    base = t * H
                    act.wait_ge(qt_ready.sem, qt_ready.at(layer, t * 4))
                    act.activation(qsp[:, :, 0, :].bitcast(F32R), q[:, ds(t, 1), :].rearrange("p o (h d) -> p (o h) d", h=H), ACT.Copy).then_inc(qhi_ready.sem, 1)

                    def queries(g):
                        act.wait_ge(qt_ready.sem, qt_ready.at(layer, t * 4 + (g + 1)))
                        act.wait_ge(s_ready.sem, s_ready.at(layer, base + (4 * g - 4)))
                        act.activation(qs[g % 2][:, :, :].rearrange("p h n -> p (h n)"), qtp, ACT.Copy).then_inc(qs_ready.sem, 1)

                    queries(0)
                    act.wait_ge(o_ready.sem, o_ready.at(layer, t * 2))
                    for j in range(H):
                        if j % 4 == 1 and j // 4 < 3:
                            queries(j // 4 + 1)
                        act.wait_ge(nmax_ready.sem, nmax_ready.at(layer, base + (j + 1)))
                        act.wait_ge(pt_ready.sem, pt_ready.at(layer, base + (j - 1)))
                        act.activation(prob[j % 2][:, 0:nk * P], scores[j % 2][:, 0:nk * P], ACT.Exp,
                                       bias=nmax[:, j % 2:j % 2 + 1], accum_out=rsum[:, j:j + 1]).then_inc(p_ready.sem, 1)
                    act.wait_ge(otp_ready.sem, otp_ready.at(layer, t + 1))
                    act.activation(oThi[:, :, ds(t * P, P)], bank(0, 2).rearrange("p (k n) -> p k n", k=KT), ACT.Copy).then_inc(ohi_ready.sem, 1)

                with act.Fori(0, LT) as t:
                    attend(t, 5)
                attend(LT, 1)
                act.wait_ge(oT_ready.sem, oT_ready.at(layer, NT))
                split(U_AO // 2, 0)
                for j in range(4):
                    split((U_AO + j + 1) // 2, (j + 1) % 2)
                    act.wait_ge(mrg_ready.sem, mrg_ready.at(layer, j + 1))
                    act.activation(mhi[:, 2 * j:2 * j + 2, :].rearrange("p a n -> p (a n)"), tw[:, :], ACT.Copy).then_inc(mhi_ready.sem, 1)
                for u in range(U_WO + 1, UNITS):
                    split(u // 2, u % 2)
                act.wait_ge(x_ready.sem, x_ready.at(layer, 1))
                for t in range(NT):
                    squares(layer, t, 1)
                for t in range(NT):
                    act.wait_ge(xn_ready.sem, xn_ready.at(layer, NT + t + 1))
                    act.activation(xnhi[:, t, :], xnb2[t % 2][:, :], ACT.Copy).then_inc(hi_ready.sem, 1)
                act.wait_ge(lgsub_ready.sem, lgsub_ready.at(layer, 1))
                copy2 = act.activation(lg[:, :, :], lg[:, :, :], ACT.Exp)
                copy2.then_inc(lgexp_ready.sem, 1)
                with act.Fori(0, E // 2) as p:
                    for e in range(2):
                        for b in range(2):
                            act.wait_ge(side_ready.sem, side_ready.at(layer, p * 18 + (3 + 2 * e + b + 1)))
                            out = ST[:, e, 0:LAT] if b == 0 else ST[:, e, LAT:T]
                            act.activation(out, side[(1 + b) % 2][0:SL, 0:LAT if b == 0 else CTX], ACT.Copy)\
                               .then_inc(side_taken[(1 + b) % 2].sem, 1)
                    for e in range(2):
                        u = p * 12 + 6 * e
                        act.wait_ge(ring_done.sem, ring_done.at(layer, u))
                        for b in range(2):
                            act.wait_ge(ring_done.sem, ring_done.at(layer, u + (2 * b + 1)))
                            act.activation(hid[:, 4 * b:4 * b + 4, :].rearrange("p a n -> p (a n)"), gate_ps[b],
                                           ACT.Silu).then_inc(silu_ready.sem, 1)
                        for b in range(2):
                            act.wait_ge(ym_ready.sem, ym_ready.at(layer, p * 4 + (2 * e + b + 1)))
                            act.activation(yhi[:, e, 512 * b:512 * (b + 1)], ym[:, :], ACT.Copy).then_inc(yhi_ready.sem, 1)
            act.wait_ge(x_ready.sem, x_ready.at(DEPTH, 0))
            for t in range(NT):
                squares(DEPTH, t, 0)

        @block.tensor
        def _(pe):
            for signal, n in ((unit_done, 2), (ktp_ready, 1), (qt_ready, 1), (s_ready, 4), (pt_ready, 2), (pv_done, 2),
                              (otp_ready, 1)):
                pe.sem_inc(signal.sem, n)
            pe.wait_ge(params_loaded, 160)
            pe.transpose(ps[:, 0:P], rowsA[:, :], ident[:, :])
            pe.transpose(ps[:, P:P + 40], rowsB[:, :], ident[0:40, 0:40]).then_inc(setup_tp, 1)
            pe.wait_ge(silu_c_ready, 1)
            with pe.Fori(0, 4) as i:
                pe.wait_ge(mod_taken, i + 1)
                for s in range(RING):
                    pe.wait_ge(ring_loaded[s].sem, i * 16 + 16)
                    for j in range(4):
                        col = 512 + 2 * (4 * s + j)
                        for kk in range(KT):
                            ins = pe.matmul(ps[:, col:col + 2], ring[s][:, kk, j * P:(j + 1) * P], sc[:, kk, :],
                                            start=(kk == 0), stop=(kk == KT - 1))
                    ins.then_inc(ring_done.sem, 1)

            with pe.Fori(0, DEPTH) as layer:
                pe.wait_ge(modl_ready.sem, modl_ready.at(layer, 1))
                for g in range(2):
                    if g:
                        pe.wait_ge(rows_taken.sem, rows_taken.at(layer, 1))
                    for s in range(2):
                        for j in range(KT):
                            col = modl[:, (16 + 24 * g + j):(17 + 24 * g + j), s].broadcast_to([P, P])
                            o = 2048 + 1024 * s + P * j
                            ins = pe.matmul(ps[:, o:o + P], col, ident[:, :], start=True, stop=True)
                    ins.then_inc(rows_ready.sem, 1)

                def transpose_tile(n, t, src):
                    pe.wait_ge(xn_ready.sem, xn_ready.at(layer, n * NT + t + 1))
                    if t >= 2:
                        pe.wait_ge(h32_ready.sem, h32_ready.at(layer, n * NT + t - 1))
                    for j in range(KT):
                        ins = pe.transpose(tp[t % 2][:, j * P:(j + 1) * P], src[:, j * P:(j + 1) * P], ident[:, :])
                    ins.then_inc(tp_ready.sem, 1)

                for t in range(NT):
                    transpose_tile(0, t, xnb1[t % 2])

                def columns(h, b, ahi, alo, nk=KT, k0=0):
                    pe.wait_ge(wlo_ready.sem, wlo_ready.at(layer, 2 * h + (b + 1)))
                    pe.wait_ge(acc_taken[b].sem, acc_taken[b].at(layer, h))
                    for a, pieces in ((0, ((0, 512), (512, T))), (1, ((0, 384), (384, T)))):
                        for kk in range(nk):
                            for n, (w, xx) in enumerate(((whi, ahi), (whi, alo), (wlo, ahi))):
                                for lo, hi in pieces:
                                    ins = pe.matmul(acc[b][:, a * T + lo:a * T + hi], w[b][:, kk, a * P:(a + 1) * P],
                                                    xx[:, k0 + kk, lo:hi], start=(kk == 0 and n == 0),
                                                    stop=(kk == nk - 1 and n == 2))
                    ins.then_inc(unit_done.sem, 1)

                def rows(h, b, ahi, alo):
                    pe.wait_ge(wlo_ready.sem, wlo_ready.at(layer, 2 * h + (b + 1)))
                    pe.wait_ge(acc_taken[b].sem, acc_taken[b].at(layer, h))
                    for t in range(NT):
                        for kk in range(KT):
                            for n, (w, xx) in enumerate(((whi, ahi), (wlo, ahi), (whi, alo))):
                                ins = pe.matmul(acc[b][:, t * UW:(t + 1) * UW], xx[:, kk, t * P:(t + 1) * P], w[b][:, kk, :],
                                                start=(kk == 0 and n == 0), stop=(kk == KT - 1 and n == 2))
                    ins.then_inc(unit_done.sem, 1)

                pe.wait_ge(lo_ready.sem, lo_ready.at(layer, NT))
                pe.sem_inc(waits_passed, 1)
                with pe.Fori(0, 3) as i:
                    for b in range(2):
                        rows(i, b, hThi, hTlo)
                with pe.Fori(0, 3) as i:
                    for b in range(2):
                        columns(U_CONV // 2 + i, b, hThi, hTlo)
                pe.wait_ge(z_ready.sem, z_ready.at(layer, 2))
                pe.sem_inc(waits_passed, 1)
                with pe.Fori(0, 4) as i:
                    columns(U_GATE // 2 + i, 0, hThi, hTlo)
                    columns(U_GATE // 2 + i, 1, zhi, zlo, KT // 2)
                with pe.Fori(0, 2) as i:
                    for b in range(2):
                        columns(U_GT // 2 + i, b, hThi, hTlo)

                for kt in range(6):
                    pe.wait_ge(ksplit.sem, ksplit.at(layer, kt + 1))
                    if kt >= 2:
                        pe.wait_ge(kst_ready.sem, kst_ready.at(layer, kt - 1))
                    for s in range(2):
                        for g in range(KV):
                            o = (s * KV + g) * P
                            ins = pe.transpose(tp[kt % 2][:, o:o + P], ksp[:, s, g].rearrange("p a d -> p (a d)"), ident[:, :])
                    ins.then_inc(ktp_ready.sem, 1)
                pe.wait_ge(kst_ready.sem, kst_ready.at(layer, 6))
                pe.sem_inc(waits_passed, 1)

                def attend(t, nk, key0):
                    base = t * H
                    n = nk * P
                    pe.wait_ge(qsplit.sem, qsplit.at(layer, t + 1))
                    pe.wait_ge(oT_ready.sem, oT_ready.at(layer, t))

                    def queries(g):
                        pe.wait_ge(qs_ready.sem, qs_ready.at(layer, t * 4 + g))
                        for h in range(4):
                            ins = pe.transpose(qtp[:, h * P:(h + 1) * P], qsp[:, 4 * g + h].rearrange("p a d -> p (a d)"),
                                               ident[:, :])
                        ins.then_inc(qt_ready.sem, 1)

                    queries(0)
                    for j in range(1, H + 4):
                        if j % 4 == 2 and j // 4 < 3:
                            queries(j // 4 + 1)
                        if j < H + 1:
                            i = j - 1
                            if i % 4 == 0:
                                pe.wait_ge(qs_ready.sem, qs_ready.at(layer, t * 4 + (i // 4 + 1)))
                            pe.wait_ge(p_ready.sem, p_ready.at(layer, base + (i - 1)))
                            for lo, hi in ((0, min(n, 512)), (512, n)):
                                if hi > lo:
                                    for s in range(2):
                                        ins = pe.matmul(scores[i % 2][:, lo:hi], qs[i // 4 % 2][:, i % 4, :],
                                                        kst[:, s, i // 4, key0 + lo:key0 + hi], start=(s == 0), stop=(s == 1))
                            ins.then_inc(s_ready.sem, 1)
                        if 3 <= j < H + 3:
                            i = j - 3
                            pe.wait_ge(p_ready.sem, p_ready.at(layer, base + (i + 1)))
                            pe.wait_ge(pts_ready.sem, pts_ready.at(layer, base + i))
                            for a in range(nk):
                                ins = pe.transpose(ptp[:, a * P:(a + 1) * P], prob[i % 2][:, a * P:(a + 1) * P], ident[:, :])
                            ins.then_inc(pt_ready.sem, 1)
                        if 4 <= j:
                            i = j - 4
                            pe.wait_ge(pts_ready.sem, pts_ready.at(layer, base + (i + 1)))
                            if i % 8 == 0:
                                pe.wait_ge(o_ready.sem, o_ready.at(layer, t * 2 + i // 8))
                            for a in range(nk):
                                g = i // 4
                                kt = key0 // P + a
                                vv = cv[:, g * HD:(g + 1) * HD] if kt == 0 else v[:, kt - 1, g * HD:(g + 1) * HD]
                                ins = pe.matmul(pso[:, i % 8 * HD:(i % 8 + 1) * HD], probT[i % 2][:, a, :], vv,
                                                start=(a == 0), stop=(a == nk - 1))
                            ins.then_inc(pv_done.sem, 1)
                    pe.wait_ge(o_ready.sem, o_ready.at(layer, t * 2 + 2))
                    for j in range(KT):
                        ins = pe.transpose(ps[:, j * P:(j + 1) * P], ot[:, j * P:(j + 1) * P], ident[:, :])
                    ins.then_inc(otp_ready.sem, 1)

                with pe.Fori(0, LT) as t:
                    attend(t, 5, 0)
                attend(LT, 1, PAST + LAT)

                pe.wait_ge(oT_ready.sem, oT_ready.at(layer, NT))
                pe.sem_inc(waits_passed, 1)
                with pe.Fori(0, 2) as i:
                    for b in range(2):
                        columns(U_AO // 2 + i, b, oThi, oTlo)
                pe.wait_ge(m_ready.sem, m_ready.at(layer, 4))
                pe.sem_inc(waits_passed, 1)
                with pe.Fori(0, 2) as i:
                    for b in range(2):
                        rows(U_WO // 2 + i, b, mhi, mlo)

                for t in range(NT + 1):
                    if t < NT:
                        transpose_tile(1, t, xnb2[t % 2])
                    if t:
                        r = t - 1
                        pe.wait_ge(h32_ready.sem, h32_ready.at(layer, NT + r + 1))
                        if r == 0:
                            pe.wait_ge(lp_loaded.sem, lp_loaded.at(layer, 48))
                        for kk in range(KT):
                            ins = pe.matmul(bank(4)[:, r * E:(r + 1) * E], hb2[r % 2][:, kk, :], wr[:, kk, :],
                                            start=(kk == 0), stop=(kk == KT - 1))
                        ins.then_inc(logits_done.sem, 1)
                pe.wait_ge(aff_ready.sem, aff_ready.at(layer, 1))
                for t in range(NT):
                    ins = pe.transpose(ps[0:E, 2560 + t * P:2560 + (t + 1) * P], aff[:, t, :], ident[:, :])
                ins.then_inc(affT_ready.sem, 1)
                pe.wait_ge(slots_ready.sem, slots_ready.at(layer, 1))
                pe.sem_inc(waits_passed, 1)
                for t in range(NT):
                    ins = pe.transpose(bank(7)[:, t * E:(t + 1) * E], work[:, t * P:(t + 1) * P], ident[0:E, 0:E])
                ins.then_inc(slotsT_ready.sem, 1)

                pe.wait_ge(lo_ready.sem, lo_ready.at(layer, 2 * NT))
                pe.sem_inc(waits_passed, 1)
                with pe.Fori(0, E // 2) as p:
                    def side_use(n):
                        pe.wait_ge(side_taken[n % 2].sem, side_taken[n % 2].at(layer, p * 9 + n // 2))
                        return side[n % 2]

                    pe.wait_ge(S_ready.sem, S_ready.at(layer, p + 1))
                    for g in range(3):
                        out = side_use(g)
                        for dd in range(3 * g, min(3 * g + 3, KT)):
                            for t in range(NT):
                                for n, part in enumerate((xnhi, xnlo)):
                                    o = (dd - 3 * g) * 2 * SL
                                    ins = pe.matmul(out[:, o:o + 2 * SL], part[:, t, dd * P:(dd + 1) * P],
                                                    S[:, t].rearrange("p e c -> p (e c)"), start=(t == 0 and n == 0),
                                                    stop=(t == NT - 1 and n == 1))
                        ins.then_inc(side_ready.sem, 1)
                    for e in range(2):
                        for b in range(2):
                            out = side_use(3 + 2 * e + b)
                            for n, t in enumerate(range(LT) if b == 0 else (LT,)):
                                ins = pe.transpose(out[0:SL, n * P:(n + 1) * P], f32(S[:, t, e, :]), ident[:, :])
                            ins.then_inc(side_ready.sem, 1)
                    out = side_use(7)
                    for e in range(2):
                        for t in range(NT):
                            ins = pe.matmul(out[0:SL, e:e + 1], f32(S[:, t, e, :]), aff[:, t, ds(p * 2 + e, 1)],
                                            start=(t == 0), stop=(t == NT - 1))
                    ins.then_inc(side_ready.sem, 1)
                    pe.wait_ge(side_taken[0].sem, side_taken[0].at(layer, p * 9 + 2))
                    for e in range(2):
                        for b in range(2):
                            for n, out in enumerate((gate_ps[b], up_ps[b])):
                                s = 2 * b + n
                                pe.wait_ge(ring_loaded[s].sem, ring_loaded[s].at(layer, p * 32 + 16 * (e + 1)))
                                free = silu_ready if n == 0 else hid_ready
                                pe.wait_ge(free.sem, free.at(layer, p * 4 + (2 * e + b - 1)))
                                for j in range(4):
                                    for kk in range(KT):
                                        ins = pe.matmul(out[:, j * SL:(j + 1) * SL], ring[s][:, kk, j * P:(j + 1) * P],
                                                        xsel[:, kk, e, :], start=(kk == 0), stop=(kk == KT - 1))
                                ins.then_inc(ring_done.sem, 1)
                        pe.wait_ge(hid_ready.sem, hid_ready.at(layer, p * 4 + 2 * e + 2))
                        for b in range(2):
                            pe.wait_ge(ring_loaded[4 + b].sem, ring_loaded[4 + b].at(layer, p * 32 + 16 * (e + 1)))
                            pe.wait_ge(ym_ready.sem, ym_ready.at(layer, p * 4 + (2 * e + b - 1)))
                            for kk in range(KT):
                                ins = pe.matmul(down_ps[b], hid[:, kk, :], ring[4 + b][:, kk, :],
                                                start=(kk == 0), stop=(kk == KT - 1))
                            ins.then_inc(ring_done.sem, 1)
                    pe.wait_ge(ylo_ready.sem, ylo_ready.at(layer, p * 4 + 4))
                    pe.wait_ge(side_taken[0].sem, side_taken[0].at(layer, p * 9 + 4))
                    for t in range(NT):
                        for b in range(2):
                            out = side_use(8 + 2 * t + b)
                            for n, (e, part) in enumerate(((0, yhi), (0, ylo), (1, yhi), (1, ylo))):
                                ins = pe.matmul(out[:, :], ST[:, e, t * P:(t + 1) * P], part[:, e, 512 * b:512 * (b + 1)],
                                                start=(n == 0), stop=(n == 3))
                            ins.then_inc(side_ready.sem, 1)

        @block.vector
        def _(dve):
            ch = Chain(dve, DVE_STEPS)
            for signal, n in ((wlo_ready, 2), (acc_taken[0], 1), (acc_taken[1], 1), (pts_ready, 1), (o_ready, 1),
                              (oT_ready, 1), (hid_ready, 2), (ym_ready, 2), (side_taken[0], 1), (side_taken[1], 1)):
                dve.sem_inc(signal.sem, n)
            dve.sem_inc(mod_taken, 1)
            dve.wait_ge(setup_tp, 1)
            dve.tensor_copy(colsA[:, :], ps[:, 0:P])
            dve.tensor_copy(colsB[:, :], ps[:, P:P + 40]).then_inc(cols_ready, 1)
            dve.wait_ge(cols_ready, 1)
            with dve.Fori(0, 4) as i:
                dve.wait_ge(ring_done.sem, i * RING + RING)
                dve.tensor_tensor(mod[:, ds(i * 24, 24), :], ps[:, 512:560].rearrange("p (a b) -> p a b", b=2),
                                  colsA[:, ds(i * 24, 24)].unsqueeze(2).to_broadcast([P, 24, 2]), ALU.add).then_inc(mod_taken, 1)
            dve.wait_ge(mod_taken, 5)
            dve.wait_ge(x_loaded, 32)
            dve.sem_inc(x_ready.sem, 1)

            with ch.layers() as layer:
                dve.tensor_copy(modl[:, :, :], mod[:, ds(layer * 48, 48), :]).then_inc(dve_chain, 1)
                dve.wait_ge(dve_chain, ch.next())
                dve.sem_inc(modl_ready.sem, 1)
                for A, n0, c0 in ((A1, 96, 8), (A2, 112, 32)):
                    g = colsA[:, ds(layer * 8 + n0, 8)].unsqueeze(2).to_broadcast([P, KT, 2])
                    dve.scalar_tensor_tensor(out=A[:, :, :], in0=modl[:, c0:c0 + 8, :], scalar=1.0, in1=g,
                                                     op0=ALU.add, op1=ALU.mult).then_inc(dve_chain, 1)
                    dve.wait_ge(dve_chain, ch.next())
                B1, B2 = modl[:, 0:8, :], modl[:, 24:32, :]

                def scale(n, t, xnb):
                    if t >= 2:
                        dve.wait_ge(tp_ready.sem, tp_ready.at(layer, n * NT + t - 1))
                        dve.wait_ge(lo_ready.sem, lo_ready.at(layer, n * NT + t - 1))
                    dve.tensor_scalar(xnb[t % 2][:, :], x[:, t, :], ss[:, n, t:t + 1], None, ALU.mult)\
                       .then_inc(xn_ready.sem, 1)

                def modulate(n, t, hb, A, B):
                    s = 0 if t < LT else 1
                    dve.wait_ge(tp_ready.sem, tp_ready.at(layer, n * NT + t + 1))
                    if n == 1 and t >= 2:
                        dve.wait_ge(logits_done.sem, logits_done.at(layer, t - 1))
                    wide = [P, KT, P]
                    dve.tensor_tensor(hb[t % 2][:, :, :], tp[t % 2].rearrange("p (k n) -> p k n", k=KT),
                                              A[:, :, s:s + 1].to_broadcast(wide), ALU.mult).then_inc(dve_chain, 1)
                    dve.wait_ge(dve_chain, ch.next())
                    dve.tensor_tensor(hb[t % 2][:, :, :], hb[t % 2][:, :, :], B[:, :, s:s + 1].to_broadcast(wide), ALU.add)\
                       .then_inc(h32_ready.sem, 1)

                dve.wait_ge(rstd_ready.sem, rstd_ready.at(layer, 1))
                scale(0, 0, xnb1)
                scale(0, 1, xnb1)
                for t in range(NT):
                    modulate(0, t, hb1, A1, B1)
                    dve.wait_ge(hi_ready.sem, hi_ready.at(layer, t + 1))
                    sl = slice(t * P, (t + 1) * P)
                    dve.tensor_tensor(hTlo[:, :, sl], hb1[t % 2][:, :, :], f32(hThi[:, :, sl]), ALU.subtract)\
                       .then_inc(lo_ready.sem, 1)
                    if t + 2 < NT:
                        scale(0, t + 2, xnb1)

                def split(h, b, nk=KT):
                    dve.wait_ge(whi_ready.sem, whi_ready.at(layer, 2 * h + (b + 1)))
                    dve.tensor_tensor(wlo[b][:, 0:nk, :], raw[b][:, 0:nk, :], f32(whi[b][:, 0:nk, :]), ALU.subtract)\
                       .then_inc(wlo_ready.sem, 1)

                def result(h, b):
                    dve.wait_ge(unit_done.sem, unit_done.at(layer, 2 * h + (b + 1)))
                    return acc[b]

                with dve.Fori(0, 3) as i:
                    for b in range(2):
                        split(i, b)

                def head_squares(src, nh, dst):
                    dve.tensor_tensor(t1[:, 0:nh * HD], src, src, ALU.mult).then_inc(dve_chain, 1)
                    dve.wait_ge(dve_chain, ch.next())
                    dve.tensor_reduce(dst, t1[:, 0:nh * HD].rearrange("p (h d) -> p h d", h=nh), AX.X, ALU.add).then_inc(dve_chain, 1)
                    dve.wait_ge(dve_chain, ch.next())

                def head_norm(src, t, nh, r, g, tc, tn, last=False):
                    v3 = src.rearrange("p (h d) -> p h d", h=nh)
                    wide = [P, nh, HD]
                    dve.tensor_tensor(v3, v3, r.unsqueeze(2).to_broadcast(wide), ALU.mult).then_inc(dve_chain, 1)
                    dve.wait_ge(dve_chain, ch.next())
                    if t == LT:
                        dve.tensor_tensor(v3, v3, g[:, :].unsqueeze(1).to_broadcast(wide), ALU.mult).then_inc(dve_chain, 1)
                        dve.wait_ge(dve_chain, ch.next())
                        return
                    a, bb = t1[:, 0:nh * HD], t2[:, 0:nh * HD]
                    dve.tensor_tensor(a.rearrange("p (h d) -> p h d", h=nh), v3, tc[:, t, :].unsqueeze(1).to_broadcast(wide),
                                      ALU.mult)
                    sv = src.rearrange("p (h s d) -> p h s d", h=2 * nh, s=2)
                    bv = bb.rearrange("p (h s d) -> p h s d", h=2 * nh, s=2)
                    tb = tn[:, t, :].rearrange("p (a s d) -> p a s d", a=2, s=2)
                    for s in range(2):
                        o = bv[:, :, s, :].rearrange("p (h a) d -> p h a d", a=2)
                        i0 = sv[:, :, 1 - s, :].rearrange("p (h a) d -> p h a d", a=2)
                        ins = dve.tensor_tensor(o, i0, tb[:, :, s, :].unsqueeze(1).to_broadcast([P, nh, 2, HALF]), ALU.mult)
                    ins.then_inc(dve_chain, 1)
                    dve.wait_ge(dve_chain, ch.next())
                    dve.tensor_tensor(src, a, bb, ALU.add).then_inc(dve_chain, 1)
                    dve.wait_ge(dve_chain, ch.next())

                def prepare(step):
                    if step == 0:
                        dve.wait_ge(acc_taken[0].sem, acc_taken[0].at(layer, 3))
                        dve.wait_ge(acc_taken[1].sem, acc_taken[1].at(layer, 3))
                        for t in range(NT):
                            head_squares(q[:, t, :], H, rq[:, t, :])
                    if step == 1:
                        for t in range(NT):
                            head_squares(k[:, t, :], KV, rk[:, t, :])
                        dve.sem_inc(ssq_ready.sem, 1)
                        dve.wait_ge(lp_loaded.sem, lp_loaded.at(layer, 48))
                        dve.tensor_scalar(gq[:, :], gq[:, :], HD ** -0.5, None, ALU.mult).then_inc(dve_chain, 1)
                        dve.wait_ge(dve_chain, ch.next())
                        for g, tc, tn in ((gq, qC, qS), (gk, kC, kS)):
                            dve.tensor_tensor(tc[:, :, :], cosT[:, :, :], g[:, :].unsqueeze(1).to_broadcast([P, LT, HD]), ALU.mult)
                            gv = g[:, :].rearrange("p (a s d) -> p a s d", a=2, s=2)
                            for t in range(LT):
                                sv = sinT[:, t, :].rearrange("p (a s d) -> p a s d", a=2, s=2)
                                tv = tn[:, t, :].rearrange("p (a s d) -> p a s d", a=2, s=2)
                                for s in range(2):
                                    ins = dve.tensor_tensor(tv[:, :, s, :], sv[:, :, s, :], gv[:, :, 1 - s, :], ALU.mult)
                            ins.then_inc(dve_chain, 1)
                            dve.wait_ge(dve_chain, ch.next())
                    if step == 2:
                        dve.wait_ge(rqk_ready.sem, rqk_ready.at(layer, 1))
                        for t in range(2):
                            head_norm(q[:, t, :], t, H, rq[:, t, :], gq, qC, qS)
                    if step == 3:
                        for t in range(2, 4):
                            head_norm(q[:, t, :], t, H, rq[:, t, :], gq, qC, qS)
                    if step == 4:
                        head_norm(q[:, LT, :], LT, H, rq[:, LT, :], gq, qC, qS)
                    if step == 5:
                        for t in range(NT):
                            head_norm(k[:, t, :], t, KV, rk[:, t, :], gk, kC, kS)
                        dve.sem_inc(qk_ready.sem, 1)

                for hf in range(2):
                    u = U_CONV + 3 * hf
                    split(u // 2, u % 2)
                    if hf == 0:
                        prepare(0)
                    else:
                        prepare(3)
                    split((u + 1) // 2, (u + 1) % 2)
                    if hf == 0:
                        prepare(1)
                    else:
                        prepare(4)
                    for col in (0, LAT + 1, T + 2):
                        dve.memset(ub[:, :, col:col + 1], 0.0)
                    dve.wait_ge(acc_taken[u % 2].sem, acc_taken[u % 2].at(layer, u // 2 + 1))
                    r = result((u + 1) // 2, (u + 1) % 2).rearrange("p (a n) -> p a n", a=2)
                    dve.tensor_tensor(ub[:, :, 1:LAT + 1], r[:, :, 0:LAT], gcs[:, :, 0:LAT], ALU.mult)
                    ins = dve.tensor_tensor(ub[:, :, LAT + 2:T + 2], r[:, :, LAT:T], gcs[:, :, LAT:T], ALU.mult)
                    ins.then_inc(acc_taken[(u + 1) % 2].sem, 1)
                    dve.wait_ge(acc_taken[(u + 1) % 2].sem, acc_taken[(u + 1) % 2].at(layer, (u + 1) // 2 + 1))
                    for tap, off in ((1, 1), (0, 0), (2, 2)):
                        for a in range(2):
                            w = colsB[:, ds(layer * 12 + (16 + 4 * tap + 2 * hf + a), 1)]
                            src, dst = ub[:, a, off:off + T + 1], cb[:, a, 1:T + 2]
                            if tap == 1:
                                ins = dve.tensor_scalar(dst, src, w, None, ALU.mult)
                            else:
                                ins = dve.scalar_tensor_tensor(out=dst, in0=src, scalar=w, in1=dst, op0=ALU.mult, op1=ALU.add)
                        ins.then_inc(dve_chain, 1)
                        dve.wait_ge(dve_chain, ch.next())
                    split((u + 2) // 2, (u + 2) % 2)
                    if hf == 0:
                        prepare(2)
                    else:
                        prepare(5)
                    r = result((u + 2) // 2, u % 2).rearrange("p (a n) -> p a n", a=2)
                    dve.tensor_tensor(gcs[:, :, 0:LAT], r[:, :, 0:LAT], cb[:, :, 1:LAT + 1], ALU.mult)
                    ins = dve.tensor_tensor(gcs[:, :, LAT:T], r[:, :, LAT:T], cb[:, :, LAT + 2:T + 2], ALU.mult)
                    ins.then_inc(acc_taken[u % 2].sem, 1)
                    dve.wait_ge(zhi_ready.sem, zhi_ready.at(layer, hf + 1))
                    dve.tensor_tensor(zlo[:, 2 * hf:2 * hf + 2, :], gcs[:, :, :], f32(zhi[:, 2 * hf:2 * hf + 2, :]), ALU.subtract)\
                       .then_inc(z_ready.sem, 1)
                with dve.Fori(0, 4) as i:
                    split(U_GATE // 2 + i, 0)
                    split(U_GATE // 2 + i, 1, KT // 2)
                    dve.wait_ge(acc_taken[0].sem, acc_taken[0].at(layer, U_GATE // 2 + 1 + i))
                    dve.tensor_tensor(m[:, ds(i * 2, 2), :].rearrange("p a n -> p (a n)"), result(U_GATE // 2 + i, 1), tw[:, :],
                                      ALU.mult).then_inc(acc_taken[1].sem, 1)
                with dve.Fori(0, 2) as i:
                    for b in range(2):
                        split(U_GT // 2 + i, b)
                dve.wait_ge(cache_loaded.sem, cache_loaded.at(layer, 32))
                dve.sem_inc(waits_passed, 1)
                for kt in range(6):
                    dve.wait_ge(khi_ready.sem, khi_ready.at(layer, kt + 1))
                    src = (ck[:, :] if kt == 0 else k[:, kt - 1, :]).rearrange("p (v d) -> p v d", v=KV)
                    for a in range(2):
                        ins = dve.tensor_tensor(ksp[:, 1, :, a, :], src, ksp[:, 0, :, a, :], ALU.subtract)
                    ins.then_inc(ksplit.sem, 1)

                def attend(t, nk):
                    base = t * H
                    dve.wait_ge(qhi_ready.sem, qhi_ready.at(layer, t + 1))
                    dve.tensor_tensor(qsp[:, :, 1, :], q[:, ds(t, 1), :].rearrange("p o (h d) -> p (o h) d", h=H),
                                      qsp[:, :, 0, :], ALU.subtract).then_inc(qsplit.sem, 1)

                    def normalise(half):
                        hs = slice(8 * half, 8 * half + 8)
                        dve.wait_ge(p_ready.sem, p_ready.at(layer, base + (8 * half + 8)))
                        dve.reciprocal(rinv[:, hs], rsum[:, hs]).then_inc(dve_chain, 1)
                        dve.wait_ge(dve_chain, ch.next())
                        dve.wait_ge(pv_done.sem, pv_done.at(layer, base + (8 * half + 8)))
                        if half == 0:
                            dve.wait_ge(otp_ready.sem, otp_ready.at(layer, t))
                        dve.tensor_tensor(ot[:, 512 * half:512 * (half + 1)].rearrange("p (h d) -> p h d", h=8),
                                          pso.rearrange("p (h d) -> p h d", h=8),
                                          rinv[:, hs].unsqueeze(2).to_broadcast([P, 8, HD]), ALU.mult).then_inc(o_ready.sem, 1)

                    for j in range(H + 2):
                        if j < H:
                            dve.wait_ge(s_ready.sem, s_ready.at(layer, base + (j + 1)))
                            dve.wait_ge(p_ready.sem, p_ready.at(layer, base + (j - 1)))
                            dve.tensor_reduce(nmax[:, j % 2:j % 2 + 1], scores[j % 2][:, 0:nk * P], AX.X, ALU.max, negate=True)\
                               .then_inc(nmax_ready.sem, 1)
                        if j == 11:
                            normalise(0)
                        if j >= 2:
                            i = j - 2
                            dve.wait_ge(pt_ready.sem, pt_ready.at(layer, base + (i + 1)))
                            dve.wait_ge(pv_done.sem, pv_done.at(layer, base + (i - 1)))
                            dve.tensor_copy(probT[i % 2][:, 0:nk, :].rearrange("p a n -> p (a n)"), ptp[:, 0:nk * P])\
                               .then_inc(pts_ready.sem, 1)
                    normalise(1)
                    dve.wait_ge(ohi_ready.sem, ohi_ready.at(layer, t + 1))
                    dve.tensor_tensor(oTlo[:, :, ds(t * P, P)], bank(0, 2).rearrange("p (k n) -> p k n", k=KT),
                                      f32(oThi[:, :, ds(t * P, P)]), ALU.subtract).then_inc(oT_ready.sem, 1)

                with ch.loop(LT, 2) as t:
                    attend(t, 5)
                attend(LT, 1)
                split(U_AO // 2, 0)
                for j in range(4):
                    h, b = (U_AO + j) // 2, j % 2
                    split((U_AO + j + 1) // 2, (j + 1) % 2)
                    if j:
                        dve.wait_ge(m_ready.sem, m_ready.at(layer, j))
                    g2 = G[:, 2 * j:2 * j + 2, :].rearrange("p a n -> p (a n)")
                    ins = dve.tensor_tensor(tw[:, :], result(h, b), g2, ALU.mult)
                    ins.then_inc(acc_taken[b].sem, 1)
                    dve.wait_ge(acc_taken[b].sem, acc_taken[b].at(layer, h + 1))
                    dve.tensor_tensor(tw[:, :], tw[:, :], m[:, 2 * j:2 * j + 2, :].rearrange("p a n -> p (a n)"), ALU.add)\
                       .then_inc(mrg_ready.sem, 1)
                    dve.wait_ge(mhi_ready.sem, mhi_ready.at(layer, j + 1))
                    dve.tensor_tensor(mlo[:, 2 * j:2 * j + 2, :].rearrange("p a n -> p (a n)"), tw[:, :],
                                      f32(mhi[:, 2 * j:2 * j + 2, :].rearrange("p a n -> p (a n)")), ALU.subtract)\
                       .then_inc(m_ready.sem, 1)
                dve.wait_ge(rows_taken.sem, rows_taken.at(layer, 2))
                t3 = tw[:, :].rearrange("p (t n) -> p t n", t=NT)
                for j in range(4):
                    h, b = (U_WO + j) // 2, j % 2
                    cols = slice(j * UW, (j + 1) * UW)
                    if j < 3:
                        split((U_WO + j + 1) // 2, (j + 1) % 2)
                    a3 = result(h, b).rearrange("p (t n) -> p t n", t=NT)
                    dve.tensor_tensor(t3[:, 0:LT, :], a3[:, 0:LT, :], gbc[:, 0, cols].unsqueeze(1).to_broadcast([P, LT, UW]), ALU.mult)
                    ins = dve.tensor_tensor(t3[:, LT, :], a3[:, LT, :], gbc[:, 1, cols], ALU.mult)
                    ins.then_inc(acc_taken[b].sem, 1)
                    dve.wait_ge(acc_taken[b].sem, acc_taken[b].at(layer, h + 1))
                    ins = dve.tensor_tensor(x[:, :, cols], x[:, :, cols], t3, ALU.add)
                    if j < 3:
                        ins.then_inc(dve_chain, 1)
                        dve.wait_ge(dve_chain, ch.next())
                    else:
                        ins.then_inc(x_ready.sem, 1)
                dve.wait_ge(rstd_ready.sem, rstd_ready.at(layer, 2))
                scale(1, 0, xnb2)
                scale(1, 1, xnb2)
                for t in range(NT):
                    modulate(1, t, hb2, A2, B2)
                    dve.wait_ge(hi_ready.sem, hi_ready.at(layer, NT + t + 1))
                    dve.tensor_tensor(xnlo[:, t, :], xnb2[t % 2][:, :], f32(xnhi[:, t, :]), ALU.subtract)\
                       .then_inc(lo_ready.sem, 1)
                    if t + 2 < NT:
                        scale(1, t + 2, xnb2)
                dve.wait_ge(logits_done.sem, logits_done.at(layer, NT))
                lps = bank(4)[:, 0:NT * E].rearrange("p (t e) -> p t e", t=NT)
                wide = [P, NT, E]
                dve.tensor_reduce(lgm[:, :], lps, AX.X, ALU.max).then_inc(dve_chain, 1)
                dve.wait_ge(dve_chain, ch.next())
                dve.tensor_tensor(lg[:, :, :], lps, lgm[:, :].unsqueeze(2).to_broadcast(wide), ALU.subtract)\
                   .then_inc(lgsub_ready.sem, 1)
                dve.wait_ge(lgexp_ready.sem, lgexp_ready.at(layer, 1))
                dve.tensor_reduce(lsum[:, :], lg[:, :, :], AX.X, ALU.add).then_inc(dve_chain, 1)
                dve.wait_ge(dve_chain, ch.next())
                dve.reciprocal(lsum[:, :], lsum[:, :]).then_inc(dve_chain, 1)
                dve.wait_ge(dve_chain, ch.next())
                dve.tensor_tensor(aff[:, :, :], lg[:, :, :], lsum[:, :].unsqueeze(2).to_broadcast(wide), ALU.mult)\
                   .then_inc(aff_ready.sem, 1)
                dve.wait_ge(affT_ready.sem, affT_ready.at(layer, 1))
                dve.tensor_copy(work[:, :], ps[0:E, 2560:2560 + T]).then_inc(dve_chain, 1)
                dve.wait_ge(dve_chain, ch.next())
                dve.sem_inc(waits_passed, 1)
                for lo, hi, cap in ((0, LAT, CAP_L), (LAT, T, CAP_C)):
                    for _ in range(cap // 8):
                        dve.max(top8[:, :], work[:, lo:hi]).then_inc(dve_chain, 1)
                        dve.wait_ge(dve_chain, ch.next())
                        dve.sem_inc(waits_passed, 1)
                        dve.match_replace(out=work[:, lo:hi], in_to_replace=top8[:, :],
                                                        in_values=work[:, lo:hi], imm_value=-1.0).then_inc(dve_chain, 1)
                        dve.wait_ge(dve_chain, ch.next())
                        dve.sem_inc(waits_passed, 1)
                dve.tensor_scalar(affT[:, :], work[:, :], 0.0, None, ALU.is_lt).then_inc(dve_chain, 1)
                dve.wait_ge(dve_chain, ch.next())
                for lo, hi, off in ((0, LAT, 0.0), (LAT, T, float(CAP_L))):
                    dve.tensor_tensor_scan(cum[:, lo:hi], affT[:, lo:hi], affT[:, lo:hi], 0.0, ALU.add, ALU.max).then_inc(dve_chain, 1)
                    dve.wait_ge(dve_chain, ch.next())
                    dve.scalar_tensor_tensor(out=work[:, lo:hi], in0=cum[:, lo:hi], scalar=off, in1=affT[:, lo:hi],
                                                     op0=ALU.add, op1=ALU.mult).then_inc(dve_chain, 1)
                    dve.wait_ge(dve_chain, ch.next())
                dve.tensor_scalar(work[:, :], work[:, :], -1.0, None, ALU.add).then_inc(slots_ready.sem, 1)
                dve.wait_ge(slotsT_ready.sem, slotsT_ready.at(layer, 1))
                dve.tensor_copy(slotT[:, :, :].rearrange("p t e -> p (t e)"), bank(7)[:, 0:NT * E]).then_inc(dve_chain, 1)
                dve.wait_ge(dve_chain, ch.next())
                dve.sem_inc(waits_passed, 1)
                with ch.loop(E // 2, PAIR_STEPS) as p:
                    dve.wait_ge(side_taken[1].sem, side_taken[1].at(layer, p * 9))
                    for t in range(NT):
                        ins = dve.tensor_tensor(S[:, t], slotT[:, t, ds(p * 2, 2)].unsqueeze(2).to_broadcast([P, 2, SL]),
                                                slot_ids[:, :].unsqueeze(1).to_broadcast([P, 2, SL]), ALU.is_equal)
                    ins.then_inc(S_ready.sem, 1)

                    def side_result(n):
                        dve.wait_ge(side_ready.sem, side_ready.at(layer, p * 18 + (n + 1)))
                        return side[n % 2]

                    for g in range(3):
                        src = side_result(g)
                        for dd in range(3 * g, min(3 * g + 3, KT)):
                            sv = src[:, (dd - 3 * g) * 2 * SL:(dd - 3 * g + 1) * 2 * SL].rearrange("p (e c) -> p e c", e=2)
                            for s, cs in ((0, slice(0, CAP_L)), (1, slice(CAP_L, SL))):
                                ins = dve.tensor_scalar(xsel[:, dd, :, cs], sv[:, :, cs], A2[:, dd, s:s + 1], B2[:, dd, s:s + 1],
                                                        ALU.mult, ALU.add)
                        ins.then_inc(side_taken[g % 2].sem, 1)
                    ins = dve.tensor_copy(vals[:, :], side_result(7)[0:SL, 0:2])
                    ins.then_inc(side_taken[1].sem, 1)
                    dve.wait_ge(side_taken[1].sem, side_taken[1].at(layer, p * 9 + 4))
                    for e in range(2):
                        for b in range(2):
                            dve.wait_ge(silu_ready.sem, silu_ready.at(layer, p * 4 + (2 * e + b + 1)))
                            dve.wait_ge(ring_done.sem, ring_done.at(layer, p * 12 + (6 * e + 2 * b + 2)))
                            hv = hid[:, 4 * b:4 * b + 4, :].rearrange("p a n -> p (a n)")
                            dve.tensor_tensor(hv, hv, up_ps[b], ALU.mult).then_inc(hid_ready.sem, 1)
                        for b in range(2):
                            dve.wait_ge(ring_done.sem, ring_done.at(layer, p * 12 + (6 * e + 5 + b)))
                            if e or b:
                                dve.wait_ge(ylo_ready.sem, ylo_ready.at(layer, p * 4 + (2 * e + b)))
                            cols = slice(512 * b, 512 * (b + 1))
                            dve.scalar_tensor_tensor(out=ym[:, :], in0=down_ps[b], scalar=vals[:, e:e + 1],
                                                     in1=g2mix[0:SL, cols], op0=ALU.mult, op1=ALU.mult).then_inc(ym_ready.sem, 1)
                            dve.wait_ge(yhi_ready.sem, yhi_ready.at(layer, p * 4 + (2 * e + b + 1)))
                            dve.tensor_tensor(ylo[:, e, cols], ym[:, :], f32(yhi[:, e, cols]), ALU.subtract)\
                               .then_inc(ylo_ready.sem, 1)
                    for t in range(NT):
                        for b in range(2):
                            src = side_result(8 + 2 * t + b)
                            xv = x[:, t, 512 * b:512 * (b + 1)]
                            dve.tensor_tensor(xv, xv, src, ALU.add).then_inc(side_taken[b].sem, 1)
                dve.wait_ge(side_taken[1].sem, side_taken[1].at(layer, 9 * E // 2))
                dve.sem_inc(x_ready.sem, 1)
            dve.wait_ge(fn_loaded, 16)
            dve.wait_ge(rstd_ready.sem, rstd_ready.at(DEPTH, 1))
            for t in range(NT):
                dve.scalar_tensor_tensor(out=x[:, t, :], in0=x[:, t, :], scalar=ss[:, 0, t:t + 1], in1=gbc[:, 0, :],
                                         op0=ALU.mult, op1=ALU.mult).then_inc(xn_ready.sem, 1)


DVE_STEPS = 113
PAIR_STEPS = 0

_INS = ["x_prompt", "x_sample", "cache_k", "cache_v", "c", "c_ctx", "w_mod", "b_mod", "norm1", "norm2", "w_in", "q_norm",
        "k_norm", "conv_w", "w_conv_out", "w_attn_out", "w_o", "w_router", "w_gate", "w_up", "w_down", "final_norm"]
_OUTS = [((1, CTX, D), "float32"), ((1, LAT, D), "float32"), ((1, DEPTH, CTX, KV, HD), "float32"),
         ((1, DEPTH, CTX, KV, HD), "float32")]


def constants():
    pos = np.arange(LAT)
    inv = (10000.0 ** (-np.arange(HALF, dtype=np.float32) / HALF)).astype(np.float32)
    cos, sin = np.zeros((LAT, 2, 2, HALF), np.float32), np.zeros((LAT, 2, 2, HALF), np.float32)
    for a, p in enumerate((pos // GRID_W, pos % GRID_W)):
        ang = p.astype(np.float32)[:, None] * inv[None, :]
        cos[:, a, :, :] = np.cos(ang)[:, None, :]
        sin[:, a, 0, :] = -np.sin(ang)
        sin[:, a, 1, :] = np.sin(ang)
    slots = np.broadcast_to(np.arange(SL, dtype=np.float32), (P, SL)).copy()
    return {"ident": np.eye(P, dtype=np.float32), "slots": slots, "cos": cos.reshape(LAT, HD), "sin": sin.reshape(LAT, HD)}


def kernel(**inputs):
    import concourse.bacc as _bacc
    from concourse import mybir as _mybir
    from concourse.bass_utils import run_bass_kernel_spmd as _run

    nc = _bacc.Bacc("TRN2", target_bir_lowering=False, num_devices=1)
    arrays, args = {}, []
    for name, a in [(n, np.ascontiguousarray(inputs[n])) for n in _INS] + list(constants().items()):
        arrays[f"in_{name}_dram"] = a
        args.append(nc.dram_tensor(f"in_{name}_dram", a.shape, _mybir.dt.from_np(a.dtype), kind="ExternalInput").ap())
    for i, (shape, dtype) in enumerate(_OUTS):
        args.append(nc.dram_tensor(f"out_{i}_dram", shape, _mybir.dt.from_np(np.dtype(dtype)), kind="ExternalOutput").ap())
    build(nc, *args)
    r = _run(nc, [arrays], core_ids=[0])
    return tuple(r.results[0][f"out_{i}_dram"] for i in range(len(_OUTS)))
```

```python
from contextlib import ExitStack, contextmanager

import numpy as np
import concourse.bass as bass
from concourse import mybir

F32 = mybir.dt.float32
F32R = mybir.dt.float32r
ALU = mybir.AluOpType
ACT = mybir.ActivationFunctionType
AX = mybir.AxisListType
ds = bass.ds

P = 128
D = 1024
KT = D // P
DEPTH = 2
LAT, CTX = 512, 128
T = LAT + CTX
NT = T // P
LT = LAT // P
H, KV, HD = 16, 4, 64
GRID_W = 64
QW, KVW, CW = H * HD, KV * HD, D // 2
E = 16
DE = 1024
CAP_L = 2 * LAT // E
CAP_C = 2 * CTX // E
SL = CAP_L + CAP_C
PAST = 128
EPS = 1e-6
KEYS = PAST + LAT + CTX
AXD = HD // 2
HALF = AXD // 2

UW = 256
U5 = NT * UW
OQ, OK_, OV = 0, QW, QW + KVW
OGB = QW + 2 * KVW
OGC, OXI = OGB + CW, OGB + 2 * CW
OGA = OGB + 3 * CW
OGT = OGA + D
U_Q, U_K, U_V, U_CONV, U_GATE, U_GT, U_AO, U_WO = 0, 4, 5, 6, 12, 20, 24, 28
UNITS = 32
RING = 6
HI = 4
KH = KT // 2
MOD_BLOCKS = DEPTH * 12
MOD_GROUPS = 4
EP = 12
PP = 2 * EP
EU = EP * E
PIECES = [(w, b, kh) for b in range(2) for w in range(2) for kh in range(2)] + [(2, b, kh) for kh in range(2) for b in range(2)]
ITEMS = NT * H


class Signal:

    def __init__(self, sem, per_layer, before=0):
        self.sem, self.per_layer, self.before = sem, per_layer, before

    def at(self, layer, n):
        return layer * self.per_layer + (self.before + n)


class Chain:

    def __init__(self, eng, per_layer):
        self.eng, self.per_layer, self.n, self.base = eng, per_layer, 0, 0

    def next(self):
        self.n += 1
        return self.base + self.n

    @contextmanager
    def loop(self, count, body):
        first, base = self.n, self.base
        with self.eng.Fori(0, count) as i:
            self.base = base + i * body
            yield i
        assert self.n - first == body, f"loop body: {self.n - first} steps"
        self.n, self.base = first + count * body, base

    @contextmanager
    def layers(self):
        first = self.n
        with self.eng.Fori(0, DEPTH) as layer:
            self.base = layer * self.per_layer
            yield layer
        assert self.n - first == self.per_layer, f"layer: {self.n - first} steps"
        self.n, self.base = first + DEPTH * self.per_layer, 0


def build(nc, x_prompt, x_sample, cache_k, cache_v, c, c_ctx, w_mod, b_mod, norm1, norm2, w_in, q_norm,
          k_norm, conv_w, w_conv_out, w_attn_out, w_o, w_router, w_gate, w_up, w_down, final_norm,
          ident_c, slots_c, cos_c, sin_c, y_prompt, y_sample, new_k, new_v):
    ctx = ExitStack()
    with ctx:
        KB = 1024
        B0 = 16640

        def at(name, shape, dt, off):
            return nc.alloc_sbuf_tensor_at(name, shape, dt, offset=B0 + off)

        x = at("x", [P, NT, D], F32, 0)
        gbc = at("gate1_rows", [P, 2, D], F32, 20 * KB)
        g2mix = at("gate2_rows", [P, D], F32, 28 * KB)
        bump = [32 * KB]

        def small(name, shape, dt=F32):
            t = at(name, shape, dt, bump[0])
            n = 4
            for s in shape[1:]:
                n *= s
            bump[0] += (n + 31) // 32 * 32
            assert bump[0] <= 44 * KB, bump
            return t

        ident = small("ident", [P, P])
        slot_ids = small("slot_ids", [P, SL])
        cosT = small("cosT", [P, LT, HD])
        sinT = small("sinT", [P, LT, HD])
        qC = small("qC", [P, LT, HD])
        qS = small("qS", [P, LT, HD])
        kC = small("kC", [P, LT, HD])
        kS = small("kS", [P, LT, HD])
        gq = small("gq", [P, HD])
        gk = small("gk", [P, HD])
        wr = small("wr", [P, KT, E])
        mod = small("mod", [P, DEPTH * 48, 2])
        modl = small("modl", [P, 48, 2])
        A1 = small("A1", [P, KT, 2])
        A2 = small("A2", [P, KT, 2])
        colsA = small("colsA", [P, P])
        colsB = small("colsB", [P, 40])
        sc = small("silu_c", [P, KT, 2])
        sc4 = small("silu_c_halves", [P, KT, 4], F32R)
        sum_halves = small("sum_halves", [4, 2])
        ss = small("ss", [P, 2, 8])
        rq = small("rq", [P, NT, H])
        rk = small("rk", [P, NT, KV])
        nmax = small("nmax", [P, 2])
        rsum = small("rsum", [P, H])
        rinv = small("rinv", [P, H])
        lgm = small("lgm", [P, NT])
        lg = small("lg", [P, NT, E])
        aff = small("aff", [P, NT, E])
        lsum = small("lsum", [P, NT])
        slotT = small("slotT", [P, NT, E + 2])
        top8 = small("top8", [E, 8])
        vals = small("vals", [SL, 2])
        minus_half = small("minus_half", [P, 1])

        ring = [at(f"ring{s}", [P, KH, 512], F32, (44 + 8 * s) * KB) for s in range(RING)]
        ring_lo = [at(f"ring_lo{s}", [P, KH, 512], F32R, (44 + 8 * s) * KB) for s in range(RING)]
        ring_hi = [at(f"ring_hi{s}", [P, KH, 512], F32R, (92 + 8 * s) * KB) for s in range(HI)]
        mod_rows = [at(f"mod_rows{s}", [4, 512], F32, (124 + 2 * s) * KB) for s in range(2)]
        raw = [at(f"raw{s}", [P, KT, UW], F32, (44 + 8 * s) * KB) for s in range(2)]
        whi = [at(f"whi{s}", [P, KT, UW], F32R, (60 + 8 * s) * KB) for s in range(2)]
        wlo = [at(f"wlo{s}", [P, KT, UW], F32R, (76 + 8 * s) * KB) for s in range(2)]
        hThi = at("hThi", [P, KT, T], F32R, 167 * KB)
        hTlo = at("hTlo", [P, KT, T], F32R, 187 * KB)
        oThi = at("oThi", [P, KT, T], F32R, 167 * KB)
        oTlo = at("oTlo", [P, KT, T], F32R, 187 * KB)
        xnhi = at("xnhi", [P, NT, D], F32R, 167 * KB)
        xnlo = at("xnlo", [P, NT, D], F32R, 187 * KB)
        mixed = at("mixed", [P, KT, T], F32, 92 * KB)
        gcs = at("gcs", [P, 2, T], F32, 92 * KB)
        ub = at("ub", [P, 2, T + 3], F32, 97 * KB)
        cb = at("cb", [P, 2, T + 3], F32, 97 * KB + 5152)
        t1 = at("t1", [P, D], F32, 97 * KB + 2 * 5152)
        rowsA = at("rowsA", [P, P], F32, 150 * KB)
        rowsB = at("rowsB", [40, P], F32, 151 * KB)
        xnb1 = [at(f"xnb1_{s}", [P, D], F32, (92 + 4 * s) * KB) for s in range(2)]
        hb1 = [at(f"hb1_{s}", [P, KT, P], F32, (100 + 4 * s) * KB) for s in range(2)]
        xnb2 = [at(f"xnb2_{s}", [P, D], F32, (140 + 4 * s) * KB) for s in range(2)]
        hb2 = [at(f"hb2_{s}", [P, KT, P], F32, (148 + 4 * s) * KB) for s in range(2)]
        zhi = at("zhi", [P, KT // 2, T], F32R, 112 * KB)
        zlo = at("zlo", [P, KT // 2, T], F32R, 122 * KB)
        G = at("G", [P, KT, T], F32, 112 * KB)
        mlo = at("mlo", [P, KT, T], F32R, 112 * KB)
        q = at("q", [P, NT, D], F32, 132 * KB)
        mhi = at("mhi", [P, KT, T], F32R, 132 * KB)
        k = at("k", [P, NT, KVW], F32, 152 * KB)
        v = at("v", [P, NT, KVW], F32, 157 * KB)
        t2 = at("t2", [P, D], F32, 162 * KB)
        tw = at("tw", [P, U5], F32, 162 * KB)
        prob = [at(f"prob{s}", [P, 5 * P], F32, 44 * KB + 2560 * s) for s in range(2)]
        probT = [at(f"probT{s}", [P, 5, P], F32, 49 * KB + 2560 * s) for s in range(2)]
        ot = at("ot", [P, D], F32, 54 * KB)
        qs = [at(f"qs{s}", [P, 4, P], F32R, (163 + 2 * s) * KB) for s in range(2)]
        ck = at("ck", [P, KVW], F32, 59 * KB)
        kst = at("kst", [P, 2, KV, KEYS], F32R, 60 * KB)
        qsp = at("qsp", [P, H, 2, HD], F32, 84 * KB)
        ksp = at("ksp", [P, 2, KV, 2, HD], F32, 49 * KB)
        cv = at("cv", [P, KVW], F32, 162 * KB)
        xsel = at("xsel", [P, KT, 2, SL], F32, 20 * KB)
        xlo = at("xlo", [P, KT, 2, SL], F32R, 20 * KB)
        hidhi = at("hidhi", [P, KT, SL], F32R, 25 * KB)
        xhi = at("xhi", [P, KT, 2, SL], F32R, 124 * KB)
        hid = [at(f"hid{s}", [SL, 512], F32, (129 + 2 * s) * KB) for s in range(2)]
        hidlo = at("hidlo", [P, KT, SL], F32R, 133 * KB)
        yhi = at("yhi", [SL, 2, D], F32R, 136 * KB)
        ym = at("ym", [SL, 2, D], F32, 144 * KB)
        ylo = at("ylo", [SL, 2, D], F32R, 144 * KB)
        S = at("S", [P, NT, 2, SL], F32R, 152 * KB)
        ST = at("ST", [SL, 2, T], F32R, 156 * KB)
        affT = at("affT", [E, T], F32, 156 * KB)
        work = at("work", [E, T], F32, 159 * KB)
        cum = at("cum", [E, T], F32, 162 * KB)

        ps = nc.alloc_psum_tensor("ps", [P, 8 * 512], F32)

        def bank(b, n=1):
            return ps[:, 512 * b:512 * (b + n)]

        acc = [ps[:, 0:U5], ps[:, 1536:1536 + U5]]
        tp = [bank(0, 2), bank(2, 2)]
        scores = [bank(0, 2), bank(2, 2)]
        ptp = ps[:, 2048:2048 + 5 * P]
        pso = bank(6)
        qtp = bank(7)
        gate_ps = [ps[0:SL, 0:512], ps[0:SL, 512:1024]]
        up_ps = [ps[0:SL, 1024:1536], ps[0:SL, 1536:2048]]
        hidT_ps = [bank(0)[:, 0:4 * SL], bank(1)[:, 0:4 * SL]]
        down_ps = [ps[0:SL, 2048:2560], ps[0:SL, 2560:3072]]
        side = [bank(6), bank(7)]

        def sem(name):
            return ctx.enter_context(nc.semaphore(name))

        waits_passed = sem("waits_passed")
        params_loaded = sem("params_loaded")
        x_loaded = sem("x_loaded")
        setup_tp = sem("setup_tp")
        cols_ready = sem("cols_ready")
        silu_c_ready = sem("silu_c_ready")
        mod_rows_ready = sem("mod_rows_ready")
        mod_cols_done = sem("mod_cols_done")
        mod_ready = sem("mod_ready")
        out_stored = sem("out_stored")
        fn_loaded = sem("fn_loaded")
        dve_chain = sem("dve_chain")
        pool_chain = sem("pool_chain")
        act_chain = sem("act_chain")

        def sig(name, per_layer, before=0):
            return Signal(sem(name), per_layer, before)

        lp_loaded = sig("lp_loaded", 16 * 3)
        cache_loaded = sig("cache_loaded", 16 * 2)
        kv_stored = sig("kv_stored", 16 * 2)
        raw_loaded = [sig(f"raw_loaded{s}", 16 * UNITS // 2) for s in range(2)]
        ring_loaded = [sig(f"ring_loaded{s}", 16 * EU // RING, 16 * 2 * MOD_BLOCKS // RING) for s in range(RING)]
        ring_split_hi = sig("ring_split_hi", EU, 2 * MOD_BLOCKS)
        ring_split_lo = sig("ring_split_lo", EU, 2 * MOD_BLOCKS)
        ring_done = sig("ring_done", EU, 2 * MOD_BLOCKS + HI)
        x_ready = sig("x_ready", 2, 1)
        modl_ready = sig("modl_ready", 1)
        rows_ready = sig("rows_ready", 2)
        rows_taken = sig("rows_taken", 2)
        sq_ready = sig("sq_ready", 10)
        rstd_ready = sig("rstd_ready", 2)
        xn_ready = sig("xn_ready", 10)
        tp_ready = sig("tp_ready", 10)
        h32_ready = sig("h32_ready", 10)
        hi_ready = sig("hi_ready", 10)
        lo_ready = sig("lo_ready", 10)
        logits_done = sig("logits_done", NT)
        whi_ready = sig("whi_ready", UNITS)
        wlo_ready = sig("wlo_ready", UNITS, 2)
        unit_done = sig("unit_done", UNITS, 2)
        acc_taken = [sig(f"acc_taken{s}", UNITS // 2, 1) for s in range(2)]
        ssq_ready = sig("ssq_ready", 1)
        rqk_ready = sig("rqk_ready", 1)
        qk_ready = sig("qk_ready", 1)
        zhi_ready = sig("zhi_ready", 2)
        z_ready = sig("z_ready", 2)
        khi_ready = sig("khi_ready", 6)
        ksplit = sig("ksplit", 6)
        ktp_ready = sig("ktp_ready", 6, 1)
        kst_ready = sig("kst_ready", 6)
        qhi_ready = sig("qhi_ready", NT)
        qsplit = sig("qsplit", NT)
        qt_ready = sig("qt_ready", ITEMS // 4, 1)
        qs_ready = sig("qs_ready", ITEMS // 4, 1)
        s_ready = sig("s_ready", ITEMS, 4)
        nmax_ready = sig("nmax_ready", ITEMS)
        p_ready = sig("p_ready", ITEMS, 2)
        pt_ready = sig("pt_ready", ITEMS, 2)
        pts_ready = sig("pts_ready", ITEMS, 1)
        pv_done = sig("pv_done", ITEMS, 2)
        o_ready = sig("o_ready", 2 * NT, 1)
        otp_ready = sig("otp_ready", NT, 1)
        ohi_ready = sig("ohi_ready", NT)
        oT_ready = sig("oT_ready", NT, 1)
        mrg_ready = sig("mrg_ready", 4)
        mhi_ready = sig("mhi_ready", 4)
        m_ready = sig("m_ready", 4)
        aff_ready = sig("aff_ready", 1)
        lgsub_ready = sig("lgsub_ready", 1)
        lgexp_ready = sig("lgexp_ready", 1)
        affT_ready = sig("affT_ready", 1)
        slots_ready = sig("slots_ready", 1)
        slotsT_ready = sig("slotsT_ready", 1)
        S_ready = sig("S_ready", E // 2 + 1)
        xhi_ready = sig("xhi_ready", 3 * E // 2)
        xlo_ready = sig("xlo_ready", 3 * E // 2)
        side_ready = sig("side_ready", 18 * E // 2, 10)
        side_taken = [sig(f"side_taken{s}", 9 * E // 2, 1) for s in range(2)]
        silu_ready = sig("silu_ready", 2 * E)
        hidT_ready = sig("hidT_ready", 2 * E)
        hidhi_ready = sig("hidhi_ready", 2 * E)
        hidlo_ready = sig("hidlo_ready", 2 * E, 2)
        hid_ready = sig("hid_ready", 2 * E, 2)
        ym_ready = sig("ym_ready", 2 * E, 2)
        yhi_ready = sig("yhi_ready", 2 * E)
        ylo_ready = sig("ylo_ready", 2 * E)

        def f32(ap):
            return ap.bitcast(F32)

        block = ctx.enter_context(nc.Block())

        @block.sync
        def _(sp):
            b_mod_rows = b_mod.rearrange("l (j p) -> (l j) p", p=P)
            for dst, src in ((rowsA[0:96, :], b_mod_rows),
                             (rowsA[96:112, :], norm1.rearrange("l (j p) -> (l j) p", p=P)),
                             (rowsA[112:128, :], norm2.rearrange("l (j p) -> (l j) p", p=P)),
                             (rowsB[0:8, :], c.rearrange("b (j p) -> (b j) p", p=P)),
                             (rowsB[8:16, :], c_ctx.rearrange("(j p) -> j p", p=P)),
                             (rowsB[16:40, :], conv_w.rearrange("l j (f p) -> (l j f) p", p=P)),
                             (ident[:, :], ident_c), (slot_ids[:, :], slots_c),
                             (cosT[:, :, :], cos_c.rearrange("(t p) d -> p t d", p=P)),
                             (sinT[:, :, :], sin_c.rearrange("(t p) d -> p t d", p=P))):
                sp.dma_start(dst, src).then_inc(params_loaded, 16)

            def mod_piece(n):
                layer, j, kh = n // 24, n % 24 // 2, n % 2
                src = w_mod[layer].rearrange("(k p) n -> p k n", p=P)
                sp.dma_start(ring[n % RING][:, :, :], src[:, KH * kh:KH * (kh + 1), 512 * j:512 * (j + 1)])\
                  .then_inc(ring_loaded[n % RING].sem, 16)

            for n in range(RING):
                mod_piece(n)
            sp.dma_start(x[:, 0:LT, :], x_sample[0].rearrange("(t p) d -> p t d", p=P)).then_inc(x_loaded, 16)
            sp.dma_start(x[:, LT, :], x_prompt[0]).then_inc(x_loaded, 16)
            for n in range(RING, 2 * MOD_BLOCKS):
                sp.wait_ge(ring_done.sem, HI + n + 1 - RING)
                mod_piece(n)

            with sp.Fori(0, DEPTH) as layer:
                one = ds(layer, 1)
                sp.wait_ge(x_ready.sem, x_ready.at(layer, 0))
                sp.dma_start(wr[:, :, :], w_router[one].rearrange("o (k p) e -> p (o k) e", p=P)).then_inc(lp_loaded.sem, 16)
                sp.dma_start(gq[:, :], q_norm[one, :].broadcast_to([P, HD])).then_inc(lp_loaded.sem, 16)
                sp.dma_start(gk[:, :], k_norm[one, :].broadcast_to([P, HD])).then_inc(lp_loaded.sem, 16)
                sp.wait_ge(ring_done.sem, ring_done.at(layer, 0))
                sp.sem_inc(waits_passed, 1)

                def unit(u, b, src):
                    sp.wait_ge(wlo_ready.sem, wlo_ready.at(layer, u - 1))
                    nk = src.shape[1]
                    sp.dma_start(raw[b][:, 0:nk, :], src).then_inc(raw_loaded[b].sem, 16)

                win = w_in[one].rearrange("o (k p) n -> p (o k) n", p=P)
                wco = w_conv_out[one].rearrange("o (k p) n -> p (o k) n", p=P)
                wao = w_attn_out[one].rearrange("o (k p) n -> p (o k) n", p=P)
                woo = w_o[one].rearrange("o (k p) n -> p (o k) n", p=P)
                with sp.Fori(0, 2) as i:
                    for b in range(2):
                        unit(U_Q + 2 * i + b, b, win[:, :, ds(OQ + (2 * i + b) * UW, UW)])
                unit(U_K, 0, win[:, :, OK_:OK_ + UW])
                unit(U_V, 1, win[:, :, OV:OV + UW])
                for hf in range(2):
                    for j, o in enumerate((OGC, OXI, OGB)):
                        u = U_CONV + 3 * hf + j
                        unit(u, u % 2, win[:, :, o + hf * UW:o + (hf + 1) * UW])
                with sp.Fori(0, 4) as i:
                    unit(U_GATE + 2 * i, 0, win[:, :, ds(OGA + i * UW, UW)])
                    unit(U_GATE + 2 * i + 1, 1, wco[:, :, ds(i * UW, UW)])
                sp.wait_ge(qk_ready.sem, qk_ready.at(layer, 1))
                nk_dst = new_k[0][one].rearrange("l s h d -> (l s) (h d)")
                nv_dst = new_v[0][one].rearrange("l s h d -> (l s) (h d)")
                sp.dma_start(nk_dst, k[:, LT, :]).then_inc(kv_stored.sem, 16)
                sp.dma_start(nv_dst, v[:, LT, :]).then_inc(kv_stored.sem, 16)
                with sp.Fori(0, 2) as i:
                    for b in range(2):
                        unit(U_GT + 2 * i + b, b, win[:, :, ds(OGT + (2 * i + b) * UW, UW)])
                sp.wait_ge(wlo_ready.sem, wlo_ready.at(layer, U_AO))
                for b in range(2):
                    sp.wait_ge(acc_taken[b].sem, acc_taken[b].at(layer, U_AO // 2))
                sp.dma_start(ck[:, :], cache_k[0][one].rearrange("l s h d -> (l s) (h d)")).then_inc(cache_loaded.sem, 16)
                sp.dma_start(cv[:, :], cache_v[0][one].rearrange("l s h d -> (l s) (h d)")).then_inc(cache_loaded.sem, 16)
                sp.wait_ge(oT_ready.sem, oT_ready.at(layer, NT))
                sp.sem_inc(waits_passed, 1)
                with sp.Fori(0, 2) as i:
                    for b in range(2):
                        unit(U_AO + 2 * i + b, b, wao[:, :, ds((2 * i + b) * UW, UW)])
                with sp.Fori(0, 2) as i:
                    for b in range(2):
                        unit(U_WO + 2 * i + b, b, woo[:, :, ds((2 * i + b) * UW, UW)])
                sp.wait_ge(kv_stored.sem, kv_stored.at(layer, 32))
                sp.sem_inc(waits_passed, 1)
                sp.wait_ge(x_ready.sem, x_ready.at(layer, 1))
                sp.sem_inc(waits_passed, 1)
                with sp.Fori(0, E) as e:
                    for n, (w, b, kh) in enumerate(PIECES):
                        sp.wait_ge(ring_done.sem, ring_done.at(layer, EP * e + (n + 1 - RING)))
                        src = (w_gate, w_up, w_down)[w][one][:, ds(e, 1)].rearrange("l e (k p) n -> p (l e k) n", p=P)
                        sp.dma_start(ring[n % RING][:, :, :], src[:, KH * kh:KH * (kh + 1), b * 512:(b + 1) * 512])\
                          .then_inc(ring_loaded[n % RING].sem, 16)

            sp.wait_ge(x_ready.sem, x_ready.at(DEPTH, 0))
            sp.dma_start(gbc[:, 0, :], final_norm.rearrange("(o d) -> o d", o=1).broadcast_to([P, D])).then_inc(fn_loaded, 16)
            ys = y_sample[0].rearrange("(t p) d -> p t d", p=P)
            for t in range(NT):
                sp.wait_ge(xn_ready.sem, xn_ready.at(DEPTH, t + 1))
                sp.dma_start(ys[:, t, :] if t < LT else y_prompt[0], x[:, t, :]).then_inc(out_stored, 16)
            sp.wait_ge(out_stored, 16 * NT)

        @block.gpsimd
        def _(pool):
            ch = Chain(pool, 5)

            def rsqrt(ap, n, done):
                pool.tensor_scalar(ap, ap, 1.0 / n, EPS, ALU.mult, ALU.add).then_inc(pool_chain, 1)
                pool.wait_ge(pool_chain, ch.next())
                pool.tensor_tensor(ap, ap, minus_half[:, 0:1].broadcast_to(list(ap.shape)), ALU.pow).then_inc(done, 1)

            pool.memset(minus_half[:, :], -0.5).then_inc(pool_chain, 1)
            ch.n = 1
            pool.wait_ge(pool_chain, 1)
            with ch.layers() as layer:
                pool.wait_ge(sq_ready.sem, sq_ready.at(layer, NT))
                pool.sem_inc(waits_passed, 1)
                rsqrt(ss[:, 0, 0:NT], D, rstd_ready.sem)
                pool.wait_ge(ssq_ready.sem, ssq_ready.at(layer, 1))
                pool.sem_inc(waits_passed, 1)
                pool.tensor_scalar(rq[:, :, :], rq[:, :, :], 1.0 / HD, EPS, ALU.mult, ALU.add).then_inc(pool_chain, 1)
                pool.wait_ge(pool_chain, ch.next())
                pool.tensor_tensor(rq[:, :, :].rearrange("p t h -> p (t h)"), rq[:, :, :].rearrange("p t h -> p (t h)"),
                                                 minus_half[:, 0:1].broadcast_to([P, NT * H]), ALU.pow).then_inc(pool_chain, 1)
                pool.wait_ge(pool_chain, ch.next())
                pool.sem_inc(waits_passed, 1)
                rsqrt(rk[:, :, :].rearrange("p t h -> p (t h)"), HD, rqk_ready.sem)
                pool.wait_ge(sq_ready.sem, sq_ready.at(layer, 2 * NT))
                pool.sem_inc(waits_passed, 1)
                rsqrt(ss[:, 1, 0:NT], D, rstd_ready.sem)
            pool.wait_ge(sq_ready.sem, sq_ready.at(DEPTH, NT))
            rsqrt(ss[:, 0, 0:NT], D, rstd_ready.sem)

        @block.scalar
        def _(act):
            act.sem_inc(qs_ready.sem, 1)
            act.sem_inc(p_ready.sem, 2)
            act.wait_ge(cols_ready, 1)
            for s in range(2):
                ins = act.activation(sc[:, :, s], colsB[:, 8 * s:8 * s + 8], ACT.Silu)
            ins.then_inc(act_chain, 1)
            act.sem_inc(mod_rows_ready, 2)
            act.wait_ge(act_chain, 1)
            act.activation(sc4[:, :, 0:2], sc[:, :, :], ACT.Copy).then_inc(silu_c_ready, 1)
            with act.Fori(0, MOD_GROUPS) as i:
                for n in range(EP):
                    act.wait_ge(ring_loaded[n % RING].sem, i * 32 + 16 * (n // RING + 1))
                    act.wait_ge(ring_done.sem, i * EP + (n + 1))
                    act.activation(ring_hi[n % HI][:, :, :], ring[n % RING][:, :, :], ACT.Copy).then_inc(ring_split_hi.sem, 1)
                    for j in {5: (0,), 7: (1,), 9: (2,), 11: (3, 4, 5)}.get(n, ()):
                        act.wait_ge(ring_done.sem, i * EP + (HI + 2 * j + 2))
                        act.wait_ge(mod_cols_done, i * 6 + (j + 1))
                        act.activation(mod_rows[j % 2][:, :], ps[0:4, 512 * (j % 2):512 * (j % 2 + 1)], ACT.Copy)                           .then_inc(mod_rows_ready, 1)

            def squares(layer, t, row):
                if t >= 2:
                    act.wait_ge(sq_ready.sem, sq_ready.at(layer, NT * row + t - 1))
                act.activation(tp[t % 2], x[:, t, :], ACT.Square, accum_out=ss[:, row, t:t + 1]).then_inc(sq_ready.sem, 1)

            with act.Fori(0, DEPTH) as layer:
                def split(h, b, nk=KT):
                    act.wait_ge(raw_loaded[b].sem, raw_loaded[b].at(layer, (h + 1) * 16))
                    act.wait_ge(unit_done.sem, unit_done.at(layer, 2 * h + (b - 1)))
                    act.activation(whi[b][:, 0:nk, :], raw[b][:, 0:nk, :], ACT.Copy).then_inc(whi_ready.sem, 1)

                def take(h, b, out, func=ACT.Copy):
                    act.wait_ge(unit_done.sem, unit_done.at(layer, 2 * h + (b + 1)))
                    act.activation(out, acc[b], func).then_inc(acc_taken[b].sem, 1)

                act.wait_ge(x_ready.sem, x_ready.at(layer, 0))
                for t in range(NT):
                    squares(layer, t, 0)
                act.wait_ge(rows_ready.sem, rows_ready.at(layer, 1))
                act.activation(gbc[:, :, :].rearrange("p s d -> p (s d)"), bank(4, 4), ACT.Copy).then_inc(rows_taken.sem, 1)
                act.wait_ge(rows_ready.sem, rows_ready.at(layer, 2))
                act.activation(g2mix[0:64, :], ps[0:64, 2048:3072], ACT.Copy)
                act.activation(g2mix[64:SL, :], ps[64:SL, 3072:4096], ACT.Copy).then_inc(rows_taken.sem, 1)
                for t in range(NT):
                    act.wait_ge(h32_ready.sem, h32_ready.at(layer, t + 1))
                    act.activation(hThi[:, :, t * P:(t + 1) * P], hb1[t % 2][:, :, :], ACT.Copy).then_inc(hi_ready.sem, 1)
                split(0, 0)
                with act.Fori(0, 2) as i:
                    split(i, 1)
                    take(i, 0, q[:, :, ds(i * (2 * UW), UW)])
                    split(i + 1, 0)
                    take(i, 1, q[:, :, ds(i * (2 * UW) + UW, UW)])
                split(2, 1)
                take(2, 0, k[:, :, :].rearrange("p t n -> p (t n)"))
                split(3, 0)
                take(2, 1, v[:, :, :].rearrange("p t n -> p (t n)"))
                for hf in range(2):
                    u = U_CONV + 3 * hf
                    split((u + 1) // 2, (u + 1) % 2)
                    if hf:
                        act.wait_ge(z_ready.sem, z_ready.at(layer, 1))
                    take(u // 2, u % 2, gcs[:, :, :].rearrange("p a n -> p (a n)"))
                    split((u + 2) // 2, (u + 2) % 2)
                    split((u + 3) // 2, (u + 3) % 2)
                    act.wait_ge(acc_taken[u % 2].sem, acc_taken[u % 2].at(layer, (u + 2) // 2 + 1))
                    act.activation(zhi[:, 2 * hf:2 * hf + 2, :], gcs[:, :, :], ACT.Copy).then_inc(zhi_ready.sem, 1)
                act.wait_ge(qk_ready.sem, qk_ready.at(layer, 1))
                act.sem_inc(waits_passed, 1)
                with act.Fori(0, 4) as i:
                    split(U_GATE // 2 + i, 1, KT // 2)
                    act.wait_ge(acc_taken[1].sem, acc_taken[1].at(layer, U_GATE // 2 + i))
                    take(U_GATE // 2 + i, 0, tw[:, :], ACT.Sigmoid)
                    split(U_GATE // 2 + 1 + i, 0)
                for j in range(4):
                    if j < 3:
                        if j:
                            split((U_GT + j + 1) // 2, (j + 1) % 2)
                        else:
                            split(U_GT // 2, 1)
                    take((U_GT + j) // 2, j % 2, G[:, 2 * j:2 * j + 2, :].rearrange("p a n -> p (a n)"), ACT.Sigmoid)
                act.wait_ge(unit_done.sem, unit_done.at(layer, U_AO))
                act.wait_ge(wlo_ready.sem, wlo_ready.at(layer, U_AO))
                act.wait_ge(cache_loaded.sem, cache_loaded.at(layer, 32))
                for kt in range(6):
                    src = ck[:, :] if kt == 0 else k[:, kt - 1, :]
                    act.wait_ge(ktp_ready.sem, ktp_ready.at(layer, kt))
                    act.activation(ksp[:, 0].bitcast(F32R), src.rearrange("p (v d) -> p v d", v=KV).unsqueeze(2).to_broadcast(
                        [P, KV, 2, HD]), ACT.Copy).then_inc(khi_ready.sem, 1)
                    act.wait_ge(ktp_ready.sem, ktp_ready.at(layer, kt + 1))
                    act.activation(kst[:, :, :, kt * P:(kt + 1) * P], tp[kt % 2].rearrange("p (s v n) -> p s v n", s=2, v=KV), ACT.Copy).then_inc(kst_ready.sem, 1)

                def attend(t, nk):
                    base = t * H
                    act.wait_ge(qt_ready.sem, qt_ready.at(layer, t * 4))
                    act.activation(qsp[:, :, 0, :].bitcast(F32R), q[:, ds(t, 1), :].rearrange("p o (h d) -> p (o h) d", h=H), ACT.Copy).then_inc(qhi_ready.sem, 1)

                    def queries(g):
                        act.wait_ge(qt_ready.sem, qt_ready.at(layer, t * 4 + (g + 1)))
                        act.wait_ge(s_ready.sem, s_ready.at(layer, base + (4 * g - 4)))
                        act.activation(qs[g % 2][:, :, :].rearrange("p h n -> p (h n)"), qtp, ACT.Copy).then_inc(qs_ready.sem, 1)

                    queries(0)
                    act.wait_ge(o_ready.sem, o_ready.at(layer, t * 2))
                    for j in range(H):
                        if j % 4 == 1 and j // 4 < 3:
                            queries(j // 4 + 1)
                        act.wait_ge(nmax_ready.sem, nmax_ready.at(layer, base + (j + 1)))
                        act.wait_ge(pt_ready.sem, pt_ready.at(layer, base + (j - 1)))
                        act.activation(prob[j % 2][:, 0:nk * P], scores[j % 2][:, 0:nk * P], ACT.Exp,
                                       bias=nmax[:, j % 2:j % 2 + 1], accum_out=rsum[:, j:j + 1]).then_inc(p_ready.sem, 1)
                    act.wait_ge(otp_ready.sem, otp_ready.at(layer, t + 1))
                    act.activation(oThi[:, :, ds(t * P, P)], bank(0, 2).rearrange("p (k n) -> p k n", k=KT), ACT.Copy).then_inc(ohi_ready.sem, 1)

                with act.Fori(0, LT) as t:
                    attend(t, 5)
                attend(LT, 1)
                act.wait_ge(oT_ready.sem, oT_ready.at(layer, NT))
                split(U_AO // 2, 0)
                for j in range(4):
                    split((U_AO + j + 1) // 2, (j + 1) % 2)
                    act.wait_ge(mrg_ready.sem, mrg_ready.at(layer, j + 1))
                    act.activation(mhi[:, 2 * j:2 * j + 2, :].rearrange("p a n -> p (a n)"), tw[:, :], ACT.Copy).then_inc(mhi_ready.sem, 1)
                for u in range(U_WO + 1, UNITS):
                    split(u // 2, u % 2)
                act.wait_ge(x_ready.sem, x_ready.at(layer, 1))
                for t in range(NT):
                    squares(layer, t, 1)
                for t in range(NT):
                    act.wait_ge(xn_ready.sem, xn_ready.at(layer, NT + t + 1))
                    act.activation(xnhi[:, t, :], xnb2[t % 2][:, :], ACT.Copy).then_inc(hi_ready.sem, 1)
                act.wait_ge(lgsub_ready.sem, lgsub_ready.at(layer, 1))
                copy2 = act.activation(lg[:, :, :], lg[:, :, :], ACT.Exp)
                copy2.then_inc(lgexp_ready.sem, 1)
                with act.Fori(0, E // 2) as p:
                    for m in range(PP + 4):
                        for e, r in ((0, m), (1, m - EP)):
                            if r in (9, 12):
                                b = int(r == 12)
                                act.wait_ge(hidT_ready.sem, hidT_ready.at(layer, p * 4 + (2 * e + b + 1)))
                                act.activation(hidhi[:, 4 * b:4 * b + 4, :].rearrange("p a n -> p (a n)"), hidT_ps[b],
                                               ACT.Copy).then_inc(hidhi_ready.sem, 1)
                        if m < PP:
                            act.wait_ge(ring_loaded[m % RING].sem, ring_loaded[m % RING].at(layer, p * 64 + 16 * (m // RING + 1)))
                            act.wait_ge(ring_done.sem, ring_done.at(layer, p * PP + (m + 1 - HI)))
                            act.activation(ring_hi[m % HI][:, :, :], ring[m % RING][:, :, :], ACT.Copy).then_inc(ring_split_hi.sem, 1)
                        if m == 3:
                            for g in range(3):
                                act.wait_ge(side_taken[g % 2].sem, side_taken[g % 2].at(layer, p * 9 + (g // 2 + 1)))
                                kk = slice(3 * g, min(3 * g + 3, KT))
                                act.activation(xhi[:, kk], xsel[:, kk], ACT.Copy).then_inc(xhi_ready.sem, 1)
                            for e in range(2):
                                for b in range(2):
                                    n = 3 + 2 * e + b
                                    act.wait_ge(side_ready.sem, side_ready.at(layer, p * 18 + (n + 1)))
                                    out = ST[:, e, 0:LAT] if b == 0 else ST[:, e, LAT:T]
                                    act.activation(out, side[n % 2][0:SL, 0:LAT if b == 0 else CTX], ACT.Copy)\
                                       .then_inc(side_taken[n % 2].sem, 1)
                        for e, r in ((0, m), (1, m - EP)):
                            if r in (5, 9):
                                b = int(r == 9)
                                act.wait_ge(ring_done.sem, ring_done.at(layer, p * PP + (EP * e + 4 * b + 2)))
                                act.activation(hid[b][:, :], gate_ps[b], ACT.Silu).then_inc(silu_ready.sem, 1)
                            if r in (14, 15):
                                b = r - 14
                                act.wait_ge(ym_ready.sem, ym_ready.at(layer, p * 4 + (2 * e + b + 1)))
                                cols = slice(512 * b, 512 * (b + 1))
                                act.activation(yhi[:, e, cols], ym[:, e, cols], ACT.Copy).then_inc(yhi_ready.sem, 1)
            act.wait_ge(x_ready.sem, x_ready.at(DEPTH, 0))
            for t in range(NT):
                squares(DEPTH, t, 0)

        @block.tensor
        def _(pe):
            for signal, n in ((unit_done, 2), (ktp_ready, 1), (qt_ready, 1), (s_ready, 4), (pt_ready, 2), (pv_done, 2),
                              (otp_ready, 1), (side_ready, 10), (ring_done, HI)):
                pe.sem_inc(signal.sem, n)
            pe.sem_inc(mod_cols_done, 2)
            pe.wait_ge(params_loaded, 160)
            pe.transpose(ps[:, 0:P], rowsA[:, :], ident[:, :])
            pe.transpose(ps[:, P:P + 40], rowsB[:, :], ident[0:40, 0:40]).then_inc(setup_tp, 1)
            pe.wait_ge(silu_c_ready, 2)
            with pe.Fori(0, MOD_GROUPS) as i:
                def mod_columns(j):
                    pe.wait_ge(mod_rows_ready, i * 6 + (j + 3))
                    for a in range(4):
                        ins = pe.matmul(ps[:, ds(i * 48 + (1024 + 2 * (4 * j + a)), 2)], mod_rows[j % 2][:, a * P:(a + 1) * P],
                                        sum_halves[:, :], start=True, stop=True)
                    ins.then_inc(mod_cols_done, 1)

                for j in range(6):
                    pe.wait_ge(mod_rows_ready, i * 6 + (j + 1))
                    for kh in range(2):
                        n = 2 * j + kh
                        pe.wait_ge(ring_split_lo.sem, i * EP + (n + 1))
                        for kk in range(KH):
                            for w in (ring_hi[n % HI], ring_lo[n % RING]):
                                ins = pe.matmul(ps[0:4, 512 * (j % 2):512 * (j % 2 + 1)], sc4[:, KH * kh + kk, :], w[:, kk, :],
                                                start=(n % 2 == 0 and kk == 0 and w is ring_hi[n % HI]),
                                                stop=(kh == 1 and kk == KH - 1 and w is ring_lo[n % RING]))
                        ins.then_inc(ring_done.sem, 1)
                    if j:
                        mod_columns(j - 1)
                mod_columns(5)

            with pe.Fori(0, DEPTH) as layer:
                pe.wait_ge(modl_ready.sem, modl_ready.at(layer, 1))
                for g in range(2):
                    if g:
                        pe.wait_ge(rows_taken.sem, rows_taken.at(layer, 1))
                    for s in range(2):
                        for j in range(KT):
                            col = modl[:, (16 + 24 * g + j):(17 + 24 * g + j), s].broadcast_to([P, P])
                            o = 2048 + 1024 * s + P * j
                            ins = pe.matmul(ps[:, o:o + P], col, ident[:, :], start=True, stop=True)
                    ins.then_inc(rows_ready.sem, 1)

                def transpose_tile(n, t, src):
                    pe.wait_ge(xn_ready.sem, xn_ready.at(layer, n * NT + t + 1))
                    if t >= 2:
                        pe.wait_ge(h32_ready.sem, h32_ready.at(layer, n * NT + t - 1))
                    for j in range(KT):
                        ins = pe.transpose(tp[t % 2][:, j * P:(j + 1) * P], src[:, j * P:(j + 1) * P], ident[:, :])
                    ins.then_inc(tp_ready.sem, 1)

                for t in range(NT):
                    transpose_tile(0, t, xnb1[t % 2])

                def columns(h, b, ahi, alo, nk=KT, k0=0):
                    pe.wait_ge(wlo_ready.sem, wlo_ready.at(layer, 2 * h + (b + 1)))
                    pe.wait_ge(acc_taken[b].sem, acc_taken[b].at(layer, h))
                    for a, pieces in ((0, ((0, 512), (512, T))), (1, ((0, 384), (384, T)))):
                        for kk in range(nk):
                            for n, (w, xx) in enumerate(((whi, ahi), (whi, alo), (wlo, ahi))):
                                for lo, hi in pieces:
                                    ins = pe.matmul(acc[b][:, a * T + lo:a * T + hi], w[b][:, kk, a * P:(a + 1) * P],
                                                    xx[:, k0 + kk, lo:hi], start=(kk == 0 and n == 0),
                                                    stop=(kk == nk - 1 and n == 2))
                    ins.then_inc(unit_done.sem, 1)

                def rows(h, b, ahi, alo):
                    pe.wait_ge(wlo_ready.sem, wlo_ready.at(layer, 2 * h + (b + 1)))
                    pe.wait_ge(acc_taken[b].sem, acc_taken[b].at(layer, h))
                    for t in range(NT):
                        for kk in range(KT):
                            for n, (w, xx) in enumerate(((whi, ahi), (wlo, ahi), (whi, alo))):
                                ins = pe.matmul(acc[b][:, t * UW:(t + 1) * UW], xx[:, kk, t * P:(t + 1) * P], w[b][:, kk, :],
                                                start=(kk == 0 and n == 0), stop=(kk == KT - 1 and n == 2))
                    ins.then_inc(unit_done.sem, 1)

                pe.wait_ge(lo_ready.sem, lo_ready.at(layer, NT))
                pe.sem_inc(waits_passed, 1)
                with pe.Fori(0, 3) as i:
                    for b in range(2):
                        rows(i, b, hThi, hTlo)
                with pe.Fori(0, 3) as i:
                    for b in range(2):
                        columns(U_CONV // 2 + i, b, hThi, hTlo)
                pe.wait_ge(z_ready.sem, z_ready.at(layer, 2))
                pe.sem_inc(waits_passed, 1)
                with pe.Fori(0, 4) as i:
                    columns(U_GATE // 2 + i, 0, hThi, hTlo)
                    columns(U_GATE // 2 + i, 1, zhi, zlo, KT // 2)
                with pe.Fori(0, 2) as i:
                    for b in range(2):
                        columns(U_GT // 2 + i, b, hThi, hTlo)

                for kt in range(6):
                    pe.wait_ge(ksplit.sem, ksplit.at(layer, kt + 1))
                    if kt >= 2:
                        pe.wait_ge(kst_ready.sem, kst_ready.at(layer, kt - 1))
                    for s in range(2):
                        for g in range(KV):
                            o = (s * KV + g) * P
                            ins = pe.transpose(tp[kt % 2][:, o:o + P], ksp[:, s, g].rearrange("p a d -> p (a d)"), ident[:, :])
                    ins.then_inc(ktp_ready.sem, 1)
                pe.wait_ge(kst_ready.sem, kst_ready.at(layer, 6))
                pe.sem_inc(waits_passed, 1)

                def attend(t, nk, key0):
                    base = t * H
                    n = nk * P
                    pe.wait_ge(qsplit.sem, qsplit.at(layer, t + 1))
                    pe.wait_ge(oT_ready.sem, oT_ready.at(layer, t))

                    def queries(g):
                        pe.wait_ge(qs_ready.sem, qs_ready.at(layer, t * 4 + g))
                        for h in range(4):
                            ins = pe.transpose(qtp[:, h * P:(h + 1) * P], qsp[:, 4 * g + h].rearrange("p a d -> p (a d)"),
                                               ident[:, :])
                        ins.then_inc(qt_ready.sem, 1)

                    queries(0)
                    for j in range(1, H + 4):
                        if j % 4 == 2 and j // 4 < 3:
                            queries(j // 4 + 1)
                        if j < H + 1:
                            i = j - 1
                            if i % 4 == 0:
                                pe.wait_ge(qs_ready.sem, qs_ready.at(layer, t * 4 + (i // 4 + 1)))
                            pe.wait_ge(p_ready.sem, p_ready.at(layer, base + (i - 1)))
                            for lo, hi in ((0, min(n, 512)), (512, n)):
                                if hi > lo:
                                    for s in range(2):
                                        ins = pe.matmul(scores[i % 2][:, lo:hi], qs[i // 4 % 2][:, i % 4, :],
                                                        kst[:, s, i // 4, key0 + lo:key0 + hi], start=(s == 0), stop=(s == 1))
                            ins.then_inc(s_ready.sem, 1)
                        if 3 <= j < H + 3:
                            i = j - 3
                            pe.wait_ge(p_ready.sem, p_ready.at(layer, base + (i + 1)))
                            pe.wait_ge(pts_ready.sem, pts_ready.at(layer, base + i))
                            for a in range(nk):
                                ins = pe.transpose(ptp[:, a * P:(a + 1) * P], prob[i % 2][:, a * P:(a + 1) * P], ident[:, :])
                            ins.then_inc(pt_ready.sem, 1)
                        if 4 <= j:
                            i = j - 4
                            pe.wait_ge(pts_ready.sem, pts_ready.at(layer, base + (i + 1)))
                            if i % 8 == 0:
                                pe.wait_ge(o_ready.sem, o_ready.at(layer, t * 2 + i // 8))
                            for a in range(nk):
                                g = i // 4
                                kt = key0 // P + a
                                vv = cv[:, g * HD:(g + 1) * HD] if kt == 0 else v[:, kt - 1, g * HD:(g + 1) * HD]
                                ins = pe.matmul(pso[:, i % 8 * HD:(i % 8 + 1) * HD], probT[i % 2][:, a, :], vv,
                                                start=(a == 0), stop=(a == nk - 1))
                            ins.then_inc(pv_done.sem, 1)
                    pe.wait_ge(o_ready.sem, o_ready.at(layer, t * 2 + 2))
                    for j in range(KT):
                        ins = pe.transpose(ps[:, j * P:(j + 1) * P], ot[:, j * P:(j + 1) * P], ident[:, :])
                    ins.then_inc(otp_ready.sem, 1)

                with pe.Fori(0, LT) as t:
                    attend(t, 5, 0)
                attend(LT, 1, PAST + LAT)

                pe.wait_ge(oT_ready.sem, oT_ready.at(layer, NT))
                pe.sem_inc(waits_passed, 1)
                with pe.Fori(0, 2) as i:
                    for b in range(2):
                        columns(U_AO // 2 + i, b, oThi, oTlo)
                pe.wait_ge(m_ready.sem, m_ready.at(layer, 4))
                pe.sem_inc(waits_passed, 1)
                with pe.Fori(0, 2) as i:
                    for b in range(2):
                        rows(U_WO // 2 + i, b, mhi, mlo)

                for t in range(NT + 1):
                    if t < NT:
                        transpose_tile(1, t, xnb2[t % 2])
                    if t:
                        r = t - 1
                        pe.wait_ge(h32_ready.sem, h32_ready.at(layer, NT + r + 1))
                        if r == 0:
                            pe.wait_ge(lp_loaded.sem, lp_loaded.at(layer, 48))
                        for kk in range(KT):
                            ins = pe.matmul(bank(4)[:, r * E:(r + 1) * E], hb2[r % 2][:, kk, :], wr[:, kk, :],
                                            start=(kk == 0), stop=(kk == KT - 1))
                        ins.then_inc(logits_done.sem, 1)
                pe.wait_ge(aff_ready.sem, aff_ready.at(layer, 1))
                for t in range(NT):
                    ins = pe.transpose(ps[0:E, 2560 + t * P:2560 + (t + 1) * P], aff[:, t, :], ident[:, :])
                ins.then_inc(affT_ready.sem, 1)
                pe.wait_ge(slots_ready.sem, slots_ready.at(layer, 1))
                pe.sem_inc(waits_passed, 1)
                for t in range(NT):
                    ins = pe.transpose(bank(7)[:, t * E:(t + 1) * E], work[:, t * P:(t + 1) * P], ident[0:E, 0:E])
                ins.then_inc(slotsT_ready.sem, 1)

                pe.wait_ge(lo_ready.sem, lo_ready.at(layer, 2 * NT))
                pe.sem_inc(waits_passed, 1)
                with pe.Fori(0, E // 2) as p:
                    def side_use(n):
                        pe.wait_ge(side_taken[n % 2].sem, side_taken[n % 2].at(layer, p * 9 + n // 2))
                        return side[n % 2]

                    pe.wait_ge(S_ready.sem, S_ready.at(layer, p + 1))
                    for g in range(3):
                        out = side_use(g)
                        for dd in range(3 * g, min(3 * g + 3, KT)):
                            for t in range(NT):
                                for n, part in enumerate((xnhi, xnlo)):
                                    o = (dd - 3 * g) * 2 * SL
                                    ins = pe.matmul(out[:, o:o + 2 * SL], part[:, t, dd * P:(dd + 1) * P],
                                                    S[:, t].rearrange("p e c -> p (e c)"), start=(t == 0 and n == 0),
                                                    stop=(t == NT - 1 and n == 1))
                        ins.then_inc(side_ready.sem, 1)
                    for e in range(2):
                        for b in range(2):
                            out = side_use(3 + 2 * e + b)
                            for n, t in enumerate(range(LT) if b == 0 else (LT,)):
                                ins = pe.transpose(out[0:SL, n * P:(n + 1) * P], f32(S[:, t, e, :]), ident[:, :])
                            ins.then_inc(side_ready.sem, 1)
                    out = side_use(7)
                    for e in range(2):
                        for t in range(NT):
                            ins = pe.matmul(out[0:SL, e:e + 1], f32(S[:, t, e, :]), aff[:, t, ds(p * 2 + e, 1)],
                                            start=(t == 0), stop=(t == NT - 1))
                    ins.then_inc(side_ready.sem, 1)
                    pe.wait_ge(xlo_ready.sem, xlo_ready.at(layer, p * 3 + 3))
                    for m in range(PP):
                        e, r = m // EP, m % EP
                        w, b, kh = PIECES[r]
                        pe.wait_ge(ring_split_lo.sem, ring_split_lo.at(layer, p * PP + (m + 1)))
                        if kh == 0:
                            free = (hidlo_ready, hid_ready, ym_ready)[w]
                            pe.wait_ge(free.sem, free.at(layer, p * 4 + (2 * e + b - 1)))
                        if w == 2 and b == 0:
                            pe.wait_ge(hidlo_ready.sem, hidlo_ready.at(layer, p * 4 + (2 * e + kh + 1)))
                        out = (gate_ps, up_ps, down_ps)[w][b]
                        for kk in range(KH):
                            k8 = KH * kh + kk
                            ahi, alo = (xhi[:, k8, e, :], xlo[:, k8, e, :]) if w < 2 else (hidhi[:, k8, :], hidlo[:, k8, :])
                            for n, (a, ww) in enumerate(((ahi, ring_hi[m % HI]), (ahi, ring_lo[m % RING]), (alo, ring_hi[m % HI]))):
                                ins = pe.matmul(out, a, ww[:, kk, :], start=(k8 == 0 and n == 0), stop=(k8 == KT - 1 and n == 2))
                        ins.then_inc(ring_done.sem, 1)
                        if r in (5, 8):
                            b = int(r == 8)
                            pe.wait_ge(hid_ready.sem, hid_ready.at(layer, p * 4 + (2 * e + b + 1)))
                            for j in range(4):
                                ins = pe.transpose(hidT_ps[b][:, j * SL:(j + 1) * SL], hid[b][:, j * P:(j + 1) * P],
                                                   ident[0:SL, 0:SL])
                            ins.then_inc(hidT_ready.sem, 1)
                    pe.wait_ge(side_taken[0].sem, side_taken[0].at(layer, p * 9 + 4))
                    for b in range(2):
                        pe.wait_ge(ylo_ready.sem, ylo_ready.at(layer, p * 4 + (3 + b)))
                        for t in range(NT):
                            out = side_use(8 + NT * b + t)
                            for n, (e, part) in enumerate(((0, yhi), (0, ylo), (1, yhi), (1, ylo))):
                                ins = pe.matmul(out[:, :], ST[:, e, t * P:(t + 1) * P], part[:, e, 512 * b:512 * (b + 1)],
                                                start=(n == 0), stop=(n == 3))
                            ins.then_inc(side_ready.sem, 1)

        @block.vector
        def _(dve):
            ch = Chain(dve, DVE_STEPS)
            for signal, n in ((wlo_ready, 2), (acc_taken[0], 1), (acc_taken[1], 1), (pts_ready, 1), (o_ready, 1),
                              (oT_ready, 1), (hid_ready, 2), (hidlo_ready, 2), (ym_ready, 2), (side_taken[0], 1), (side_taken[1], 1)):
                dve.sem_inc(signal.sem, n)
            dve.wait_ge(setup_tp, 1)
            dve.tensor_copy(colsA[:, :], ps[:, 0:P])
            dve.tensor_copy(colsB[:, :], ps[:, P:P + 40]).then_inc(cols_ready, 1)
            dve.wait_ge(cols_ready, 1)
            dve.wait_ge(silu_c_ready, 1)
            dve.memset(slotT[:, :, E:E + 2], -1.0)
            dve.tensor_tensor(sum_halves[:, :], ident[0:4, 0:2], ident[0:4, 2:4], ALU.add)
            dve.tensor_tensor(sc4[:, :, 2:4], sc[:, :, :], f32(sc4[:, :, 0:2]), ALU.subtract).then_inc(silu_c_ready, 1)
            with dve.Fori(0, MOD_GROUPS) as i:
                for n in range(EP):
                    dve.wait_ge(ring_split_hi.sem, i * EP + (n + 1))
                    dve.tensor_tensor(ring_lo[n % RING][:, :, :], ring[n % RING][:, :, :], f32(ring_hi[n % HI][:, :, :]), ALU.subtract)\
                       .then_inc(ring_split_lo.sem, 1)
            dve.wait_ge(mod_cols_done, 2 + MOD_BLOCKS)
            dve.tensor_tensor(mod[:, :, :], ps[:, 1024:1216].rearrange("p (a b) -> p a b", b=2),
                              colsA[:, 0:96].unsqueeze(2).to_broadcast([P, 96, 2]), ALU.add).then_inc(mod_ready, 1)
            dve.wait_ge(mod_ready, 1)
            dve.wait_ge(x_loaded, 32)
            dve.sem_inc(x_ready.sem, 1)

            with ch.layers() as layer:
                dve.tensor_copy(modl[:, :, :], mod[:, ds(layer * 48, 48), :]).then_inc(dve_chain, 1)
                dve.wait_ge(dve_chain, ch.next())
                dve.sem_inc(modl_ready.sem, 1)
                for A, n0, c0 in ((A1, 96, 8), (A2, 112, 32)):
                    g = colsA[:, ds(layer * 8 + n0, 8)].unsqueeze(2).to_broadcast([P, KT, 2])
                    dve.scalar_tensor_tensor(out=A[:, :, :], in0=modl[:, c0:c0 + 8, :], scalar=1.0, in1=g,
                                                     op0=ALU.add, op1=ALU.mult).then_inc(dve_chain, 1)
                    dve.wait_ge(dve_chain, ch.next())
                B1, B2 = modl[:, 0:8, :], modl[:, 24:32, :]

                def scale(n, t, xnb):
                    if t >= 2:
                        dve.wait_ge(tp_ready.sem, tp_ready.at(layer, n * NT + t - 1))
                        dve.wait_ge(lo_ready.sem, lo_ready.at(layer, n * NT + t - 1))
                    dve.tensor_scalar(xnb[t % 2][:, :], x[:, t, :], ss[:, n, t:t + 1], None, ALU.mult)\
                       .then_inc(xn_ready.sem, 1)

                def modulate(n, t, hb, A, B):
                    s = 0 if t < LT else 1
                    dve.wait_ge(tp_ready.sem, tp_ready.at(layer, n * NT + t + 1))
                    if n == 1 and t >= 2:
                        dve.wait_ge(logits_done.sem, logits_done.at(layer, t - 1))
                    wide = [P, KT, P]
                    dve.tensor_tensor(hb[t % 2][:, :, :], tp[t % 2].rearrange("p (k n) -> p k n", k=KT),
                                              A[:, :, s:s + 1].to_broadcast(wide), ALU.mult).then_inc(dve_chain, 1)
                    dve.wait_ge(dve_chain, ch.next())
                    dve.tensor_tensor(hb[t % 2][:, :, :], hb[t % 2][:, :, :], B[:, :, s:s + 1].to_broadcast(wide), ALU.add)\
                       .then_inc(h32_ready.sem, 1)

                dve.wait_ge(rstd_ready.sem, rstd_ready.at(layer, 1))
                scale(0, 0, xnb1)
                scale(0, 1, xnb1)
                for t in range(NT):
                    modulate(0, t, hb1, A1, B1)
                    dve.wait_ge(hi_ready.sem, hi_ready.at(layer, t + 1))
                    sl = slice(t * P, (t + 1) * P)
                    dve.tensor_tensor(hTlo[:, :, sl], hb1[t % 2][:, :, :], f32(hThi[:, :, sl]), ALU.subtract)\
                       .then_inc(lo_ready.sem, 1)
                    if t + 2 < NT:
                        scale(0, t + 2, xnb1)

                def split(h, b, nk=KT):
                    dve.wait_ge(whi_ready.sem, whi_ready.at(layer, 2 * h + (b + 1)))
                    dve.tensor_tensor(wlo[b][:, 0:nk, :], raw[b][:, 0:nk, :], f32(whi[b][:, 0:nk, :]), ALU.subtract)\
                       .then_inc(wlo_ready.sem, 1)

                def result(h, b):
                    dve.wait_ge(unit_done.sem, unit_done.at(layer, 2 * h + (b + 1)))
                    return acc[b]

                with dve.Fori(0, 3) as i:
                    for b in range(2):
                        split(i, b)

                def head_squares(src, nh, dst):
                    dve.tensor_tensor(t1[:, 0:nh * HD], src, src, ALU.mult).then_inc(dve_chain, 1)
                    dve.wait_ge(dve_chain, ch.next())
                    dve.tensor_reduce(dst, t1[:, 0:nh * HD].rearrange("p (h d) -> p h d", h=nh), AX.X, ALU.add).then_inc(dve_chain, 1)
                    dve.wait_ge(dve_chain, ch.next())

                def head_norm(src, t, nh, r, g, tc, tn, last=False):
                    v3 = src.rearrange("p (h d) -> p h d", h=nh)
                    wide = [P, nh, HD]
                    dve.tensor_tensor(v3, v3, r.unsqueeze(2).to_broadcast(wide), ALU.mult).then_inc(dve_chain, 1)
                    dve.wait_ge(dve_chain, ch.next())
                    if t == LT:
                        dve.tensor_tensor(v3, v3, g[:, :].unsqueeze(1).to_broadcast(wide), ALU.mult).then_inc(dve_chain, 1)
                        dve.wait_ge(dve_chain, ch.next())
                        return
                    a, bb = t1[:, 0:nh * HD], t2[:, 0:nh * HD]
                    dve.tensor_tensor(a.rearrange("p (h d) -> p h d", h=nh), v3, tc[:, t, :].unsqueeze(1).to_broadcast(wide),
                                      ALU.mult)
                    sv = src.rearrange("p (h s d) -> p h s d", h=2 * nh, s=2)
                    bv = bb.rearrange("p (h s d) -> p h s d", h=2 * nh, s=2)
                    tb = tn[:, t, :].rearrange("p (a s d) -> p a s d", a=2, s=2)
                    for s in range(2):
                        o = bv[:, :, s, :].rearrange("p (h a) d -> p h a d", a=2)
                        i0 = sv[:, :, 1 - s, :].rearrange("p (h a) d -> p h a d", a=2)
                        ins = dve.tensor_tensor(o, i0, tb[:, :, s, :].unsqueeze(1).to_broadcast([P, nh, 2, HALF]), ALU.mult)
                    ins.then_inc(dve_chain, 1)
                    dve.wait_ge(dve_chain, ch.next())
                    dve.tensor_tensor(src, a, bb, ALU.add).then_inc(dve_chain, 1)
                    dve.wait_ge(dve_chain, ch.next())

                def prepare(step):
                    if step == 0:
                        dve.wait_ge(acc_taken[0].sem, acc_taken[0].at(layer, 3))
                        dve.wait_ge(acc_taken[1].sem, acc_taken[1].at(layer, 3))
                        for t in range(NT):
                            head_squares(q[:, t, :], H, rq[:, t, :])
                    if step == 1:
                        for t in range(NT):
                            head_squares(k[:, t, :], KV, rk[:, t, :])
                        dve.sem_inc(ssq_ready.sem, 1)
                        dve.wait_ge(lp_loaded.sem, lp_loaded.at(layer, 48))
                        dve.tensor_scalar(gq[:, :], gq[:, :], HD ** -0.5, None, ALU.mult).then_inc(dve_chain, 1)
                        dve.wait_ge(dve_chain, ch.next())
                        for g, tc, tn in ((gq, qC, qS), (gk, kC, kS)):
                            dve.tensor_tensor(tc[:, :, :], cosT[:, :, :], g[:, :].unsqueeze(1).to_broadcast([P, LT, HD]), ALU.mult)
                            gv = g[:, :].rearrange("p (a s d) -> p a s d", a=2, s=2)
                            for t in range(LT):
                                sv = sinT[:, t, :].rearrange("p (a s d) -> p a s d", a=2, s=2)
                                tv = tn[:, t, :].rearrange("p (a s d) -> p a s d", a=2, s=2)
                                for s in range(2):
                                    ins = dve.tensor_tensor(tv[:, :, s, :], sv[:, :, s, :], gv[:, :, 1 - s, :], ALU.mult)
                            ins.then_inc(dve_chain, 1)
                            dve.wait_ge(dve_chain, ch.next())
                    if step == 2:
                        dve.wait_ge(rqk_ready.sem, rqk_ready.at(layer, 1))
                        for t in range(2):
                            head_norm(q[:, t, :], t, H, rq[:, t, :], gq, qC, qS)
                    if step == 3:
                        for t in range(2, 4):
                            head_norm(q[:, t, :], t, H, rq[:, t, :], gq, qC, qS)
                    if step == 4:
                        head_norm(q[:, LT, :], LT, H, rq[:, LT, :], gq, qC, qS)
                    if step == 5:
                        for t in range(NT):
                            head_norm(k[:, t, :], t, KV, rk[:, t, :], gk, kC, kS)
                        dve.sem_inc(qk_ready.sem, 1)

                for hf in range(2):
                    u = U_CONV + 3 * hf
                    split(u // 2, u % 2)
                    if hf == 0:
                        prepare(0)
                    else:
                        prepare(3)
                    split((u + 1) // 2, (u + 1) % 2)
                    if hf == 0:
                        prepare(1)
                    else:
                        prepare(4)
                    for col in (0, LAT + 1, T + 2):
                        dve.memset(ub[:, :, col:col + 1], 0.0)
                    dve.wait_ge(acc_taken[u % 2].sem, acc_taken[u % 2].at(layer, u // 2 + 1))
                    r = result((u + 1) // 2, (u + 1) % 2).rearrange("p (a n) -> p a n", a=2)
                    dve.tensor_tensor(ub[:, :, 1:LAT + 1], r[:, :, 0:LAT], gcs[:, :, 0:LAT], ALU.mult)
                    ins = dve.tensor_tensor(ub[:, :, LAT + 2:T + 2], r[:, :, LAT:T], gcs[:, :, LAT:T], ALU.mult)
                    ins.then_inc(acc_taken[(u + 1) % 2].sem, 1)
                    dve.wait_ge(acc_taken[(u + 1) % 2].sem, acc_taken[(u + 1) % 2].at(layer, (u + 1) // 2 + 1))
                    for tap, off in ((1, 1), (0, 0), (2, 2)):
                        for a in range(2):
                            w = colsB[:, ds(layer * 12 + (16 + 4 * tap + 2 * hf + a), 1)]
                            src, dst = ub[:, a, off:off + T + 1], cb[:, a, 1:T + 2]
                            if tap == 1:
                                ins = dve.tensor_scalar(dst, src, w, None, ALU.mult)
                            else:
                                ins = dve.scalar_tensor_tensor(out=dst, in0=src, scalar=w, in1=dst, op0=ALU.mult, op1=ALU.add)
                        ins.then_inc(dve_chain, 1)
                        dve.wait_ge(dve_chain, ch.next())
                    split((u + 2) // 2, (u + 2) % 2)
                    if hf == 0:
                        prepare(2)
                    else:
                        prepare(5)
                    r = result((u + 2) // 2, u % 2).rearrange("p (a n) -> p a n", a=2)
                    dve.tensor_tensor(gcs[:, :, 0:LAT], r[:, :, 0:LAT], cb[:, :, 1:LAT + 1], ALU.mult)
                    ins = dve.tensor_tensor(gcs[:, :, LAT:T], r[:, :, LAT:T], cb[:, :, LAT + 2:T + 2], ALU.mult)
                    ins.then_inc(acc_taken[u % 2].sem, 1)
                    dve.wait_ge(zhi_ready.sem, zhi_ready.at(layer, hf + 1))
                    dve.tensor_tensor(zlo[:, 2 * hf:2 * hf + 2, :], gcs[:, :, :], f32(zhi[:, 2 * hf:2 * hf + 2, :]), ALU.subtract)\
                       .then_inc(z_ready.sem, 1)
                with dve.Fori(0, 4) as i:
                    split(U_GATE // 2 + i, 0)
                    split(U_GATE // 2 + i, 1, KT // 2)
                    dve.wait_ge(acc_taken[0].sem, acc_taken[0].at(layer, U_GATE // 2 + 1 + i))
                    dve.tensor_tensor(mixed[:, ds(i * 2, 2), :].rearrange("p a n -> p (a n)"), result(U_GATE // 2 + i, 1), tw[:, :],
                                      ALU.mult).then_inc(acc_taken[1].sem, 1)
                with dve.Fori(0, 2) as i:
                    for b in range(2):
                        split(U_GT // 2 + i, b)
                dve.wait_ge(cache_loaded.sem, cache_loaded.at(layer, 32))
                dve.sem_inc(waits_passed, 1)
                for kt in range(6):
                    dve.wait_ge(khi_ready.sem, khi_ready.at(layer, kt + 1))
                    src = (ck[:, :] if kt == 0 else k[:, kt - 1, :]).rearrange("p (v d) -> p v d", v=KV)
                    for a in range(2):
                        ins = dve.tensor_tensor(ksp[:, 1, :, a, :], src, ksp[:, 0, :, a, :], ALU.subtract)
                    ins.then_inc(ksplit.sem, 1)

                def attend(t, nk):
                    base = t * H
                    dve.wait_ge(qhi_ready.sem, qhi_ready.at(layer, t + 1))
                    dve.tensor_tensor(qsp[:, :, 1, :], q[:, ds(t, 1), :].rearrange("p o (h d) -> p (o h) d", h=H),
                                      qsp[:, :, 0, :], ALU.subtract).then_inc(qsplit.sem, 1)

                    def normalise(half):
                        hs = slice(8 * half, 8 * half + 8)
                        dve.wait_ge(p_ready.sem, p_ready.at(layer, base + (8 * half + 8)))
                        dve.reciprocal(rinv[:, hs], rsum[:, hs]).then_inc(dve_chain, 1)
                        dve.wait_ge(dve_chain, ch.next())
                        dve.wait_ge(pv_done.sem, pv_done.at(layer, base + (8 * half + 8)))
                        if half == 0:
                            dve.wait_ge(otp_ready.sem, otp_ready.at(layer, t))
                        dve.tensor_tensor(ot[:, 512 * half:512 * (half + 1)].rearrange("p (h d) -> p h d", h=8),
                                          pso.rearrange("p (h d) -> p h d", h=8),
                                          rinv[:, hs].unsqueeze(2).to_broadcast([P, 8, HD]), ALU.mult).then_inc(o_ready.sem, 1)

                    for j in range(H + 2):
                        if j < H:
                            dve.wait_ge(s_ready.sem, s_ready.at(layer, base + (j + 1)))
                            dve.wait_ge(p_ready.sem, p_ready.at(layer, base + (j - 1)))
                            dve.tensor_reduce(nmax[:, j % 2:j % 2 + 1], scores[j % 2][:, 0:nk * P], AX.X, ALU.max, negate=True)\
                               .then_inc(nmax_ready.sem, 1)
                        if j == 11:
                            normalise(0)
                        if j >= 2:
                            i = j - 2
                            dve.wait_ge(pt_ready.sem, pt_ready.at(layer, base + (i + 1)))
                            dve.wait_ge(pv_done.sem, pv_done.at(layer, base + (i - 1)))
                            dve.tensor_copy(probT[i % 2][:, 0:nk, :].rearrange("p a n -> p (a n)"), ptp[:, 0:nk * P])\
                               .then_inc(pts_ready.sem, 1)
                    normalise(1)
                    dve.wait_ge(ohi_ready.sem, ohi_ready.at(layer, t + 1))
                    dve.tensor_tensor(oTlo[:, :, ds(t * P, P)], bank(0, 2).rearrange("p (k n) -> p k n", k=KT),
                                      f32(oThi[:, :, ds(t * P, P)]), ALU.subtract).then_inc(oT_ready.sem, 1)

                with ch.loop(LT, 2) as t:
                    attend(t, 5)
                attend(LT, 1)
                split(U_AO // 2, 0)
                for j in range(4):
                    h, b = (U_AO + j) // 2, j % 2
                    split((U_AO + j + 1) // 2, (j + 1) % 2)
                    if j:
                        dve.wait_ge(m_ready.sem, m_ready.at(layer, j))
                    g2 = G[:, 2 * j:2 * j + 2, :].rearrange("p a n -> p (a n)")
                    ins = dve.tensor_tensor(tw[:, :], result(h, b), g2, ALU.mult)
                    ins.then_inc(acc_taken[b].sem, 1)
                    dve.wait_ge(acc_taken[b].sem, acc_taken[b].at(layer, h + 1))
                    dve.tensor_tensor(tw[:, :], tw[:, :], mixed[:, 2 * j:2 * j + 2, :].rearrange("p a n -> p (a n)"), ALU.add)\
                       .then_inc(mrg_ready.sem, 1)
                    dve.wait_ge(mhi_ready.sem, mhi_ready.at(layer, j + 1))
                    dve.tensor_tensor(mlo[:, 2 * j:2 * j + 2, :].rearrange("p a n -> p (a n)"), tw[:, :],
                                      f32(mhi[:, 2 * j:2 * j + 2, :].rearrange("p a n -> p (a n)")), ALU.subtract)\
                       .then_inc(m_ready.sem, 1)
                dve.wait_ge(rows_taken.sem, rows_taken.at(layer, 2))
                t3 = tw[:, :].rearrange("p (t n) -> p t n", t=NT)
                for j in range(4):
                    h, b = (U_WO + j) // 2, j % 2
                    cols = slice(j * UW, (j + 1) * UW)
                    if j < 3:
                        split((U_WO + j + 1) // 2, (j + 1) % 2)
                    a3 = result(h, b).rearrange("p (t n) -> p t n", t=NT)
                    dve.tensor_tensor(t3[:, 0:LT, :], a3[:, 0:LT, :], gbc[:, 0, cols].unsqueeze(1).to_broadcast([P, LT, UW]), ALU.mult)
                    ins = dve.tensor_tensor(t3[:, LT, :], a3[:, LT, :], gbc[:, 1, cols], ALU.mult)
                    ins.then_inc(acc_taken[b].sem, 1)
                    dve.wait_ge(acc_taken[b].sem, acc_taken[b].at(layer, h + 1))
                    ins = dve.tensor_tensor(x[:, :, cols], x[:, :, cols], t3, ALU.add)
                    if j < 3:
                        ins.then_inc(dve_chain, 1)
                        dve.wait_ge(dve_chain, ch.next())
                    else:
                        ins.then_inc(x_ready.sem, 1)
                dve.wait_ge(rstd_ready.sem, rstd_ready.at(layer, 2))
                scale(1, 0, xnb2)
                scale(1, 1, xnb2)
                for t in range(NT):
                    modulate(1, t, hb2, A2, B2)
                    dve.wait_ge(hi_ready.sem, hi_ready.at(layer, NT + t + 1))
                    dve.tensor_tensor(xnlo[:, t, :], xnb2[t % 2][:, :], f32(xnhi[:, t, :]), ALU.subtract)\
                       .then_inc(lo_ready.sem, 1)
                    if t + 2 < NT:
                        scale(1, t + 2, xnb2)
                dve.wait_ge(logits_done.sem, logits_done.at(layer, NT))
                lps = bank(4)[:, 0:NT * E].rearrange("p (t e) -> p t e", t=NT)
                wide = [P, NT, E]
                dve.tensor_reduce(lgm[:, :], lps, AX.X, ALU.max).then_inc(dve_chain, 1)
                dve.wait_ge(dve_chain, ch.next())
                dve.tensor_tensor(lg[:, :, :], lps, lgm[:, :].unsqueeze(2).to_broadcast(wide), ALU.subtract)\
                   .then_inc(lgsub_ready.sem, 1)
                dve.wait_ge(lgexp_ready.sem, lgexp_ready.at(layer, 1))
                dve.tensor_reduce(lsum[:, :], lg[:, :, :], AX.X, ALU.add).then_inc(dve_chain, 1)
                dve.wait_ge(dve_chain, ch.next())
                dve.reciprocal(lsum[:, :], lsum[:, :]).then_inc(dve_chain, 1)
                dve.wait_ge(dve_chain, ch.next())
                dve.tensor_tensor(aff[:, :, :], lg[:, :, :], lsum[:, :].unsqueeze(2).to_broadcast(wide), ALU.mult)\
                   .then_inc(aff_ready.sem, 1)
                dve.wait_ge(affT_ready.sem, affT_ready.at(layer, 1))
                dve.tensor_copy(work[:, :], ps[0:E, 2560:2560 + T]).then_inc(dve_chain, 1)
                dve.wait_ge(dve_chain, ch.next())
                dve.sem_inc(waits_passed, 1)
                for lo, hi, cap in ((0, LAT, CAP_L), (LAT, T, CAP_C)):
                    for _ in range(cap // 8):
                        dve.max(top8[:, :], work[:, lo:hi]).then_inc(dve_chain, 1)
                        dve.wait_ge(dve_chain, ch.next())
                        dve.sem_inc(waits_passed, 1)
                        dve.match_replace(out=work[:, lo:hi], in_to_replace=top8[:, :],
                                                        in_values=work[:, lo:hi], imm_value=-1.0).then_inc(dve_chain, 1)
                        dve.wait_ge(dve_chain, ch.next())
                        dve.sem_inc(waits_passed, 1)
                dve.tensor_scalar(affT[:, :], work[:, :], 0.0, None, ALU.is_lt).then_inc(dve_chain, 1)
                dve.wait_ge(dve_chain, ch.next())
                for lo, hi, off in ((0, LAT, 0.0), (LAT, T, float(CAP_L))):
                    dve.tensor_tensor_scan(cum[:, lo:hi], affT[:, lo:hi], affT[:, lo:hi], 0.0, ALU.add, ALU.max).then_inc(dve_chain, 1)
                    dve.wait_ge(dve_chain, ch.next())
                    dve.scalar_tensor_tensor(out=work[:, lo:hi], in0=cum[:, lo:hi], scalar=off, in1=affT[:, lo:hi],
                                                     op0=ALU.add, op1=ALU.mult).then_inc(dve_chain, 1)
                    dve.wait_ge(dve_chain, ch.next())
                dve.tensor_scalar(work[:, :], work[:, :], -1.0, None, ALU.add).then_inc(slots_ready.sem, 1)
                dve.wait_ge(slotsT_ready.sem, slotsT_ready.at(layer, 1))
                dve.tensor_copy(slotT[:, :, 0:E], bank(7)[:, 0:NT * E].rearrange("p (t e) -> p t e", t=NT)).then_inc(dve_chain, 1)
                dve.wait_ge(dve_chain, ch.next())
                dve.sem_inc(waits_passed, 1)

                def selection(pair):
                    for t in range(NT):
                        ins = dve.tensor_tensor(S[:, t], slotT[:, t, ds(pair * 2, 2)].unsqueeze(2).to_broadcast([P, 2, SL]),
                                                slot_ids[:, :].unsqueeze(1).to_broadcast([P, 2, SL]), ALU.is_equal)
                    ins.then_inc(S_ready.sem, 1)

                selection(0)
                with ch.loop(E // 2, PAIR_STEPS) as p:
                    def side_result(n):
                        dve.wait_ge(side_ready.sem, side_ready.at(layer, p * 18 + (n + 1)))
                        return side[n % 2]

                    def tokens(g):
                        src = side_result(g)
                        for dd in range(3 * g, min(3 * g + 3, KT)):
                            sv = src[:, (dd - 3 * g) * 2 * SL:(dd - 3 * g + 1) * 2 * SL].rearrange("p (e c) -> p e c", e=2)
                            for s, cs in ((0, slice(0, CAP_L)), (1, slice(CAP_L, SL))):
                                ins = dve.tensor_scalar(xsel[:, dd, :, cs], sv[:, :, cs], A2[:, dd, s:s + 1], B2[:, dd, s:s + 1],
                                                        ALU.mult, ALU.add)
                        ins.then_inc(side_taken[g % 2].sem, 1)

                    for m in range(PP + 5):
                        for e, r in ((1, m - EP), (0, m)):
                            if r in (7, 11):
                                b = int(r == 11)
                                dve.wait_ge(silu_ready.sem, silu_ready.at(layer, p * 4 + (2 * e + b + 1)))
                                dve.wait_ge(ring_done.sem, ring_done.at(layer, p * PP + (EP * e + 4 * b + 4)))
                                dve.tensor_tensor(hid[b][:, :], hid[b][:, :], up_ps[b], ALU.mult).then_inc(hid_ready.sem, 1)
                            if r in (9, 12):
                                b = int(r == 12)
                                dve.wait_ge(hidhi_ready.sem, hidhi_ready.at(layer, p * 4 + (2 * e + b + 1)))
                                hh = slice(4 * b, 4 * b + 4)
                                dve.tensor_tensor(hidlo[:, hh, :].rearrange("p a n -> p (a n)"), hidT_ps[b],
                                                  f32(hidhi[:, hh, :].rearrange("p a n -> p (a n)")), ALU.subtract)\
                                   .then_inc(hidlo_ready.sem, 1)
                            if r in (14, 15):
                                b = r - 14
                                cols = slice(512 * b, 512 * (b + 1))
                                dve.wait_ge(ring_done.sem, ring_done.at(layer, p * PP + (EP * e + 11 + b)))
                                dve.scalar_tensor_tensor(out=ym[:, e, cols], in0=down_ps[b], scalar=vals[:, e:e + 1],
                                                         in1=g2mix[0:SL, cols], op0=ALU.mult, op1=ALU.mult).then_inc(ym_ready.sem, 1)
                            if r in (15, 16):
                                b = r - 15
                                cols = slice(512 * b, 512 * (b + 1))
                                dve.wait_ge(yhi_ready.sem, yhi_ready.at(layer, p * 4 + (2 * e + b + 1)))
                                dve.tensor_tensor(ylo[:, e, cols], ym[:, e, cols], f32(yhi[:, e, cols]), ALU.subtract)\
                                   .then_inc(ylo_ready.sem, 1)
                        if m < PP:
                            dve.wait_ge(ring_split_hi.sem, ring_split_hi.at(layer, p * PP + (m + 1)))
                            dve.tensor_tensor(ring_lo[m % RING][:, :, :], ring[m % RING][:, :, :], f32(ring_hi[m % HI][:, :, :]),
                                              ALU.subtract).then_inc(ring_split_lo.sem, 1)
                        if m < 3:
                            tokens(m)
                        if m == 2:
                            for g in range(3):
                                dve.wait_ge(xhi_ready.sem, xhi_ready.at(layer, p * 3 + (g + 1)))
                                kk = slice(3 * g, min(3 * g + 3, KT))
                                dve.tensor_tensor(xlo[:, kk], xsel[:, kk], f32(xhi[:, kk]), ALU.subtract).then_inc(xlo_ready.sem, 1)
                        if m == 3:
                            dve.tensor_copy(vals[:, :], side_result(7)[0:SL, 0:2]).then_inc(side_taken[1].sem, 1)
                            selection(p + 1)
                    for n in range(2 * NT):
                        b, t = n // NT, n % NT
                        src = side_result(8 + n)
                        xv = x[:, t, 512 * b:512 * (b + 1)]
                        dve.tensor_tensor(xv, xv, src, ALU.add).then_inc(side_taken[n % 2].sem, 1)
                dve.wait_ge(side_taken[1].sem, side_taken[1].at(layer, 9 * E // 2))
                dve.sem_inc(x_ready.sem, 1)
            dve.wait_ge(fn_loaded, 16)
            dve.wait_ge(rstd_ready.sem, rstd_ready.at(DEPTH, 1))
            for t in range(NT):
                dve.scalar_tensor_tensor(out=x[:, t, :], in0=x[:, t, :], scalar=ss[:, 0, t:t + 1], in1=gbc[:, 0, :],
                                         op0=ALU.mult, op1=ALU.mult).then_inc(xn_ready.sem, 1)


DVE_STEPS = 113
PAIR_STEPS = 0

_INS = ["x_prompt", "x_sample", "cache_k", "cache_v", "c", "c_ctx", "w_mod", "b_mod", "norm1", "norm2", "w_in", "q_norm",
        "k_norm", "conv_w", "w_conv_out", "w_attn_out", "w_o", "w_router", "w_gate", "w_up", "w_down", "final_norm"]
_OUTS = [((1, CTX, D), "float32"), ((1, LAT, D), "float32"), ((1, DEPTH, CTX, KV, HD), "float32"),
         ((1, DEPTH, CTX, KV, HD), "float32")]


def constants():
    pos = np.arange(LAT)
    inv = (10000.0 ** (-np.arange(HALF, dtype=np.float32) / HALF)).astype(np.float32)
    cos, sin = np.zeros((LAT, 2, 2, HALF), np.float32), np.zeros((LAT, 2, 2, HALF), np.float32)
    for a, p in enumerate((pos // GRID_W, pos % GRID_W)):
        ang = p.astype(np.float32)[:, None] * inv[None, :]
        cos[:, a, :, :] = np.cos(ang)[:, None, :]
        sin[:, a, 0, :] = -np.sin(ang)
        sin[:, a, 1, :] = np.sin(ang)
    slots = np.broadcast_to(np.arange(SL, dtype=np.float32), (P, SL)).copy()
    return {"ident": np.eye(P, dtype=np.float32), "slots": slots, "cos": cos.reshape(LAT, HD), "sin": sin.reshape(LAT, HD)}


def kernel(**inputs):
    import concourse.bacc as _bacc
    from concourse import mybir as _mybir
    from concourse.bass_utils import run_bass_kernel_spmd as _run

    nc = _bacc.Bacc("TRN2", target_bir_lowering=False, num_devices=1)
    arrays, args = {}, []
    for name, a in [(n, np.ascontiguousarray(inputs[n])) for n in _INS] + list(constants().items()):
        arrays[f"in_{name}_dram"] = a
        args.append(nc.dram_tensor(f"in_{name}_dram", a.shape, _mybir.dt.from_np(a.dtype), kind="ExternalInput").ap())
    for i, (shape, dtype) in enumerate(_OUTS):
        args.append(nc.dram_tensor(f"out_{i}_dram", shape, _mybir.dt.from_np(np.dtype(dtype)), kind="ExternalOutput").ap())
    build(nc, *args)
    r = _run(nc, [arrays], core_ids=[0])
    return tuple(r.results[0][f"out_{i}_dram"] for i in range(len(_OUTS)))
```

```python
from contextlib import ExitStack, contextmanager

import numpy as np
import concourse.bass as bass
from concourse import mybir

F32 = mybir.dt.float32
F32R = mybir.dt.float32r
ALU = mybir.AluOpType
ACT = mybir.ActivationFunctionType
AX = mybir.AxisListType
ds = bass.ds

P = 128
D = 1024
KT = D // P
DEPTH = 2
LAT, CTX = 512, 128
T = LAT + CTX
NT = T // P
LT = LAT // P
H, KV, HD = 16, 4, 64
GRID_W = 64
QW, KVW, CW = H * HD, KV * HD, D // 2
E = 16
DE = 1024
CAP_L = 2 * LAT // E
CAP_C = 2 * CTX // E
SL = CAP_L + CAP_C
PAST = 128
EPS = 1e-6
KEYS = PAST + LAT + CTX
AXD = HD // 2
HALF = AXD // 2

UW = 256
U5 = NT * UW
OQ, OK_, OV = 0, QW, QW + KVW
OGB = QW + 2 * KVW
OGC, OXI = OGB + CW, OGB + 2 * CW
OGA = OGB + 3 * CW
OGT = OGA + D
U_Q, U_K, U_V, U_CONV, U_GATE, U_GT, U_AO, U_WO = 0, 4, 5, 6, 12, 20, 24, 28
UNITS = 32
RING = 6
HI = 4
KH = KT // 2
MOD_BLOCKS = DEPTH * 12
MOD_GROUPS = 2
MP = 2 * MOD_BLOCKS // MOD_GROUPS
EP = 12
PP = 2 * EP
EU = EP * E
POOL_LO = (3, 8, 13, 18)
DVE_LO = [m for m in range(PP) if m not in POOL_LO]
TURNED = ((9, 12), (9, 11))
SIDES = 22
PIECES = [(w, b, kh) for b in range(2) for w in range(2) for kh in range(2)] + [(2, b, kh) for kh in range(2) for b in range(2)]
ITEMS = NT * H


class Signal:

    def __init__(self, sem, per_layer, before=0):
        self.sem, self.per_layer, self.before = sem, per_layer, before

    def at(self, layer, n):
        return layer * self.per_layer + (self.before + n)


class Chain:

    def __init__(self, eng, per_layer):
        self.eng, self.per_layer, self.n, self.base = eng, per_layer, 0, 0

    def next(self):
        self.n += 1
        return self.base + self.n

    @contextmanager
    def loop(self, count, body):
        first, base = self.n, self.base
        with self.eng.Fori(0, count) as i:
            self.base = base + i * body
            yield i
        assert self.n - first == body, f"loop body: {self.n - first} steps"
        self.n, self.base = first + count * body, base

    @contextmanager
    def layers(self):
        first = self.n
        with self.eng.Fori(0, DEPTH) as layer:
            self.base = layer * self.per_layer
            yield layer
        assert self.n - first == self.per_layer, f"layer: {self.n - first} steps"
        self.n, self.base = first + DEPTH * self.per_layer, 0


def build(nc, x_prompt, x_sample, cache_k, cache_v, c, c_ctx, w_mod, b_mod, norm1, norm2, w_in, q_norm,
          k_norm, conv_w, w_conv_out, w_attn_out, w_o, w_router, w_gate, w_up, w_down, final_norm,
          ident_c, slots_c, cos_c, sin_c, y_prompt, y_sample, new_k, new_v):
    ctx = ExitStack()
    with ctx:
        KB = 1024
        B0 = 16640

        def at(name, shape, dt, off):
            return nc.alloc_sbuf_tensor_at(name, shape, dt, offset=B0 + off)

        x = at("x", [P, NT, D], F32, 0)
        gbc = at("gate1_rows", [P, 2, D], F32, 20 * KB)
        g2mix = at("gate2_rows", [P, D], F32, 28 * KB)
        bump = [32 * KB]

        def small(name, shape, dt=F32):
            t = at(name, shape, dt, bump[0])
            n = 4
            for s in shape[1:]:
                n *= s
            bump[0] += (n + 31) // 32 * 32
            assert bump[0] <= 44 * KB, bump
            return t

        ident = small("ident", [P, P])
        slot_ids = small("slot_ids", [P, SL])
        cosT = small("cosT", [P, LT, HD])
        sinT = small("sinT", [P, LT, HD])
        qC = small("qC", [P, LT, HD])
        qS = small("qS", [P, LT, HD])
        kC = small("kC", [P, LT, HD])
        kS = small("kS", [P, LT, HD])
        gq = small("gq", [P, HD])
        gk = small("gk", [P, HD])
        wr = small("wr", [P, KT, E])
        mod = small("mod", [P, DEPTH * 48, 2])
        modl = small("modl", [P, 48, 2])
        A1 = small("A1", [P, KT, 2])
        A2 = small("A2", [P, KT, 2])
        colsA = small("colsA", [P, P])
        colsB = small("colsB", [P, 40])
        sc = small("silu_c", [P, KT, 2])
        sc4 = small("silu_c_halves", [P, KT, 4], F32R)
        sum_halves = small("sum_halves", [4, 2])
        ss = small("ss", [P, 2, 8])
        rq = small("rq", [P, NT, H])
        rk = small("rk", [P, NT, KV])
        nmax = small("nmax", [P, 2])
        rsum = small("rsum", [P, H])
        rinv = small("rinv", [P, H])
        lgm = small("lgm", [P, NT])
        lg = small("lg", [P, NT, E])
        aff = small("aff", [P, NT, E])
        lsum = small("lsum", [P, NT])
        slotT = small("slotT", [P, NT, E + 2])
        top8 = small("top8", [E, 8])
        vals = small("vals", [SL, 4])
        minus_half = small("minus_half", [P, 1])

        ring = [at(f"ring{s}", [P, KH, 512], F32, (44 + 8 * s) * KB) for s in range(RING)]
        ring_lo = [at(f"ring_lo{s}", [P, KH, 512], F32R, (44 + 8 * s) * KB) for s in range(RING)]
        ring_hi = [at(f"ring_hi{s}", [P, KH, 512], F32R, (92 + 8 * s) * KB) for s in range(HI)]
        mod_rows = [at(f"mod_rows{s}", [4, 512], F32, (124 + 2 * s) * KB) for s in range(2)]
        raw = [at(f"raw{s}", [P, KT, UW], F32, (44 + 8 * s) * KB) for s in range(2)]
        raw_ao = [at(f"raw_ao{s}", [P, KT, UW], F32, (132 + 8 * s) * KB) for s in range(2)]
        whi = [at(f"whi{s}", [P, KT, UW], F32R, (60 + 8 * s) * KB) for s in range(2)]
        wlo = [at(f"wlo{s}", [P, KT, UW], F32R, (76 + 8 * s) * KB) for s in range(2)]
        hThi = at("hThi", [P, KT, T], F32R, 167 * KB)
        hTlo = at("hTlo", [P, KT, T], F32R, 187 * KB)
        oThi = at("oThi", [P, KT, T], F32R, 167 * KB)
        oTlo = at("oTlo", [P, KT, T], F32R, 187 * KB)
        xnhi = at("xnhi", [P, NT, D], F32R, 167 * KB)
        xnlo = at("xnlo", [P, NT, D], F32R, 187 * KB)
        mixed = at("mixed", [P, KT, T], F32, 92 * KB)
        gcs = at("gcs", [P, 2, T], F32, 92 * KB)
        ub = at("ub", [P, 2, T + 3], F32, 97 * KB)
        cb = at("cb", [P, 2, T + 3], F32, 97 * KB + 5152)
        t1 = at("t1", [P, D], F32, 97 * KB + 2 * 5152)
        rowsA = at("rowsA", [P, P], F32, 150 * KB)
        rowsB = at("rowsB", [40, P], F32, 151 * KB)
        xnb1 = [at(f"xnb1_{s}", [P, D], F32, (92 + 4 * s) * KB) for s in range(2)]
        hb1 = [at(f"hb1_{s}", [P, KT, P], F32, (100 + 4 * s) * KB) for s in range(2)]
        xnb2 = [at(f"xnb2_{s}", [P, D], F32, (140 + 4 * s) * KB) for s in range(2)]
        hb2 = [at(f"hb2_{s}", [P, KT, P], F32, (148 + 4 * s) * KB) for s in range(2)]
        zhi = at("zhi", [P, KT // 2, T], F32R, 112 * KB)
        zlo = at("zlo", [P, KT // 2, T], F32R, 122 * KB)
        G = at("G", [P, KT, T], F32, 112 * KB)
        mlo = at("mlo", [P, KT, T], F32R, 112 * KB)
        q = at("q", [P, NT, D], F32, 132 * KB)
        mhi = at("mhi", [P, KT, T], F32R, 132 * KB)
        k = at("k", [P, NT, KVW], F32, 152 * KB)
        v = at("v", [P, NT, KVW], F32, 157 * KB)
        t2 = at("t2", [P, D], F32, 162 * KB)
        tw = at("tw", [P, U5], F32, 162 * KB)
        prob = [at(f"prob{s}", [P, 5 * P], F32, 44 * KB + 2560 * s) for s in range(2)]
        probT = [at(f"probT{s}", [P, 5, P], F32, 49 * KB + 2560 * s) for s in range(2)]
        ot = at("ot", [P, D], F32, 54 * KB)
        qs = [at(f"qs{s}", [P, 4, P], F32R, (163 + 2 * s) * KB) for s in range(2)]
        ck = at("ck", [P, KVW], F32, 59 * KB)
        kst = at("kst", [P, 2, KV, KEYS], F32R, 60 * KB)
        qsp = at("qsp", [P, H, 2, HD], F32, 84 * KB)
        ksp = [at(f"ksp{s}", [P, 2, KV, 2, HD], F32, (44 + 4 * s) * KB) for s in range(2)]
        cv = at("cv", [P, KVW], F32, 162 * KB)
        xsel = at("xsel", [P, KT, 2, SL], F32, 20 * KB)
        xlo = at("xlo", [P, KT, 2, SL], F32R, 20 * KB)
        hidhi = at("hidhi", [P, KT, SL], F32R, 25 * KB)
        xhi = at("xhi", [P, KT, 2, SL], F32R, 124 * KB)
        affhi = at("affhi", [P, NT, E], F32R, 27 * KB + 640)
        afflo = at("afflo", [P, NT, E], F32R, 155 * KB + 256)
        xg_lat = at("xg_lat", [P, D], F32, 161 * KB)
        xg_ctx = at("xg_ctx", [2 * CAP_C, D], F32, 136 * KB)
        hid = [at(f"hid{s}", [SL, 512], F32, (129 + 2 * s) * KB) for s in range(2)]
        hidlo = at("hidlo", [P, KT, SL], F32R, 133 * KB)
        yhi = at("yhi", [SL, 2, D], F32R, 136 * KB)
        ym = at("ym", [SL, 2, D], F32, 144 * KB)
        ylo = at("ylo", [SL, 2, D], F32R, 144 * KB)
        S = at("S", [P, NT, 2, SL], F32R, 152 * KB)
        Sg_lat = at("Sg_lat", [P, LT, 2, CAP_L], F32R, 165 * KB)
        Sg_ctx = at("Sg_ctx", [P, 2, CAP_C], F32R, 27 * KB + 512)
        ST = at("ST", [SL, 2, T], F32R, 156 * KB)
        affT = at("affT", [E, T], F32, 156 * KB)
        work = at("work", [E, T], F32, 159 * KB)
        cum = at("cum", [E, T], F32, 162 * KB)

        ps = nc.alloc_psum_tensor("ps", [P, 8 * 512], F32)

        def bank(b, n=1):
            return ps[:, 512 * b:512 * (b + n)]

        acc = [ps[:, 0:U5], ps[:, 1536:1536 + U5]]
        accc = [ps[:, 1536 * s + P:1536 * s + P + U5] for s in range(2)]
        tp = [bank(0, 2), bank(2, 2)]
        scores = [bank(0, 2), bank(2, 2)]
        ptp = ps[:, 2048:2048 + 5 * P]
        pso = bank(6)
        qtp = bank(7)
        gate_ps = [ps[0:SL, 0:512], ps[0:SL, 512:1024]]
        up_ps = [ps[0:SL, 1024:1536], ps[0:SL, 1536:2048]]
        hidT_ps = [bank(0)[:, 0:4 * SL], bank(1)[:, 0:4 * SL]]
        down_ps = [ps[0:SL, 2048:2560], ps[0:SL, 2560:3072]]
        side = [bank(6), bank(7)]

        def sem(name):
            return ctx.enter_context(nc.semaphore(name))

        waits_passed = sem("waits_passed")
        params_loaded = sem("params_loaded")
        x_loaded = sem("x_loaded")
        setup_tp = sem("setup_tp")
        cols_ready = sem("cols_ready")
        silu_c_ready = sem("silu_c_ready")
        mod_rows_ready = sem("mod_rows_ready")
        mod_cols_done = sem("mod_cols_done")
        mod_ready = sem("mod_ready")
        out_stored = sem("out_stored")
        fn_loaded = sem("fn_loaded")
        dve_chain = sem("dve_chain")
        pool_chain = sem("pool_chain")
        act_chain = sem("act_chain")

        def sig(name, per_layer, before=0):
            return Signal(sem(name), per_layer, before)

        lp_loaded = sig("lp_loaded", 16 * 3)
        cache_loaded = sig("cache_loaded", 16 * 2)
        kv_stored = sig("kv_stored", 16 * 2)
        raw_loaded = [sig(f"raw_loaded{s}", 16 * (UNITS // 2 - 1)) for s in range(2)]
        raw_ao_loaded = [sig(f"raw_ao_loaded{s}", 16) for s in range(2)]
        ring_loaded = [sig(f"ring_loaded{s}", 16 * EU // RING, 16 * 2 * MOD_BLOCKS // RING) for s in range(RING)]
        ring_split_hi = sig("ring_split_hi", EU, 2 * MOD_BLOCKS)
        ring_split_lo = sig("ring_split_lo", len(DVE_LO) * E // 2, 2 * MOD_BLOCKS)
        pool_split_lo = sig("pool_split_lo", len(POOL_LO) * E // 2)
        ring_done = sig("ring_done", EU, 2 * MOD_BLOCKS + HI)
        x_ready = sig("x_ready", 2, 1)
        modl_ready = sig("modl_ready", 1)
        rows_ready = sig("rows_ready", 2)
        rows_taken = sig("rows_taken", 2)
        sq_ready = sig("sq_ready", 10)
        rstd_ready = sig("rstd_ready", 2)
        xn_ready = sig("xn_ready", 10)
        tp_ready = sig("tp_ready", 10)
        h32_ready = sig("h32_ready", 10)
        hi_ready = sig("hi_ready", 10)
        lo_ready = sig("lo_ready", 10)
        logits_done = sig("logits_done", NT)
        whi_ready = sig("whi_ready", UNITS)
        wlo_ready = sig("wlo_ready", UNITS, 2)
        unit_done = sig("unit_done", UNITS, 2)
        acc_taken = [sig(f"acc_taken{s}", UNITS // 2, 1) for s in range(2)]
        ssq_ready = sig("ssq_ready", 1)
        rqk_ready = sig("rqk_ready", 1)
        qk_ready = sig("qk_ready", 1)
        zhi_ready = sig("zhi_ready", 2)
        z_ready = sig("z_ready", 2)
        khi_ready = sig("khi_ready", 6)
        ksplit = sig("ksplit", 6)
        ktp_ready = sig("ktp_ready", 6, 2)
        kst_ready = sig("kst_ready", 6)
        qhi_ready = sig("qhi_ready", NT)
        qsplit = sig("qsplit", NT)
        qt_ready = sig("qt_ready", ITEMS // 4, 1)
        qs_ready = sig("qs_ready", ITEMS // 4, 1)
        s_ready = sig("s_ready", ITEMS, 4)
        nmax_ready = sig("nmax_ready", ITEMS)
        p_ready = sig("p_ready", ITEMS, 2)
        pt_ready = sig("pt_ready", ITEMS, 2)
        pts_ready = sig("pts_ready", ITEMS, 1)
        pv_done = sig("pv_done", ITEMS, 2)
        o_ready = sig("o_ready", 2 * NT, 1)
        otp_ready = sig("otp_ready", NT, 1)
        ohi_ready = sig("ohi_ready", NT)
        oT_ready = sig("oT_ready", NT, 1)
        mrg_ready = sig("mrg_ready", 4)
        mhi_ready = sig("mhi_ready", 4)
        m_ready = sig("m_ready", 4)
        aff_ready = sig("aff_ready", 1)
        lgsub_ready = sig("lgsub_ready", 1)
        lgexp_ready = sig("lgexp_ready", 1)
        affhi_ready = sig("affhi_ready", 1)
        affT_ready = sig("affT_ready", 1)
        slots_ready = sig("slots_ready", 1)
        slotsT_ready = sig("slotsT_ready", 1)
        S_ready = sig("S_ready", E // 2 + 1)
        xhi_ready = sig("xhi_ready", E)
        xlo_ready = sig("xlo_ready", E)
        side_ready = sig("side_ready", SIDES * E // 2)
        side_taken = [sig(f"side_taken{s}", SIDES // 2 * E // 2, 1) for s in range(2)]
        silu_ready = sig("silu_ready", 2 * E)
        hidT_ready = sig("hidT_ready", 2 * E)
        hidhi_ready = sig("hidhi_ready", 2 * E)
        hidlo_ready = sig("hidlo_ready", 2 * E, 2)
        hid_ready = sig("hid_ready", 2 * E, 2)
        ym_ready = sig("ym_ready", 2 * E, 2)
        yhi_ready = sig("yhi_ready", 2 * E)
        ylo_ready = sig("ylo_ready", 2 * E)

        def f32(ap):
            return ap.bitcast(F32)

        block = ctx.enter_context(nc.Block())

        @block.sync
        def _(sp):
            b_mod_rows = b_mod.rearrange("l (j p) -> (l j) p", p=P)
            for dst, src in ((rowsA[0:96, :], b_mod_rows),
                             (rowsA[96:112, :], norm1.rearrange("l (j p) -> (l j) p", p=P)),
                             (rowsA[112:128, :], norm2.rearrange("l (j p) -> (l j) p", p=P)),
                             (rowsB[0:8, :], c.rearrange("b (j p) -> (b j) p", p=P)),
                             (rowsB[8:16, :], c_ctx.rearrange("(j p) -> j p", p=P)),
                             (rowsB[16:40, :], conv_w.rearrange("l j (f p) -> (l j f) p", p=P)),
                             (ident[:, :], ident_c), (slot_ids[:, :], slots_c),
                             (cosT[:, :, :], cos_c.rearrange("(t p) d -> p t d", p=P)),
                             (sinT[:, :, :], sin_c.rearrange("(t p) d -> p t d", p=P))):
                sp.dma_start(dst, src).then_inc(params_loaded, 16)

            def mod_piece(n):
                layer, j, kh = n // 24, n % 24 // 2, n % 2
                src = w_mod[layer].rearrange("(k p) n -> p k n", p=P)
                sp.dma_start(ring[n % RING][:, :, :], src[:, KH * kh:KH * (kh + 1), 512 * j:512 * (j + 1)])\
                  .then_inc(ring_loaded[n % RING].sem, 16)

            for n in range(RING):
                mod_piece(n)
            sp.dma_start(x[:, 0:LT, :], x_sample[0].rearrange("(t p) d -> p t d", p=P)).then_inc(x_loaded, 16)
            sp.dma_start(x[:, LT, :], x_prompt[0]).then_inc(x_loaded, 16)
            for n in range(RING, 2 * MOD_BLOCKS):
                sp.wait_ge(ring_done.sem, HI + n + 1 - RING)
                mod_piece(n)

            with sp.Fori(0, DEPTH) as layer:
                one = ds(layer, 1)
                sp.wait_ge(x_ready.sem, x_ready.at(layer, 0))
                sp.dma_start(wr[:, :, :], w_router[one].rearrange("o (k p) e -> p (o k) e", p=P)).then_inc(lp_loaded.sem, 16)
                sp.dma_start(gq[:, :], q_norm[one, :].broadcast_to([P, HD])).then_inc(lp_loaded.sem, 16)
                sp.dma_start(gk[:, :], k_norm[one, :].broadcast_to([P, HD])).then_inc(lp_loaded.sem, 16)
                sp.wait_ge(ring_done.sem, ring_done.at(layer, 0))
                sp.sem_inc(waits_passed, 1)

                def unit(u, b, src):
                    sp.wait_ge(wlo_ready.sem, wlo_ready.at(layer, u - 1))
                    nk = src.shape[1]
                    sp.dma_start(raw[b][:, 0:nk, :], src).then_inc(raw_loaded[b].sem, 16)

                win = w_in[one].rearrange("o (k p) n -> p (o k) n", p=P)
                wco = w_conv_out[one].rearrange("o (k p) n -> p (o k) n", p=P)
                wao = w_attn_out[one].rearrange("o (k p) n -> p (o k) n", p=P)
                woo = w_o[one].rearrange("o (k p) n -> p (o k) n", p=P)
                with sp.Fori(0, 2) as i:
                    for b in range(2):
                        unit(U_Q + 2 * i + b, b, win[:, :, ds(OQ + (2 * i + b) * UW, UW)])
                unit(U_K, 0, win[:, :, OK_:OK_ + UW])
                unit(U_V, 1, win[:, :, OV:OV + UW])
                for hf in range(2):
                    for j, o in enumerate((OGC, OXI, OGB)):
                        u = U_CONV + 3 * hf + j
                        unit(u, u % 2, win[:, :, o + hf * UW:o + (hf + 1) * UW])
                with sp.Fori(0, 4) as i:
                    unit(U_GATE + 2 * i, 0, win[:, :, ds(OGA + i * UW, UW)])
                    unit(U_GATE + 2 * i + 1, 1, wco[:, :, ds(i * UW, UW)])
                sp.wait_ge(qk_ready.sem, qk_ready.at(layer, 1))
                nk_dst = new_k[0][one].rearrange("l s h d -> (l s) (h d)")
                nv_dst = new_v[0][one].rearrange("l s h d -> (l s) (h d)")
                sp.dma_start(nk_dst, k[:, LT, :]).then_inc(kv_stored.sem, 16)
                sp.dma_start(nv_dst, v[:, LT, :]).then_inc(kv_stored.sem, 16)
                with sp.Fori(0, 2) as i:
                    for b in range(2):
                        unit(U_GT + 2 * i + b, b, win[:, :, ds(OGT + (2 * i + b) * UW, UW)])
                sp.wait_ge(wlo_ready.sem, wlo_ready.at(layer, U_AO))
                for b in range(2):
                    sp.wait_ge(acc_taken[b].sem, acc_taken[b].at(layer, U_AO // 2))
                sp.dma_start(ck[:, :], cache_k[0][one].rearrange("l s h d -> (l s) (h d)")).then_inc(cache_loaded.sem, 16)
                sp.dma_start(cv[:, :], cache_v[0][one].rearrange("l s h d -> (l s) (h d)")).then_inc(cache_loaded.sem, 16)
                sp.wait_ge(qsplit.sem, qsplit.at(layer, NT))
                for b in range(2):
                    sp.dma_start(raw_ao[b][:, :, :], wao[:, :, b * UW:(b + 1) * UW]).then_inc(raw_ao_loaded[b].sem, 16)
                sp.wait_ge(oT_ready.sem, oT_ready.at(layer, NT))
                sp.sem_inc(waits_passed, 1)
                for b in range(2):
                    sp.dma_start(raw[b][:, :, :], wao[:, :, (2 + b) * UW:(3 + b) * UW]).then_inc(raw_loaded[b].sem, 16)
                with sp.Fori(0, 2) as i:
                    for b in range(2):
                        unit(U_WO + 2 * i + b, b, woo[:, :, ds((2 * i + b) * UW, UW)])
                sp.wait_ge(kv_stored.sem, kv_stored.at(layer, 32))
                sp.sem_inc(waits_passed, 1)
                sp.wait_ge(x_ready.sem, x_ready.at(layer, 1))
                sp.sem_inc(waits_passed, 1)
                with sp.Fori(0, E) as e:
                    for n, (w, b, kh) in enumerate(PIECES):
                        sp.wait_ge(ring_done.sem, ring_done.at(layer, EP * e + (n + 1 - RING)))
                        src = (w_gate, w_up, w_down)[w][one][:, ds(e, 1)].rearrange("l e (k p) n -> p (l e k) n", p=P)
                        sp.dma_start(ring[n % RING][:, :, :], src[:, KH * kh:KH * (kh + 1), b * 512:(b + 1) * 512])\
                          .then_inc(ring_loaded[n % RING].sem, 16)

            sp.wait_ge(x_ready.sem, x_ready.at(DEPTH, 0))
            sp.dma_start(gbc[:, 0, :], final_norm.rearrange("(o d) -> o d", o=1).broadcast_to([P, D])).then_inc(fn_loaded, 16)
            ys = y_sample[0].rearrange("(t p) d -> p t d", p=P)
            for t in range(NT):
                sp.wait_ge(xn_ready.sem, xn_ready.at(DEPTH, t + 1))
                sp.dma_start(ys[:, t, :] if t < LT else y_prompt[0], x[:, t, :]).then_inc(out_stored, 16)
            sp.wait_ge(out_stored, 16 * NT)

        @block.gpsimd
        def _(pool):
            ch = Chain(pool, 5)

            def rsqrt(ap, n, done):
                pool.tensor_scalar(ap, ap, 1.0 / n, EPS, ALU.mult, ALU.add).then_inc(pool_chain, 1)
                pool.wait_ge(pool_chain, ch.next())
                pool.tensor_tensor(ap, ap, minus_half[:, 0:1].broadcast_to(list(ap.shape)), ALU.pow).then_inc(done, 1)

            pool.memset(minus_half[:, :], -0.5).then_inc(pool_chain, 1)
            ch.n = 1
            pool.wait_ge(pool_chain, 1)
            with ch.layers() as layer:
                pool.wait_ge(sq_ready.sem, sq_ready.at(layer, NT))
                pool.sem_inc(waits_passed, 1)
                rsqrt(ss[:, 0, 0:NT], D, rstd_ready.sem)
                pool.wait_ge(ssq_ready.sem, ssq_ready.at(layer, 1))
                pool.sem_inc(waits_passed, 1)
                pool.tensor_scalar(rq[:, :, :], rq[:, :, :], 1.0 / HD, EPS, ALU.mult, ALU.add).then_inc(pool_chain, 1)
                pool.wait_ge(pool_chain, ch.next())
                pool.tensor_tensor(rq[:, :, :].rearrange("p t h -> p (t h)"), rq[:, :, :].rearrange("p t h -> p (t h)"),
                                                 minus_half[:, 0:1].broadcast_to([P, NT * H]), ALU.pow).then_inc(pool_chain, 1)
                pool.wait_ge(pool_chain, ch.next())
                pool.sem_inc(waits_passed, 1)
                rsqrt(rk[:, :, :].rearrange("p t h -> p (t h)"), HD, rqk_ready.sem)
                pool.wait_ge(sq_ready.sem, sq_ready.at(layer, 2 * NT))
                pool.sem_inc(waits_passed, 1)
                rsqrt(ss[:, 1, 0:NT], D, rstd_ready.sem)
                with pool.Fori(0, E // 2) as p:
                    for m in POOL_LO:
                        pool.wait_ge(ring_split_hi.sem, ring_split_hi.at(layer, p * PP + (m + 1)))
                        pool.sem_inc(waits_passed, 1)
                        pool.tensor_tensor(ring_lo[m % RING][:, :, :], ring[m % RING][:, :, :], f32(ring_hi[m % HI][:, :, :]),
                                           ALU.subtract).then_inc(pool_split_lo.sem, 1)
            pool.wait_ge(sq_ready.sem, sq_ready.at(DEPTH, NT))
            rsqrt(ss[:, 0, 0:NT], D, rstd_ready.sem)

        @block.scalar
        def _(act):
            act.sem_inc(qs_ready.sem, 1)
            act.sem_inc(p_ready.sem, 2)
            act.wait_ge(cols_ready, 1)
            for s in range(2):
                ins = act.activation(sc[:, :, s], colsB[:, 8 * s:8 * s + 8], ACT.Silu)
            ins.then_inc(act_chain, 1)
            act.sem_inc(mod_rows_ready, 2)
            act.wait_ge(act_chain, 1)
            act.activation(sc4[:, :, 0:2], sc[:, :, :], ACT.Copy).then_inc(silu_c_ready, 1)
            with act.Fori(0, MOD_GROUPS) as i:
                for n in range(MP):
                    act.wait_ge(ring_loaded[n % RING].sem, i * (16 * MP // RING) + 16 * (n // RING + 1))
                    act.wait_ge(ring_done.sem, i * MP + (n + 1))
                    act.activation(ring_hi[n % HI][:, :, :], ring[n % RING][:, :, :], ACT.Copy).then_inc(ring_split_hi.sem, 1)
                    last = MP // 2 - 1
                    for j in (range(last - 2, last + 1) if n == MP - 1 else ((n - 5) // 2,) if n % 2 and n >= 5 else ()):
                        act.wait_ge(ring_done.sem, i * MP + (HI + 2 * j + 2))
                        act.wait_ge(mod_cols_done, i * (MP // 2) + (j + 1))
                        act.activation(mod_rows[j % 2][:, :], ps[0:4, 512 * (j % 2):512 * (j % 2 + 1)], ACT.Copy)                           .then_inc(mod_rows_ready, 1)

            def squares(layer, t, row):
                if t >= 2:
                    act.wait_ge(sq_ready.sem, sq_ready.at(layer, NT * row + t - 1))
                act.activation(tp[t % 2], x[:, t, :], ACT.Square, accum_out=ss[:, row, t:t + 1]).then_inc(sq_ready.sem, 1)

            with act.Fori(0, DEPTH) as layer:
                def split(h, b, nk=KT, raw=raw):
                    if raw is raw_ao:
                        act.wait_ge(raw_ao_loaded[b].sem, raw_ao_loaded[b].at(layer, 16))
                    else:
                        own = 0 if isinstance(h, int) and h > U_AO // 2 else 1
                        act.wait_ge(raw_loaded[b].sem, raw_loaded[b].at(layer, (h + own) * 16))
                    act.wait_ge(unit_done.sem, unit_done.at(layer, 2 * h + (b - 1)))
                    act.activation(whi[b][:, 0:nk, :], raw[b][:, 0:nk, :], ACT.Copy).then_inc(whi_ready.sem, 1)

                def take(h, b, out, func=ACT.Copy, acc=accc):
                    act.wait_ge(unit_done.sem, unit_done.at(layer, 2 * h + (b + 1)))
                    act.activation(out, acc[b], func).then_inc(acc_taken[b].sem, 1)

                act.wait_ge(x_ready.sem, x_ready.at(layer, 0))
                for t in range(NT):
                    squares(layer, t, 0)
                act.wait_ge(rows_ready.sem, rows_ready.at(layer, 1))
                act.activation(gbc[:, :, :].rearrange("p s d -> p (s d)"), bank(4, 4), ACT.Copy).then_inc(rows_taken.sem, 1)
                act.wait_ge(rows_ready.sem, rows_ready.at(layer, 2))
                act.activation(g2mix[0:64, :], ps[0:64, 2048:3072], ACT.Copy)
                act.activation(g2mix[64:SL, :], ps[64:SL, 3072:4096], ACT.Copy).then_inc(rows_taken.sem, 1)
                for t in range(NT):
                    act.wait_ge(h32_ready.sem, h32_ready.at(layer, t + 1))
                    act.activation(hThi[:, :, t * P:(t + 1) * P], hb1[t % 2][:, :, :], ACT.Copy).then_inc(hi_ready.sem, 1)
                split(0, 0)
                with act.Fori(0, 2) as i:
                    split(i, 1)
                    take(i, 0, q[:, :, ds(i * (2 * UW), UW)], acc=acc)
                    split(i + 1, 0)
                    take(i, 1, q[:, :, ds(i * (2 * UW) + UW, UW)], acc=acc)
                split(2, 1)
                take(2, 0, k[:, :, :].rearrange("p t n -> p (t n)"), acc=acc)
                split(3, 0)
                take(2, 1, v[:, :, :].rearrange("p t n -> p (t n)"), acc=acc)
                for hf in range(2):
                    u = U_CONV + 3 * hf
                    if hf == 0:
                        split((u + 1) // 2, (u + 1) % 2)
                    else:
                        act.wait_ge(z_ready.sem, z_ready.at(layer, 1))
                    take(u // 2, u % 2, gcs[:, :, :].rearrange("p a n -> p (a n)"))
                    split((u + 2) // 2, (u + 2) % 2)
                    split((u + 3) // 2, (u + 3) % 2)
                    act.wait_ge(acc_taken[u % 2].sem, acc_taken[u % 2].at(layer, (u + 2) // 2 + 1))
                    act.activation(zhi[:, 2 * hf:2 * hf + 2, :], gcs[:, :, :], ACT.Copy).then_inc(zhi_ready.sem, 1)
                    if hf == 0:
                        split((u + 4) // 2, (u + 4) % 2)
                act.wait_ge(qk_ready.sem, qk_ready.at(layer, 1))
                act.sem_inc(waits_passed, 1)
                with act.Fori(0, 4) as i:
                    split(U_GATE // 2 + i, 1, KT // 2)
                    act.wait_ge(acc_taken[1].sem, acc_taken[1].at(layer, U_GATE // 2 + i))
                    take(U_GATE // 2 + i, 0, tw[:, :], ACT.Sigmoid)
                    split(U_GATE // 2 + 1 + i, 0)
                for j in range(4):
                    if j < 3:
                        if j:
                            split((U_GT + j + 1) // 2, (j + 1) % 2)
                        else:
                            split(U_GT // 2, 1)
                    take((U_GT + j) // 2, j % 2, G[:, 2 * j:2 * j + 2, :].rearrange("p a n -> p (a n)"), ACT.Sigmoid)
                act.wait_ge(unit_done.sem, unit_done.at(layer, U_AO))
                act.wait_ge(wlo_ready.sem, wlo_ready.at(layer, U_AO))
                act.wait_ge(cache_loaded.sem, cache_loaded.at(layer, 32))
                for kt in range(7):
                    if kt < 6:
                        src = ck[:, :] if kt == 0 else k[:, kt - 1, :]
                        act.wait_ge(ktp_ready.sem, ktp_ready.at(layer, kt - 1))
                        act.activation(ksp[kt % 2][:, 0].bitcast(F32R), src.rearrange("p (v d) -> p v d", v=KV).unsqueeze(2).to_broadcast(
                            [P, KV, 2, HD]), ACT.Copy).then_inc(khi_ready.sem, 1)
                    if kt:
                        act.wait_ge(ktp_ready.sem, ktp_ready.at(layer, kt))
                        act.activation(kst[:, :, :, (kt - 1) * P:kt * P], tp[(kt - 1) % 2].rearrange("p (s v n) -> p s v n", s=2, v=KV),
                                       ACT.Copy).then_inc(kst_ready.sem, 1)

                def query_halves(t):
                    act.wait_ge(qt_ready.sem, qt_ready.at(layer, t * 4))
                    act.activation(qsp[:, :, 0, :].bitcast(F32R), q[:, ds(t, 1), :].rearrange("p o (h d) -> p (o h) d", h=H),
                                   ACT.Copy).then_inc(qhi_ready.sem, 1)

                query_halves(0)
                act.wait_ge(qt_ready.sem, qt_ready.at(layer, 1))
                act.wait_ge(s_ready.sem, s_ready.at(layer, -4))
                act.activation(qs[0][:, :, :].rearrange("p h n -> p (h n)"), qtp, ACT.Copy).then_inc(qs_ready.sem, 1)

                def attend(t, nk, more=True):
                    base = t * H

                    def queries(g):
                        act.wait_ge(qt_ready.sem, qt_ready.at(layer, t * 4 + (g + 1)))
                        act.wait_ge(s_ready.sem, s_ready.at(layer, base + (4 * g - 4)))
                        act.activation(qs[g % 2][:, :, :].rearrange("p h n -> p (h n)"), qtp, ACT.Copy).then_inc(qs_ready.sem, 1)

                    act.wait_ge(o_ready.sem, o_ready.at(layer, t * 2))
                    for j in range(H):
                        if j % 4 == 1 and j // 4 < 3:
                            queries(j // 4 + 1)
                        act.wait_ge(nmax_ready.sem, nmax_ready.at(layer, base + (j + 1)))
                        act.wait_ge(pt_ready.sem, pt_ready.at(layer, base + (j - 1)))
                        act.activation(prob[j % 2][:, 0:nk * P], scores[j % 2][:, 0:nk * P], ACT.Exp,
                                       bias=nmax[:, j % 2:j % 2 + 1], accum_out=rsum[:, j:j + 1]).then_inc(p_ready.sem, 1)
                        if j == 12 and more:
                            query_halves(t + 1)
                    if more:
                        queries(4)
                    act.wait_ge(otp_ready.sem, otp_ready.at(layer, t + 1))
                    act.activation(oThi[:, :, ds(t * P, P)], bank(2, 2).rearrange("p (k n) -> p k n", k=KT), ACT.Copy).then_inc(ohi_ready.sem, 1)

                with act.Fori(0, LT) as t:
                    attend(t, 5)
                attend(LT, 1, more=False)
                act.wait_ge(oT_ready.sem, oT_ready.at(layer, NT))
                split(U_AO // 2, 0, KT, raw_ao)
                for j in range(4):
                    split((U_AO + j + 1) // 2, (j + 1) % 2, KT, raw_ao if j == 0 else raw)
                    act.wait_ge(mrg_ready.sem, mrg_ready.at(layer, j + 1))
                    act.activation(mhi[:, 2 * j:2 * j + 2, :].rearrange("p a n -> p (a n)"), tw[:, :], ACT.Copy).then_inc(mhi_ready.sem, 1)
                for u in range(U_WO + 1, UNITS):
                    split(u // 2, u % 2)
                act.wait_ge(x_ready.sem, x_ready.at(layer, 1))
                for t in range(NT):
                    squares(layer, t, 1)
                for t in range(NT):
                    act.wait_ge(xn_ready.sem, xn_ready.at(layer, NT + t + 1))
                    act.activation(xnhi[:, t, :], xnb2[t % 2][:, :], ACT.Copy).then_inc(hi_ready.sem, 1)
                act.wait_ge(lgsub_ready.sem, lgsub_ready.at(layer, 1))
                copy2 = act.activation(lg[:, :, :], lg[:, :, :], ACT.Exp)
                copy2.then_inc(lgexp_ready.sem, 1)
                act.wait_ge(aff_ready.sem, aff_ready.at(layer, 1))
                act.activation(affhi[:, :, :], aff[:, :, :], ACT.Copy).then_inc(affhi_ready.sem, 1)
                with act.Fori(0, E // 2) as p:
                    for m in range(PP + 4):
                        for e, r in ((0, m), (1, m - EP)):
                            if r in TURNED[e]:
                                b = TURNED[e].index(r)
                                act.wait_ge(hidT_ready.sem, hidT_ready.at(layer, p * 4 + (2 * e + b + 1)))
                                act.activation(hidhi[:, 4 * b:4 * b + 4, :].rearrange("p a n -> p (a n)"), hidT_ps[b],
                                               ACT.Copy).then_inc(hidhi_ready.sem, 1)
                        if m in (9, 10):
                            e = m - 9
                            for b in range(2):
                                n = 7 + 2 * e + b
                                act.wait_ge(side_ready.sem, side_ready.at(layer, p * SIDES + (n + 1)))
                                out = ST[:, e, 0:LAT] if b == 0 else ST[:, e, LAT:T]
                                act.activation(out, side[n % 2][0:SL, 0:LAT if b == 0 else CTX], ACT.Copy)\
                                   .then_inc(side_taken[n % 2].sem, 1)
                        if m < PP:
                            act.wait_ge(ring_loaded[m % RING].sem, ring_loaded[m % RING].at(layer, p * 64 + 16 * (m // RING + 1)))
                            act.wait_ge(ring_done.sem, ring_done.at(layer, p * PP + (m + 1 - HI)))
                            act.activation(ring_hi[m % HI][:, :, :], ring[m % RING][:, :, :], ACT.Copy).then_inc(ring_split_hi.sem, 1)
                        if m == 3:
                            def gathered(n, out):
                                act.wait_ge(side_ready.sem, side_ready.at(layer, p * SIDES + (n + 1)))
                                act.activation(out, side[n % 2][0:out.shape[0], :], ACT.Copy).then_inc(side_taken[n % 2].sem, 1)

                            gathered(0, xg_ctx[:, 0:512])
                            gathered(1, xg_ctx[:, 512:D])
                            gathered(2, xg_lat[:, 0:512])
                            act.wait_ge(side_taken[0].sem, side_taken[0].at(layer, p * (SIDES // 2) + 3))
                            act.activation(xhi[:, 0:4], xsel[:, 0:4], ACT.Copy).then_inc(xhi_ready.sem, 1)
                            gathered(5, xg_lat[:, 512:D])
                            act.wait_ge(side_ready.sem, side_ready.at(layer, p * SIDES + 7))
                            src = side[0].rearrange("p (k e c) -> p k e c", k=4, e=2)
                            for dd in range(4, KT):
                                ins = act.activation(xsel[:, dd, :, 0:CAP_L], src[:, dd % 4], ACT.Identity,
                                                     bias=modl[:, 24 + dd, 0:1], scale=A2[:, dd, 0:1])
                            ins.then_inc(side_taken[0].sem, 1)
                            act.wait_ge(side_taken[0].sem, side_taken[0].at(layer, p * (SIDES // 2) + 4))
                            act.activation(xhi[:, 4:8], xsel[:, 4:8], ACT.Copy).then_inc(xhi_ready.sem, 1)
                        for e, r in ((0, m), (1, m - EP)):
                            if r in (5, 9):
                                b = int(r == 9)
                                act.wait_ge(ring_done.sem, ring_done.at(layer, p * PP + (EP * e + 4 * b + 2)))
                                act.activation(hid[b][:, :], gate_ps[b], ACT.Silu).then_inc(silu_ready.sem, 1)
                            if r in (14, 15):
                                b = r - 14
                                act.wait_ge(ym_ready.sem, ym_ready.at(layer, p * 4 + (2 * e + b + 1)))
                                cols = slice(512 * b, 512 * (b + 1))
                                act.activation(yhi[:, e, cols], ym[:, e, cols], ACT.Copy).then_inc(yhi_ready.sem, 1)
            act.wait_ge(x_ready.sem, x_ready.at(DEPTH, 0))
            for t in range(NT):
                squares(DEPTH, t, 0)

        @block.tensor
        def _(pe):
            for signal, n in ((unit_done, 2), (ktp_ready, 2), (qt_ready, 1), (s_ready, 4), (pt_ready, 2), (pv_done, 2),
                              (otp_ready, 1), (ring_done, HI)):
                pe.sem_inc(signal.sem, n)
            pe.sem_inc(mod_cols_done, 2)
            pe.wait_ge(params_loaded, 160)
            pe.transpose(ps[:, 0:P], rowsA[:, :], ident[:, :])
            pe.transpose(ps[:, P:P + 40], rowsB[:, :], ident[0:40, 0:40]).then_inc(setup_tp, 1)
            pe.wait_ge(silu_c_ready, 2)
            with pe.Fori(0, MOD_GROUPS) as i:
                def mod_columns(j):
                    pe.wait_ge(mod_rows_ready, i * (MP // 2) + (j + 3))
                    for a in range(4):
                        ins = pe.matmul(ps[:, ds(i * (4 * MP) + (1024 + 2 * (4 * j + a)), 2)], mod_rows[j % 2][:, a * P:(a + 1) * P],
                                        sum_halves[:, :], start=True, stop=True)
                    ins.then_inc(mod_cols_done, 1)

                for j in range(MP // 2):
                    pe.wait_ge(mod_rows_ready, i * (MP // 2) + (j + 1))
                    for kh in range(2):
                        n = 2 * j + kh
                        pe.wait_ge(ring_split_lo.sem, i * MP + (n + 1))
                        for kk in range(KH):
                            for w in (ring_hi[n % HI], ring_lo[n % RING]):
                                ins = pe.matmul(ps[0:4, 512 * (j % 2):512 * (j % 2 + 1)], sc4[:, KH * kh + kk, :], w[:, kk, :],
                                                start=(n % 2 == 0 and kk == 0 and w is ring_hi[n % HI]),
                                                stop=(kh == 1 and kk == KH - 1 and w is ring_lo[n % RING]))
                        ins.then_inc(ring_done.sem, 1)
                    if j:
                        mod_columns(j - 1)
                mod_columns(MP // 2 - 1)

            with pe.Fori(0, DEPTH) as layer:
                pe.wait_ge(modl_ready.sem, modl_ready.at(layer, 1))
                for g in range(2):
                    if g:
                        pe.wait_ge(rows_taken.sem, rows_taken.at(layer, 1))
                    for s in range(2):
                        for j in range(KT):
                            col = modl[:, (16 + 24 * g + j):(17 + 24 * g + j), s].broadcast_to([P, P])
                            o = 2048 + 1024 * s + P * j
                            ins = pe.matmul(ps[:, o:o + P], col, ident[:, :], start=True, stop=True)
                    ins.then_inc(rows_ready.sem, 1)

                def transpose_tile(n, t, src):
                    pe.wait_ge(xn_ready.sem, xn_ready.at(layer, n * NT + t + 1))
                    if t >= 2:
                        pe.wait_ge(h32_ready.sem, h32_ready.at(layer, n * NT + t - 1))
                    for j in range(KT):
                        ins = pe.transpose(tp[t % 2][:, j * P:(j + 1) * P], src[:, j * P:(j + 1) * P], ident[:, :])
                    ins.then_inc(tp_ready.sem, 1)

                for t in range(NT):
                    transpose_tile(0, t, xnb1[t % 2])

                def columns(h, b, ahi, alo, nk=KT, k0=0):
                    pe.wait_ge(wlo_ready.sem, wlo_ready.at(layer, 2 * h + (b + 1)))
                    pe.wait_ge(acc_taken[b].sem, acc_taken[b].at(layer, h))
                    for a, pieces in ((0, ((0, 384), (384, T))), (1, ((0, 256), (256, T)))):
                        for kk in range(nk):
                            for n, (w, xx) in enumerate(((whi, ahi), (whi, alo), (wlo, ahi))):
                                for lo, hi in pieces:
                                    ins = pe.matmul(accc[b][:, a * T + lo:a * T + hi], w[b][:, kk, a * P:(a + 1) * P],
                                                    xx[:, k0 + kk, lo:hi], start=(kk == 0 and n == 0),
                                                    stop=(kk == nk - 1 and n == 2))
                    ins.then_inc(unit_done.sem, 1)

                def rows(h, b, ahi, alo):
                    pe.wait_ge(wlo_ready.sem, wlo_ready.at(layer, 2 * h + (b + 1)))
                    pe.wait_ge(acc_taken[b].sem, acc_taken[b].at(layer, h))
                    for t in range(NT):
                        for kk in range(KT):
                            for n, (w, xx) in enumerate(((whi, ahi), (wlo, ahi), (whi, alo))):
                                ins = pe.matmul(acc[b][:, t * UW:(t + 1) * UW], xx[:, kk, t * P:(t + 1) * P], w[b][:, kk, :],
                                                start=(kk == 0 and n == 0), stop=(kk == KT - 1 and n == 2))
                    ins.then_inc(unit_done.sem, 1)

                pe.wait_ge(lo_ready.sem, lo_ready.at(layer, NT))
                pe.sem_inc(waits_passed, 1)
                with pe.Fori(0, 3) as i:
                    for b in range(2):
                        rows(i, b, hThi, hTlo)
                with pe.Fori(0, 3) as i:
                    for b in range(2):
                        columns(U_CONV // 2 + i, b, hThi, hTlo)
                with pe.Fori(0, 4) as i:
                    columns(U_GATE // 2 + i, 0, hThi, hTlo)
                    pe.wait_ge(z_ready.sem, z_ready.at(layer, 2))
                    columns(U_GATE // 2 + i, 1, zhi, zlo, KT // 2)
                with pe.Fori(0, 2) as i:
                    for b in range(2):
                        columns(U_GT // 2 + i, b, hThi, hTlo)

                for kt in range(6):
                    pe.wait_ge(ksplit.sem, ksplit.at(layer, kt + 1))
                    if kt >= 2:
                        pe.wait_ge(kst_ready.sem, kst_ready.at(layer, kt - 1))
                    for s in range(2):
                        for g in range(KV):
                            o = (s * KV + g) * P
                            ins = pe.transpose(tp[kt % 2][:, o:o + P], ksp[kt % 2][:, s, g].rearrange("p a d -> p (a d)"), ident[:, :])
                    ins.then_inc(ktp_ready.sem, 1)
                pe.wait_ge(kst_ready.sem, kst_ready.at(layer, 6))
                pe.sem_inc(waits_passed, 1)

                def queries(t, g):
                    if g == 0:
                        pe.wait_ge(qsplit.sem, qsplit.at(layer, t + 1))
                    pe.wait_ge(qs_ready.sem, qs_ready.at(layer, t * 4 + g))
                    for h in range(4):
                        ins = pe.transpose(qtp[:, h * P:(h + 1) * P], qsp[:, 4 * g + h].rearrange("p a d -> p (a d)"), ident[:, :])
                    ins.then_inc(qt_ready.sem, 1)

                queries(0, 0)

                def attend(t, nk, key0, more=True):
                    base = t * H
                    n = nk * P

                    for j in range(1, H + 4):
                        if j % 4 == 2 and j // 4 < 3:
                            queries(t, j // 4 + 1)
                        if j < H + 1:
                            i = j - 1
                            if i == 1:
                                pe.wait_ge(oT_ready.sem, oT_ready.at(layer, t))
                            if i % 4 == 0:
                                pe.wait_ge(qs_ready.sem, qs_ready.at(layer, t * 4 + (i // 4 + 1)))
                            pe.wait_ge(p_ready.sem, p_ready.at(layer, base + (i - 1)))
                            for lo, hi in ((0, min(n, 512)), (512, n)):
                                if hi > lo:
                                    for s in range(2):
                                        ins = pe.matmul(scores[i % 2][:, lo:hi], qs[i // 4 % 2][:, i % 4, :],
                                                        kst[:, s, i // 4, key0 + lo:key0 + hi], start=(s == 0), stop=(s == 1))
                            ins.then_inc(s_ready.sem, 1)
                        if 3 <= j < H + 3:
                            i = j - 3
                            pe.wait_ge(p_ready.sem, p_ready.at(layer, base + (i + 1)))
                            pe.wait_ge(pts_ready.sem, pts_ready.at(layer, base + i))
                            for a in range(nk):
                                ins = pe.transpose(ptp[:, a * P:(a + 1) * P], prob[i % 2][:, a * P:(a + 1) * P], ident[:, :])
                            ins.then_inc(pt_ready.sem, 1)
                        if 4 <= j:
                            i = j - 4
                            pe.wait_ge(pts_ready.sem, pts_ready.at(layer, base + (i + 1)))
                            if i % 8 == 0:
                                pe.wait_ge(o_ready.sem, o_ready.at(layer, t * 2 + i // 8))
                            for a in range(nk):
                                g = i // 4
                                kt = key0 // P + a
                                vv = cv[:, g * HD:(g + 1) * HD] if kt == 0 else v[:, kt - 1, g * HD:(g + 1) * HD]
                                ins = pe.matmul(pso[:, i % 8 * HD:(i % 8 + 1) * HD], probT[i % 2][:, a, :], vv,
                                                start=(a == 0), stop=(a == nk - 1))
                            ins.then_inc(pv_done.sem, 1)
                    if more:
                        queries(t + 1, 0)
                    pe.wait_ge(o_ready.sem, o_ready.at(layer, t * 2 + 2))
                    for j in range(KT):
                        ins = pe.transpose(ps[:, 1024 + j * P:1024 + (j + 1) * P], ot[:, j * P:(j + 1) * P], ident[:, :])
                    ins.then_inc(otp_ready.sem, 1)

                with pe.Fori(0, LT) as t:
                    attend(t, 5, 0)
                attend(LT, 1, PAST + LAT, more=False)

                pe.wait_ge(oT_ready.sem, oT_ready.at(layer, NT))
                pe.sem_inc(waits_passed, 1)
                with pe.Fori(0, 2) as i:
                    for b in range(2):
                        columns(U_AO // 2 + i, b, oThi, oTlo)
                pe.wait_ge(m_ready.sem, m_ready.at(layer, 4))
                pe.sem_inc(waits_passed, 1)
                with pe.Fori(0, 2) as i:
                    for b in range(2):
                        rows(U_WO // 2 + i, b, mhi, mlo)

                for t in range(NT + 1):
                    if t < NT:
                        transpose_tile(1, t, xnb2[t % 2])
                    if t:
                        r = t - 1
                        pe.wait_ge(h32_ready.sem, h32_ready.at(layer, NT + r + 1))
                        if r == 0:
                            pe.wait_ge(lp_loaded.sem, lp_loaded.at(layer, 48))
                        for kk in range(KT):
                            ins = pe.matmul(bank(4)[:, r * E:(r + 1) * E], hb2[r % 2][:, kk, :], wr[:, kk, :],
                                            start=(kk == 0), stop=(kk == KT - 1))
                        ins.then_inc(logits_done.sem, 1)
                pe.wait_ge(aff_ready.sem, aff_ready.at(layer, 1))
                for t in range(NT):
                    ins = pe.transpose(ps[0:E, 2560 + t * P:2560 + (t + 1) * P], aff[:, t, :], ident[:, :])
                ins.then_inc(affT_ready.sem, 1)
                pe.wait_ge(slots_ready.sem, slots_ready.at(layer, 1))
                pe.sem_inc(waits_passed, 1)
                for t in range(NT):
                    ins = pe.transpose(bank(7)[:, t * E:(t + 1) * E], work[:, t * P:(t + 1) * P], ident[0:E, 0:E])
                ins.then_inc(slotsT_ready.sem, 1)

                pe.wait_ge(lo_ready.sem, lo_ready.at(layer, 2 * NT))
                pe.sem_inc(waits_passed, 1)
                with pe.Fori(0, E // 2) as p:
                    def side_use(n):
                        pe.wait_ge(side_taken[n % 2].sem, side_taken[n % 2].at(layer, p * (SIDES // 2) + n // 2))
                        return side[n % 2]

                    pe.wait_ge(S_ready.sem, S_ready.at(layer, p + 1))
                    def gather(n, chosen, tiles, half):
                        out = side_use(n)[0:chosen(tiles[0]).shape[1], :]
                        for t in tiles:
                            for part in (xnhi, xnlo):
                                ins = pe.matmul(out, chosen(t), part[:, t, 512 * half:512 * (half + 1)],
                                                start=(t == tiles[0] and part is xnhi), stop=(t == tiles[-1] and part is xnlo))
                        ins.then_inc(side_ready.sem, 1)

                    def turn_latent(n, half):
                        out = side_use(n)
                        for j in range(4):
                            ins = pe.transpose(out[:, j * P:(j + 1) * P], xg_lat[:, (4 * half + j) * P:(4 * half + j + 1) * P],
                                               ident[:, :])
                        ins.then_inc(side_ready.sem, 1)

                    def latent(t):
                        return Sg_lat[:, t].rearrange("p e c -> p (e c)")

                    def context(t):
                        return Sg_ctx[:, :, :].rearrange("p e c -> p (e c)")

                    gather(0, context, (LT,), 0)
                    gather(1, context, (LT,), 1)
                    gather(2, latent, range(LT), 0)
                    out = side_use(3)
                    pe.sem_inc(waits_passed, 1)
                    for j in range(KT):
                        ins = pe.transpose(out[:, j * 2 * CAP_C:(j + 1) * 2 * CAP_C], xg_ctx[:, j * P:(j + 1) * P],
                                           ident[0:2 * CAP_C, 0:2 * CAP_C])
                    ins.then_inc(side_ready.sem, 1)
                    turn_latent(4, 0)
                    gather(5, latent, range(LT), 1)
                    pe.wait_ge(side_taken[1].sem, side_taken[1].at(layer, p * (SIDES // 2) + 3))
                    turn_latent(6, 1)
                    for m in range(PP):
                        e, r = m // EP, m % EP
                        w, b, kh = PIECES[r]
                        if m < 2:
                            pe.wait_ge(xlo_ready.sem, xlo_ready.at(layer, p * 2 + (m + 1)))
                        if m in POOL_LO:
                            pe.wait_ge(pool_split_lo.sem, pool_split_lo.at(layer, p * len(POOL_LO) + (POOL_LO.index(m) + 1)))
                        else:
                            pe.wait_ge(ring_split_lo.sem, ring_split_lo.at(layer, p * len(DVE_LO) + (DVE_LO.index(m) + 1)))
                        if kh == 0:
                            free = (hidlo_ready, hid_ready, ym_ready)[w]
                            pe.wait_ge(free.sem, free.at(layer, p * 4 + (2 * e + b - 1)))
                        if w == 2 and b == 0:
                            pe.wait_ge(hidlo_ready.sem, hidlo_ready.at(layer, p * 4 + (2 * e + kh + 1)))
                        out = (gate_ps, up_ps, down_ps)[w][b]
                        for kk in range(KH):
                            k8 = KH * kh + kk
                            ahi, alo = (xhi[:, k8, e, :], xlo[:, k8, e, :]) if w < 2 else (hidhi[:, k8, :], hidlo[:, k8, :])
                            for n, (a, ww) in enumerate(((ahi, ring_hi[m % HI]), (ahi, ring_lo[m % RING]), (alo, ring_hi[m % HI]))):
                                ins = pe.matmul(out, a, ww[:, kk, :], start=(k8 == 0 and n == 0), stop=(k8 == KT - 1 and n == 2))
                        ins.then_inc(ring_done.sem, 1)
                        if r in (5, 8):
                            b = int(r == 8)
                            pe.wait_ge(hid_ready.sem, hid_ready.at(layer, p * 4 + (2 * e + b + 1)))
                            for j in range(4):
                                ins = pe.transpose(hidT_ps[b][:, j * SL:(j + 1) * SL], hid[b][:, j * P:(j + 1) * P],
                                                   ident[0:SL, 0:SL])
                            ins.then_inc(hidT_ready.sem, 1)
                        if m in (5, 6):
                            for b in range(2):
                                out = side_use(7 + 2 * (m - 5) + b)
                                for n, t in enumerate(range(LT) if b == 0 else (LT,)):
                                    ins = pe.transpose(out[0:SL, n * P:(n + 1) * P], f32(S[:, t, m - 5, :]), ident[:, :])
                                ins.then_inc(side_ready.sem, 1)
                        if m in (8, 9):
                            c = 2 * (m - 8)
                            if m == 8:
                                side_use(11)
                            for t in range(NT):
                                for part in (affhi, afflo):
                                    ins = pe.matmul(side[1][0:SL, c:c + 2], S[:, t, m - 8, :], part[:, t, ds(p * 2, 2)],
                                                    start=(t == 0 and part is affhi), stop=(t == NT - 1 and part is afflo))
                            if m == 9:
                                ins.then_inc(side_ready.sem, 1)
                    pe.wait_ge(side_taken[0].sem, side_taken[0].at(layer, p * (SIDES // 2) + 6))
                    for b in range(2):
                        pe.wait_ge(ylo_ready.sem, ylo_ready.at(layer, p * 4 + (3 + b)))
                        for t in range(NT):
                            out = side_use(12 + NT * b + t)
                            for n, (e, part) in enumerate(((0, yhi), (0, ylo), (1, yhi), (1, ylo))):
                                ins = pe.matmul(out[:, :], ST[:, e, t * P:(t + 1) * P], part[:, e, 512 * b:512 * (b + 1)],
                                                start=(n == 0), stop=(n == 3))
                            ins.then_inc(side_ready.sem, 1)

        @block.vector
        def _(dve):
            ch = Chain(dve, DVE_STEPS)
            for signal, n in ((wlo_ready, 2), (acc_taken[0], 1), (acc_taken[1], 1), (pts_ready, 1), (o_ready, 1),
                              (oT_ready, 1), (hid_ready, 2), (hidlo_ready, 2), (ym_ready, 2), (side_taken[0], 1), (side_taken[1], 1)):
                dve.sem_inc(signal.sem, n)
            dve.wait_ge(setup_tp, 1)
            dve.tensor_copy(colsA[:, :], ps[:, 0:P])
            dve.tensor_copy(colsB[:, :], ps[:, P:P + 40]).then_inc(cols_ready, 1)
            dve.wait_ge(cols_ready, 1)
            dve.wait_ge(silu_c_ready, 1)
            dve.memset(slotT[:, :, E:E + 2], -1.0)
            dve.tensor_tensor(sum_halves[:, :], ident[0:4, 0:2], ident[0:4, 2:4], ALU.add)
            dve.tensor_tensor(sc4[:, :, 2:4], sc[:, :, :], f32(sc4[:, :, 0:2]), ALU.subtract).then_inc(silu_c_ready, 1)
            with dve.Fori(0, MOD_GROUPS) as i:
                for n in range(MP):
                    dve.wait_ge(ring_split_hi.sem, i * MP + (n + 1))
                    dve.tensor_tensor(ring_lo[n % RING][:, :, :], ring[n % RING][:, :, :], f32(ring_hi[n % HI][:, :, :]), ALU.subtract)\
                       .then_inc(ring_split_lo.sem, 1)
            dve.wait_ge(mod_cols_done, 2 + MOD_BLOCKS)
            dve.tensor_tensor(mod[:, :, :], ps[:, 1024:1216].rearrange("p (a b) -> p a b", b=2),
                              colsA[:, 0:96].unsqueeze(2).to_broadcast([P, 96, 2]), ALU.add).then_inc(mod_ready, 1)
            dve.wait_ge(mod_ready, 1)
            dve.wait_ge(x_loaded, 32)
            dve.sem_inc(x_ready.sem, 1)

            with ch.layers() as layer:
                dve.tensor_copy(modl[:, :, :], mod[:, ds(layer * 48, 48), :]).then_inc(dve_chain, 1)
                dve.wait_ge(dve_chain, ch.next())
                dve.sem_inc(modl_ready.sem, 1)
                for A, n0, c0 in ((A1, 96, 8), (A2, 112, 32)):
                    g = colsA[:, ds(layer * 8 + n0, 8)].unsqueeze(2).to_broadcast([P, KT, 2])
                    dve.scalar_tensor_tensor(out=A[:, :, :], in0=modl[:, c0:c0 + 8, :], scalar=1.0, in1=g,
                                                     op0=ALU.add, op1=ALU.mult).then_inc(dve_chain, 1)
                    dve.wait_ge(dve_chain, ch.next())
                B1, B2 = modl[:, 0:8, :], modl[:, 24:32, :]

                def scale(n, t, xnb):
                    if t >= 2:
                        dve.wait_ge(tp_ready.sem, tp_ready.at(layer, n * NT + t - 1))
                        dve.wait_ge(lo_ready.sem, lo_ready.at(layer, n * NT + t - 1))
                    dve.tensor_scalar(xnb[t % 2][:, :], x[:, t, :], ss[:, n, t:t + 1], None, ALU.mult)\
                       .then_inc(xn_ready.sem, 1)

                def modulate(n, t, hb, A, B):
                    s = 0 if t < LT else 1
                    dve.wait_ge(tp_ready.sem, tp_ready.at(layer, n * NT + t + 1))
                    if n == 1 and t >= 2:
                        dve.wait_ge(logits_done.sem, logits_done.at(layer, t - 1))
                    wide = [P, KT, P]
                    dve.tensor_tensor(hb[t % 2][:, :, :], tp[t % 2].rearrange("p (k n) -> p k n", k=KT),
                                              A[:, :, s:s + 1].to_broadcast(wide), ALU.mult).then_inc(dve_chain, 1)
                    dve.wait_ge(dve_chain, ch.next())
                    dve.tensor_tensor(hb[t % 2][:, :, :], hb[t % 2][:, :, :], B[:, :, s:s + 1].to_broadcast(wide), ALU.add)\
                       .then_inc(h32_ready.sem, 1)

                dve.wait_ge(rstd_ready.sem, rstd_ready.at(layer, 1))
                scale(0, 0, xnb1)
                scale(0, 1, xnb1)
                for t in range(NT):
                    modulate(0, t, hb1, A1, B1)
                    dve.wait_ge(hi_ready.sem, hi_ready.at(layer, t + 1))
                    sl = slice(t * P, (t + 1) * P)
                    dve.tensor_tensor(hTlo[:, :, sl], hb1[t % 2][:, :, :], f32(hThi[:, :, sl]), ALU.subtract)\
                       .then_inc(lo_ready.sem, 1)
                    if t + 2 < NT:
                        scale(0, t + 2, xnb1)

                def split(h, b, nk=KT, raw=raw):
                    dve.wait_ge(whi_ready.sem, whi_ready.at(layer, 2 * h + (b + 1)))
                    dve.tensor_tensor(wlo[b][:, 0:nk, :], raw[b][:, 0:nk, :], f32(whi[b][:, 0:nk, :]), ALU.subtract)\
                       .then_inc(wlo_ready.sem, 1)

                def result(h, b, acc=accc):
                    dve.wait_ge(unit_done.sem, unit_done.at(layer, 2 * h + (b + 1)))
                    return acc[b]

                with dve.Fori(0, 3) as i:
                    for b in range(2):
                        split(i, b)

                def head_squares(src, nh, dst):
                    dve.tensor_tensor(t1[:, 0:nh * HD], src, src, ALU.mult).then_inc(dve_chain, 1)
                    dve.wait_ge(dve_chain, ch.next())
                    dve.tensor_reduce(dst, t1[:, 0:nh * HD].rearrange("p (h d) -> p h d", h=nh), AX.X, ALU.add).then_inc(dve_chain, 1)
                    dve.wait_ge(dve_chain, ch.next())

                def head_norm(src, t, nh, r, g, tc, tn, last=False):
                    v3 = src.rearrange("p (h d) -> p h d", h=nh)
                    wide = [P, nh, HD]
                    dve.tensor_tensor(v3, v3, r.unsqueeze(2).to_broadcast(wide), ALU.mult).then_inc(dve_chain, 1)
                    dve.wait_ge(dve_chain, ch.next())
                    if t == LT:
                        dve.tensor_tensor(v3, v3, g[:, :].unsqueeze(1).to_broadcast(wide), ALU.mult).then_inc(dve_chain, 1)
                        dve.wait_ge(dve_chain, ch.next())
                        return
                    a, bb = t1[:, 0:nh * HD], t2[:, 0:nh * HD]
                    dve.tensor_tensor(a.rearrange("p (h d) -> p h d", h=nh), v3, tc[:, t, :].unsqueeze(1).to_broadcast(wide),
                                      ALU.mult)
                    sv = src.rearrange("p (h s d) -> p h s d", h=2 * nh, s=2)
                    bv = bb.rearrange("p (h s d) -> p h s d", h=2 * nh, s=2)
                    tb = tn[:, t, :].rearrange("p (a s d) -> p a s d", a=2, s=2)
                    for s in range(2):
                        o = bv[:, :, s, :].rearrange("p (h a) d -> p h a d", a=2)
                        i0 = sv[:, :, 1 - s, :].rearrange("p (h a) d -> p h a d", a=2)
                        ins = dve.tensor_tensor(o, i0, tb[:, :, s, :].unsqueeze(1).to_broadcast([P, nh, 2, HALF]), ALU.mult)
                    ins.then_inc(dve_chain, 1)
                    dve.wait_ge(dve_chain, ch.next())
                    dve.tensor_tensor(src, a, bb, ALU.add).then_inc(dve_chain, 1)
                    dve.wait_ge(dve_chain, ch.next())

                def prepare(step):
                    if step == 0:
                        dve.wait_ge(acc_taken[0].sem, acc_taken[0].at(layer, 3))
                        dve.wait_ge(acc_taken[1].sem, acc_taken[1].at(layer, 3))
                        for t in range(NT):
                            head_squares(q[:, t, :], H, rq[:, t, :])
                    if step == 1:
                        for t in range(NT):
                            head_squares(k[:, t, :], KV, rk[:, t, :])
                        dve.sem_inc(ssq_ready.sem, 1)
                        dve.wait_ge(lp_loaded.sem, lp_loaded.at(layer, 48))
                        dve.tensor_scalar(gq[:, :], gq[:, :], HD ** -0.5, None, ALU.mult).then_inc(dve_chain, 1)
                        dve.wait_ge(dve_chain, ch.next())
                        for g, tc, tn in ((gq, qC, qS), (gk, kC, kS)):
                            dve.tensor_tensor(tc[:, :, :], cosT[:, :, :], g[:, :].unsqueeze(1).to_broadcast([P, LT, HD]), ALU.mult)
                            gv = g[:, :].rearrange("p (a s d) -> p a s d", a=2, s=2)
                            for t in range(LT):
                                sv = sinT[:, t, :].rearrange("p (a s d) -> p a s d", a=2, s=2)
                                tv = tn[:, t, :].rearrange("p (a s d) -> p a s d", a=2, s=2)
                                for s in range(2):
                                    ins = dve.tensor_tensor(tv[:, :, s, :], sv[:, :, s, :], gv[:, :, 1 - s, :], ALU.mult)
                            ins.then_inc(dve_chain, 1)
                            dve.wait_ge(dve_chain, ch.next())
                    if step == 2:
                        dve.wait_ge(rqk_ready.sem, rqk_ready.at(layer, 1))
                        for t in range(2):
                            head_norm(q[:, t, :], t, H, rq[:, t, :], gq, qC, qS)
                    if step == 3:
                        for t in range(2, 4):
                            head_norm(q[:, t, :], t, H, rq[:, t, :], gq, qC, qS)
                    if step == 4:
                        head_norm(q[:, LT, :], LT, H, rq[:, LT, :], gq, qC, qS)
                    if step == 5:
                        for t in range(NT):
                            head_norm(k[:, t, :], t, KV, rk[:, t, :], gk, kC, kS)
                        dve.sem_inc(qk_ready.sem, 1)

                for hf in range(2):
                    u = U_CONV + 3 * hf
                    if hf == 0:
                        split(u // 2, u % 2)
                        split((u + 1) // 2, (u + 1) % 2)
                    prepare(3 * hf)
                    split((u + 2) // 2, (u + 2) % 2)
                    prepare(3 * hf + 1)
                    for col in (0, LAT + 1, T + 2):
                        dve.memset(ub[:, :, col:col + 1], 0.0)
                    dve.wait_ge(acc_taken[u % 2].sem, acc_taken[u % 2].at(layer, u // 2 + 1))
                    r = result((u + 1) // 2, (u + 1) % 2).rearrange("p (a n) -> p a n", a=2)
                    dve.tensor_tensor(ub[:, :, 1:LAT + 1], r[:, :, 0:LAT], gcs[:, :, 0:LAT], ALU.mult)
                    ins = dve.tensor_tensor(ub[:, :, LAT + 2:T + 2], r[:, :, LAT:T], gcs[:, :, LAT:T], ALU.mult)
                    ins.then_inc(acc_taken[(u + 1) % 2].sem, 1)
                    dve.wait_ge(acc_taken[(u + 1) % 2].sem, acc_taken[(u + 1) % 2].at(layer, (u + 1) // 2 + 1))
                    for tap, off in ((1, 1), (0, 0), (2, 2)):
                        for a in range(2):
                            w = colsB[:, ds(layer * 12 + (16 + 4 * tap + 2 * hf + a), 1)]
                            src, dst = ub[:, a, off:off + T + 1], cb[:, a, 1:T + 2]
                            if tap == 1:
                                ins = dve.tensor_scalar(dst, src, w, None, ALU.mult)
                            else:
                                ins = dve.scalar_tensor_tensor(out=dst, in0=src, scalar=w, in1=dst, op0=ALU.mult, op1=ALU.add)
                        ins.then_inc(dve_chain, 1)
                        dve.wait_ge(dve_chain, ch.next())
                    split((u + 3) // 2, (u + 3) % 2)
                    prepare(3 * hf + 2)
                    r = result((u + 2) // 2, u % 2).rearrange("p (a n) -> p a n", a=2)
                    dve.tensor_tensor(gcs[:, :, 0:LAT], r[:, :, 0:LAT], cb[:, :, 1:LAT + 1], ALU.mult)
                    ins = dve.tensor_tensor(gcs[:, :, LAT:T], r[:, :, LAT:T], cb[:, :, LAT + 2:T + 2], ALU.mult)
                    ins.then_inc(acc_taken[u % 2].sem, 1)
                    dve.wait_ge(zhi_ready.sem, zhi_ready.at(layer, hf + 1))
                    dve.tensor_tensor(zlo[:, 2 * hf:2 * hf + 2, :], gcs[:, :, :], f32(zhi[:, 2 * hf:2 * hf + 2, :]), ALU.subtract)\
                       .then_inc(z_ready.sem, 1)
                    if hf == 0:
                        split((u + 4) // 2, (u + 4) % 2)
                with dve.Fori(0, 4) as i:
                    split(U_GATE // 2 + i, 1, KT // 2)
                    split(U_GATE // 2 + 1 + i, 0)
                    dve.wait_ge(acc_taken[0].sem, acc_taken[0].at(layer, U_GATE // 2 + 1 + i))
                    dve.tensor_tensor(mixed[:, ds(i * 2, 2), :].rearrange("p a n -> p (a n)"), result(U_GATE // 2 + i, 1), tw[:, :],
                                      ALU.mult).then_inc(acc_taken[1].sem, 1)
                for u in range(U_GT + 1, U_AO):
                    split(u // 2, u % 2)
                dve.wait_ge(cache_loaded.sem, cache_loaded.at(layer, 32))
                dve.sem_inc(waits_passed, 1)
                for kt in range(6):
                    dve.wait_ge(khi_ready.sem, khi_ready.at(layer, kt + 1))
                    src = (ck[:, :] if kt == 0 else k[:, kt - 1, :]).rearrange("p (v d) -> p v d", v=KV)
                    for a in range(2):
                        ins = dve.tensor_tensor(ksp[kt % 2][:, 1, :, a, :], src, ksp[kt % 2][:, 0, :, a, :], ALU.subtract)
                    ins.then_inc(ksplit.sem, 1)

                def query_halves(t):
                    dve.wait_ge(qhi_ready.sem, qhi_ready.at(layer, t + 1))
                    dve.tensor_tensor(qsp[:, :, 1, :], q[:, ds(t, 1), :].rearrange("p o (h d) -> p (o h) d", h=H),
                                      qsp[:, :, 0, :], ALU.subtract).then_inc(qsplit.sem, 1)

                query_halves(0)

                def attend(t, nk, more=True):
                    base = t * H

                    def normalise(half):
                        hs = slice(8 * half, 8 * half + 8)
                        dve.wait_ge(p_ready.sem, p_ready.at(layer, base + (8 * half + 8)))
                        dve.reciprocal(rinv[:, hs], rsum[:, hs]).then_inc(dve_chain, 1)
                        dve.wait_ge(dve_chain, ch.next())
                        dve.wait_ge(pv_done.sem, pv_done.at(layer, base + (8 * half + 8)))
                        if half == 0:
                            dve.wait_ge(otp_ready.sem, otp_ready.at(layer, t))
                        dve.tensor_tensor(ot[:, 512 * half:512 * (half + 1)].rearrange("p (h d) -> p h d", h=8),
                                          pso.rearrange("p (h d) -> p h d", h=8),
                                          rinv[:, hs].unsqueeze(2).to_broadcast([P, 8, HD]), ALU.mult).then_inc(o_ready.sem, 1)

                    for j in range(H + 2):
                        if j < H:
                            dve.wait_ge(s_ready.sem, s_ready.at(layer, base + (j + 1)))
                            dve.wait_ge(p_ready.sem, p_ready.at(layer, base + (j - 1)))
                            dve.tensor_reduce(nmax[:, j % 2:j % 2 + 1], scores[j % 2][:, 0:nk * P], AX.X, ALU.max, negate=True)\
                               .then_inc(nmax_ready.sem, 1)
                        if j == 11:
                            normalise(0)
                        if j >= 2:
                            i = j - 2
                            dve.wait_ge(pt_ready.sem, pt_ready.at(layer, base + (i + 1)))
                            dve.wait_ge(pv_done.sem, pv_done.at(layer, base + (i - 1)))
                            dve.tensor_copy(probT[i % 2][:, 0:nk, :].rearrange("p a n -> p (a n)"), ptp[:, 0:nk * P])\
                               .then_inc(pts_ready.sem, 1)
                        if j == 14 and more:
                            query_halves(t + 1)
                    normalise(1)
                    dve.wait_ge(ohi_ready.sem, ohi_ready.at(layer, t + 1))
                    dve.tensor_tensor(oTlo[:, :, ds(t * P, P)], bank(2, 2).rearrange("p (k n) -> p k n", k=KT),
                                      f32(oThi[:, :, ds(t * P, P)]), ALU.subtract).then_inc(oT_ready.sem, 1)

                with ch.loop(LT, 2) as t:
                    attend(t, 5)
                attend(LT, 1, more=False)
                split(U_AO // 2, 0, KT, raw_ao)
                for j in range(4):
                    h, b = (U_AO + j) // 2, j % 2
                    split((U_AO + j + 1) // 2, (j + 1) % 2, KT, raw_ao if j == 0 else raw)
                    if j:
                        dve.wait_ge(m_ready.sem, m_ready.at(layer, j))
                    g2 = G[:, 2 * j:2 * j + 2, :].rearrange("p a n -> p (a n)")
                    ins = dve.tensor_tensor(tw[:, :], result(h, b), g2, ALU.mult)
                    ins.then_inc(acc_taken[b].sem, 1)
                    dve.wait_ge(acc_taken[b].sem, acc_taken[b].at(layer, h + 1))
                    dve.tensor_tensor(tw[:, :], tw[:, :], mixed[:, 2 * j:2 * j + 2, :].rearrange("p a n -> p (a n)"), ALU.add)\
                       .then_inc(mrg_ready.sem, 1)
                    dve.wait_ge(mhi_ready.sem, mhi_ready.at(layer, j + 1))
                    dve.tensor_tensor(mlo[:, 2 * j:2 * j + 2, :].rearrange("p a n -> p (a n)"), tw[:, :],
                                      f32(mhi[:, 2 * j:2 * j + 2, :].rearrange("p a n -> p (a n)")), ALU.subtract)\
                       .then_inc(m_ready.sem, 1)
                dve.wait_ge(rows_taken.sem, rows_taken.at(layer, 2))
                t3 = tw[:, :].rearrange("p (t n) -> p t n", t=NT)
                for j in range(4):
                    h, b = (U_WO + j) // 2, j % 2
                    cols = slice(j * UW, (j + 1) * UW)
                    if j < 3:
                        split((U_WO + j + 1) // 2, (j + 1) % 2)
                    a3 = result(h, b, acc).rearrange("p (t n) -> p t n", t=NT)
                    dve.tensor_tensor(t3[:, 0:LT, :], a3[:, 0:LT, :], gbc[:, 0, cols].unsqueeze(1).to_broadcast([P, LT, UW]), ALU.mult)
                    ins = dve.tensor_tensor(t3[:, LT, :], a3[:, LT, :], gbc[:, 1, cols], ALU.mult)
                    ins.then_inc(acc_taken[b].sem, 1)
                    dve.wait_ge(acc_taken[b].sem, acc_taken[b].at(layer, h + 1))
                    ins = dve.tensor_tensor(x[:, :, cols], x[:, :, cols], t3, ALU.add)
                    if j < 3:
                        ins.then_inc(dve_chain, 1)
                        dve.wait_ge(dve_chain, ch.next())
                    else:
                        ins.then_inc(x_ready.sem, 1)
                dve.wait_ge(rstd_ready.sem, rstd_ready.at(layer, 2))
                scale(1, 0, xnb2)
                scale(1, 1, xnb2)
                for t in range(NT):
                    modulate(1, t, hb2, A2, B2)
                    dve.wait_ge(hi_ready.sem, hi_ready.at(layer, NT + t + 1))
                    dve.tensor_tensor(xnlo[:, t, :], xnb2[t % 2][:, :], f32(xnhi[:, t, :]), ALU.subtract)\
                       .then_inc(lo_ready.sem, 1)
                    if t + 2 < NT:
                        scale(1, t + 2, xnb2)
                dve.wait_ge(logits_done.sem, logits_done.at(layer, NT))
                lps = bank(4)[:, 0:NT * E].rearrange("p (t e) -> p t e", t=NT)
                wide = [P, NT, E]
                dve.tensor_reduce(lgm[:, :], lps, AX.X, ALU.max).then_inc(dve_chain, 1)
                dve.wait_ge(dve_chain, ch.next())
                dve.tensor_tensor(lg[:, :, :], lps, lgm[:, :].unsqueeze(2).to_broadcast(wide), ALU.subtract)\
                   .then_inc(lgsub_ready.sem, 1)
                dve.wait_ge(lgexp_ready.sem, lgexp_ready.at(layer, 1))
                dve.tensor_reduce(lsum[:, :], lg[:, :, :], AX.X, ALU.add).then_inc(dve_chain, 1)
                dve.wait_ge(dve_chain, ch.next())
                dve.reciprocal(lsum[:, :], lsum[:, :]).then_inc(dve_chain, 1)
                dve.wait_ge(dve_chain, ch.next())
                dve.tensor_tensor(aff[:, :, :], lg[:, :, :], lsum[:, :].unsqueeze(2).to_broadcast(wide), ALU.mult)\
                   .then_inc(aff_ready.sem, 1)
                dve.wait_ge(affhi_ready.sem, affhi_ready.at(layer, 1))
                dve.tensor_tensor(afflo[:, :, :], aff[:, :, :], f32(affhi[:, :, :]), ALU.subtract)
                dve.wait_ge(affT_ready.sem, affT_ready.at(layer, 1))
                dve.tensor_copy(work[:, :], ps[0:E, 2560:2560 + T]).then_inc(dve_chain, 1)
                dve.wait_ge(dve_chain, ch.next())
                dve.sem_inc(waits_passed, 1)
                for lo, hi, cap in ((0, LAT, CAP_L), (LAT, T, CAP_C)):
                    for _ in range(cap // 8):
                        dve.max(top8[:, :], work[:, lo:hi]).then_inc(dve_chain, 1)
                        dve.wait_ge(dve_chain, ch.next())
                        dve.sem_inc(waits_passed, 1)
                        dve.match_replace(out=work[:, lo:hi], in_to_replace=top8[:, :],
                                                        in_values=work[:, lo:hi], imm_value=-1.0).then_inc(dve_chain, 1)
                        dve.wait_ge(dve_chain, ch.next())
                        dve.sem_inc(waits_passed, 1)
                dve.tensor_scalar(affT[:, :], work[:, :], 0.0, None, ALU.is_lt).then_inc(dve_chain, 1)
                dve.wait_ge(dve_chain, ch.next())
                for lo, hi, off in ((0, LAT, 0.0), (LAT, T, float(CAP_L))):
                    dve.tensor_tensor_scan(cum[:, lo:hi], affT[:, lo:hi], affT[:, lo:hi], 0.0, ALU.add, ALU.max).then_inc(dve_chain, 1)
                    dve.wait_ge(dve_chain, ch.next())
                    dve.scalar_tensor_tensor(out=work[:, lo:hi], in0=cum[:, lo:hi], scalar=off, in1=affT[:, lo:hi],
                                                     op0=ALU.add, op1=ALU.mult).then_inc(dve_chain, 1)
                    dve.wait_ge(dve_chain, ch.next())
                dve.tensor_scalar(work[:, :], work[:, :], -1.0, None, ALU.add).then_inc(slots_ready.sem, 1)
                dve.wait_ge(slotsT_ready.sem, slotsT_ready.at(layer, 1))
                dve.tensor_copy(slotT[:, :, 0:E], bank(7)[:, 0:NT * E].rearrange("p (t e) -> p t e", t=NT)).then_inc(dve_chain, 1)
                dve.wait_ge(dve_chain, ch.next())
                dve.sem_inc(waits_passed, 1)

                def selection(pair):
                    for t in range(NT):
                        ins = dve.tensor_tensor(S[:, t], slotT[:, t, ds(pair * 2, 2)].unsqueeze(2).to_broadcast([P, 2, SL]),
                                                slot_ids[:, :].unsqueeze(1).to_broadcast([P, 2, SL]), ALU.is_equal)
                    dve.tensor_tensor(Sg_lat[:, :, :, :],
                                      slotT[:, 0:LT, ds(pair * 2, 2)].unsqueeze(3).to_broadcast([P, LT, 2, CAP_L]),
                                      slot_ids[:, 0:CAP_L].unsqueeze(1).unsqueeze(1).to_broadcast([P, LT, 2, CAP_L]), ALU.is_equal)
                    ins = dve.tensor_tensor(Sg_ctx[:, :, :], slotT[:, LT, ds(pair * 2, 2)].unsqueeze(2).to_broadcast([P, 2, CAP_C]),
                                            slot_ids[:, CAP_L:SL].unsqueeze(1).to_broadcast([P, 2, CAP_C]), ALU.is_equal)
                    ins.then_inc(S_ready.sem, 1)

                selection(0)
                with ch.loop(E // 2, PAIR_STEPS) as p:
                    def side_result(n):
                        dve.wait_ge(side_ready.sem, side_ready.at(layer, p * SIDES + (n + 1)))
                        return side[n % 2]

                    def tokens():
                        src = side_result(4).rearrange("p (k e c) -> p k e c", k=4, e=2)
                        for dd in range(4):
                            ins = dve.tensor_scalar(xsel[:, dd, :, 0:CAP_L], src[:, dd], A2[:, dd, 0:1], B2[:, dd, 0:1],
                                                    ALU.mult, ALU.add)
                        ins.then_inc(side_taken[0].sem, 1)

                    def context_tokens():
                        src = side_result(3)[:, 0:KT * 2 * CAP_C].rearrange("p (k e c) -> p k e c", k=KT, e=2)
                        wide = [P, KT, 2, CAP_C]
                        xc = xsel[:, :, :, CAP_L:SL]
                        dve.tensor_tensor(xc, src, A2[:, :, 1:2].unsqueeze(3).to_broadcast(wide), ALU.mult).then_inc(side_taken[1].sem, 1)
                        dve.wait_ge(side_taken[1].sem, side_taken[1].at(layer, p * (SIDES // 2) + 2))
                        dve.tensor_tensor(xc, xc, B2[:, :, 1:2].unsqueeze(3).to_broadcast(wide), ALU.add)

                    def add_sum(n):
                        b, t = n // NT, n % NT
                        xv = x[:, t, 512 * b:512 * (b + 1)]
                        dve.tensor_tensor(xv, xv, side_result(12 + n), ALU.add).then_inc(side_taken[n % 2].sem, 1)

                    for m in range(PP + 5):
                        if m == PP + 4:
                            add_sum(0)
                            add_sum(1)
                        for e, r in ((1, m - EP), (0, m)):
                            if r in (6, 10):
                                b = int(r == 10)
                                dve.wait_ge(silu_ready.sem, silu_ready.at(layer, p * 4 + (2 * e + b + 1)))
                                dve.wait_ge(ring_done.sem, ring_done.at(layer, p * PP + (EP * e + 4 * b + 4)))
                                dve.tensor_tensor(hid[b][:, :], hid[b][:, :], up_ps[b], ALU.mult).then_inc(hid_ready.sem, 1)
                            if r in TURNED[e]:
                                b = TURNED[e].index(r)
                                dve.wait_ge(hidhi_ready.sem, hidhi_ready.at(layer, p * 4 + (2 * e + b + 1)))
                                hh = slice(4 * b, 4 * b + 4)
                                dve.tensor_tensor(hidlo[:, hh, :].rearrange("p a n -> p (a n)"), hidT_ps[b],
                                                  f32(hidhi[:, hh, :].rearrange("p a n -> p (a n)")), ALU.subtract)\
                                   .then_inc(hidlo_ready.sem, 1)
                            if r in (15, 16):
                                b = r - 15
                                cols = slice(512 * b, 512 * (b + 1))
                                dve.wait_ge(yhi_ready.sem, yhi_ready.at(layer, p * 4 + (2 * e + b + 1)))
                                dve.tensor_tensor(ylo[:, e, cols], ym[:, e, cols], f32(yhi[:, e, cols]), ALU.subtract)\
                                   .then_inc(ylo_ready.sem, 1)
                            if r in (14, 15):
                                b = r - 14
                                cols = slice(512 * b, 512 * (b + 1))
                                dve.wait_ge(ring_done.sem, ring_done.at(layer, p * PP + (EP * e + 11 + b)))
                                if e == 0 and b == 0:
                                    dve.wait_ge(side_taken[1].sem, side_taken[1].at(layer, p * (SIDES // 2) + 6))
                                dve.scalar_tensor_tensor(out=ym[:, e, cols], in0=down_ps[b], scalar=vals[:, 3 * e:3 * e + 1],
                                                         in1=g2mix[0:SL, cols], op0=ALU.mult, op1=ALU.mult).then_inc(ym_ready.sem, 1)
                        if m in DVE_LO:
                            dve.wait_ge(ring_split_hi.sem, ring_split_hi.at(layer, p * PP + (m + 1)))
                            dve.tensor_tensor(ring_lo[m % RING][:, :, :], ring[m % RING][:, :, :], f32(ring_hi[m % HI][:, :, :]),
                                              ALU.subtract).then_inc(ring_split_lo.sem, 1)
                        if m == 0:
                            context_tokens()
                            tokens()
                        if m < 2:
                            dve.wait_ge(xhi_ready.sem, xhi_ready.at(layer, p * 2 + (m + 1)))
                            kk = slice(4 * m, 4 * m + 4)
                            dve.tensor_tensor(xlo[:, kk], xsel[:, kk], f32(xhi[:, kk]), ALU.subtract).then_inc(xlo_ready.sem, 1)
                        if m == 12:
                            dve.tensor_copy(vals[:, :], side_result(11)[0:SL, 0:4]).then_inc(side_taken[1].sem, 1)
                        if m == 13:
                            selection(p + 1)
                    for n in range(2, 2 * NT):
                        add_sum(n)
                dve.wait_ge(side_taken[1].sem, side_taken[1].at(layer, SIDES // 2 * E // 2))
                dve.sem_inc(x_ready.sem, 1)
            dve.wait_ge(fn_loaded, 16)
            dve.wait_ge(rstd_ready.sem, rstd_ready.at(DEPTH, 1))
            for t in range(NT):
                dve.scalar_tensor_tensor(out=x[:, t, :], in0=x[:, t, :], scalar=ss[:, 0, t:t + 1], in1=gbc[:, 0, :],
                                         op0=ALU.mult, op1=ALU.mult).then_inc(xn_ready.sem, 1)


DVE_STEPS = 113
PAIR_STEPS = 0

_INS = ["x_prompt", "x_sample", "cache_k", "cache_v", "c", "c_ctx", "w_mod", "b_mod", "norm1", "norm2", "w_in", "q_norm",
        "k_norm", "conv_w", "w_conv_out", "w_attn_out", "w_o", "w_router", "w_gate", "w_up", "w_down", "final_norm"]
_OUTS = [((1, CTX, D), "float32"), ((1, LAT, D), "float32"), ((1, DEPTH, CTX, KV, HD), "float32"),
         ((1, DEPTH, CTX, KV, HD), "float32")]


def constants():
    pos = np.arange(LAT)
    inv = (10000.0 ** (-np.arange(HALF, dtype=np.float32) / HALF)).astype(np.float32)
    cos, sin = np.zeros((LAT, 2, 2, HALF), np.float32), np.zeros((LAT, 2, 2, HALF), np.float32)
    for a, p in enumerate((pos // GRID_W, pos % GRID_W)):
        ang = p.astype(np.float32)[:, None] * inv[None, :]
        cos[:, a, :, :] = np.cos(ang)[:, None, :]
        sin[:, a, 0, :] = -np.sin(ang)
        sin[:, a, 1, :] = np.sin(ang)
    slots = np.broadcast_to(np.arange(SL, dtype=np.float32), (P, SL)).copy()
    return {"ident": np.eye(P, dtype=np.float32), "slots": slots, "cos": cos.reshape(LAT, HD), "sin": sin.reshape(LAT, HD)}


def kernel(**inputs):
    import concourse.bacc as _bacc
    from concourse import mybir as _mybir
    from concourse.bass_utils import run_bass_kernel_spmd as _run

    nc = _bacc.Bacc("TRN2", target_bir_lowering=False, num_devices=1)
    arrays, args = {}, []
    for name, a in [(n, np.ascontiguousarray(inputs[n])) for n in _INS] + list(constants().items()):
        arrays[f"in_{name}_dram"] = a
        args.append(nc.dram_tensor(f"in_{name}_dram", a.shape, _mybir.dt.from_np(a.dtype), kind="ExternalInput").ap())
    for i, (shape, dtype) in enumerate(_OUTS):
        args.append(nc.dram_tensor(f"out_{i}_dram", shape, _mybir.dt.from_np(np.dtype(dtype)), kind="ExternalOutput").ap())
    build(nc, *args)
    r = _run(nc, [arrays], core_ids=[0])
    return tuple(r.results[0][f"out_{i}_dram"] for i in range(len(_OUTS)))
```
